# Optimizing a Trainium2 kernel written in Bass

```python
import jax, jax.numpy as jnp
from jax import lax
import numpy as np

D_MODEL = 2048
BATCH = 1
SEQ = 512
DEPTH = 2
DEC_BATCH = 1
DEC_SEQ = 32
PAST_LEN = 256

CHUNK = 64
QBLOCK = 128
HEAD_DIM = 128
GROUP_W = D_MODEL // 4
H_FOX = GROUP_W // HEAD_DIM
H_BAND = GROUP_W // HEAD_DIM
H_SWA_Q = GROUP_W // HEAD_DIM
H_SWA_KV = H_SWA_Q // 2
H_MEM = 4
MEM_HD = GROUP_W // H_MEM
N_MEM = 256
BAND_PREV = 8
BAND_CTX = BAND_PREV * CHUNK
SWA_WINDOW = 128
SWA_PREV = SWA_WINDOW // CHUNK
REL_CLIP = 128
ROPE_THETA = 10000.0
LN_EPS = 1e-5
FORGET_BIAS_INIT = 3.0
NEG_INF = -1e30
ALPHA = (2 * DEPTH) ** 0.25
BETA = (8 * DEPTH) ** -0.25
FOX_W = H_FOX * HEAD_DIM
BAND_W = H_BAND * HEAD_DIM
SWA_Q_W = H_SWA_Q * HEAD_DIM
SWA_KV_W = H_SWA_KV * HEAD_DIM
MEM_W = H_MEM * MEM_HD
IN_SIZES = (FOX_W, FOX_W, FOX_W, H_FOX, BAND_W, BAND_W, BAND_W, SWA_Q_W, SWA_KV_W, SWA_KV_W, MEM_W, D_MODEL)
IN_TOTAL = sum(IN_SIZES)

kernel_name = 'hybrid_streaming_encoder_step'

def _layer_norm(x, g, b):
    xf = x.astype(jnp.float32)
    mu = jnp.mean(xf, -1, keepdims=True)
    var = jnp.mean(jnp.square(xf - mu), -1, keepdims=True)
    y = (xf - mu) * lax.rsqrt(var + LN_EPS) * g.astype(jnp.float32) + b.astype(jnp.float32)
    return y.astype(x.dtype)

def _rope(x, pos):
    half = HEAD_DIM // 2
    inv = ROPE_THETA ** (-jnp.arange(half, dtype=jnp.float32) / half)
    ang = pos.astype(jnp.float32)[:, None] * inv[None, :]
    cos = jnp.cos(ang)[None, :, None, :]
    sin = jnp.sin(ang)[None, :, None, :]
    xf = x.astype(jnp.float32)
    x1, x2 = xf[..., :half], xf[..., half:]
    return jnp.concatenate([x1 * cos - x2 * sin, x2 * cos + x1 * sin], -1).astype(x.dtype)

def _in_proj(x, w):
    bsz, t = x.shape[0], x.shape[1]
    z = jnp.einsum('btd,de->bte', x, w)
    fq, fk, fv, ff, bq, bk, bv, sq, sk, sv, mq, gate = jnp.split(z, np.cumsum(IN_SIZES)[:-1].tolist(), axis=-1)
    heads = lambda a, h: a.reshape(bsz, t, h, -1)
    return (heads(fq, H_FOX), heads(fk, H_FOX), heads(fv, H_FOX), ff,
            heads(bq, H_BAND), heads(bk, H_BAND), heads(bv, H_BAND),
            heads(sq, H_SWA_Q), heads(sk, H_SWA_KV), heads(sv, H_SWA_KV),
            heads(mq, H_MEM), gate)

def _mem_kv(mem, w):
    bsz, n = mem.shape[0], mem.shape[1]
    mk, mv = jnp.split(jnp.einsum('bmd,de->bme', mem, w), 2, axis=-1)
    return mk.reshape(bsz, n, H_MEM, MEM_HD), mv.reshape(bsz, n, H_MEM, MEM_HD)

def _fox_prompt(q, k, v, logf):
    bsz, s_len, nh, hd = q.shape
    scale = hd ** -0.5
    c = jnp.cumsum(logf, axis=1)
    ct = c.transpose(0, 2, 1)
    nb = s_len // QBLOCK
    qb = q.reshape(bsz, nb, QBLOCK, nh, hd).transpose(1, 0, 2, 3, 4)
    cb = c.reshape(bsz, nb, QBLOCK, nh).transpose(1, 0, 2, 3)
    kpos = jnp.arange(s_len)

    def blk(args):
        i, qi, ci = args
        s = jnp.einsum('bqhd,bkhd->bhqk', qi, k).astype(jnp.float32) * scale
        s = s + ci.transpose(0, 2, 1)[..., None] - ct[:, :, None, :]
        qpos = i * QBLOCK + jnp.arange(QBLOCK)
        s = jnp.where(kpos[None, :] <= qpos[:, None], s, NEG_INF)
        p = jax.nn.softmax(s, -1).astype(v.dtype)
        return jnp.einsum('bhqk,bkhd->bqhd', p, v)

    out = lax.map(blk, (jnp.arange(nb), qb, cb))
    return out.transpose(1, 0, 2, 3, 4).reshape(bsz, s_len, nh, hd)

def _fox_sample(q, k, v, logf, ck, cv, clogf):
    t = q.shape[1]
    p_len = ck.shape[1]
    scale = q.shape[-1] ** -0.5
    kk = jnp.concatenate([ck.astype(k.dtype), k], 1)
    vv = jnp.concatenate([cv.astype(v.dtype), v], 1)
    c = jnp.cumsum(jnp.concatenate([clogf.astype(jnp.float32), logf], 1), axis=1)
    ct = c.transpose(0, 2, 1)
    s = jnp.einsum('bqhd,bkhd->bhqk', q, kk).astype(jnp.float32) * scale
    s = s + ct[:, :, p_len:, None] - ct[:, :, None, :]
    mask = jnp.arange(p_len + t)[None, :] <= (p_len + jnp.arange(t))[:, None]
    s = jnp.where(mask, s, NEG_INF)
    p = jax.nn.softmax(s, -1).astype(vv.dtype)
    return jnp.einsum('bhqk,bkhd->bqhd', p, vv)

def _softmax_with_sink(s, sink):
    m = jnp.maximum(jnp.max(s, -1, keepdims=True), sink)
    e = jnp.exp(s - m)
    return e / (jnp.sum(e, -1, keepdims=True) + jnp.exp(sink - m))

def _local_attn(q, k, v, qpos, kpos, rel_table, sink):
    hkv, grp = q.shape[3], q.shape[4]
    s = jnp.einsum('bnqhgd,bnkhd->bnhgqk', q, k).astype(jnp.float32) * (q.shape[-1] ** -0.5)
    if rel_table is not None:
        rel = jnp.clip(kpos[:, None, :] - qpos[:, :, None], -REL_CLIP, REL_CLIP) + REL_CLIP
        bias = rel_table.astype(jnp.float32)[:, rel]
        bias = bias.reshape(hkv, grp, *rel.shape).transpose(2, 0, 1, 3, 4)
        s = s + bias[None]
    valid = (kpos >= 0)[None, :, None, None, None, :]
    s = jnp.where(valid, s, NEG_INF)
    if sink is None:
        p = jax.nn.softmax(s, -1)
    else:
        p = _softmax_with_sink(s, sink.astype(jnp.float32).reshape(hkv, grp, 1, 1))
    return jnp.einsum('bnhgqk,bnkhd->bnqhgd', p.astype(v.dtype), v)

def _band_prompt(q, k, v, n_prev, rel_table, sink):
    bsz, s_len, hq, hd = q.shape
    hkv = k.shape[2]
    nc = s_len // CHUNK
    band = (n_prev + 1) * CHUNK
    pad = ((0, 0), (n_prev * CHUNK, 0), (0, 0), (0, 0))
    kc = jnp.pad(k, pad).reshape(bsz, nc + n_prev, CHUNK, hkv, hd)
    vc = jnp.pad(v, pad).reshape(bsz, nc + n_prev, CHUNK, hkv, hd)
    kb = jnp.concatenate([kc[:, j:j + nc] for j in range(n_prev + 1)], axis=2)
    vb = jnp.concatenate([vc[:, j:j + nc] for j in range(n_prev + 1)], axis=2)
    qc = q.reshape(bsz, nc, CHUNK, hkv, hq // hkv, hd)
    cidx = jnp.arange(nc)[:, None]
    qpos = cidx * CHUNK + jnp.arange(CHUNK)[None, :]
    kpos = (cidx - n_prev) * CHUNK + jnp.arange(band)[None, :]
    o = _local_attn(qc, kb, vb, qpos, kpos, rel_table, sink)
    return o.reshape(bsz, s_len, hq, hd)

def _band_sample(q, k, v, ck, cv, past_len, rel_table, sink):
    bsz, t, hq, hd = q.shape
    hkv = k.shape[2]
    lc = ck.shape[1]
    kk = jnp.concatenate([ck.astype(k.dtype), k], 1)[:, None]
    vv = jnp.concatenate([cv.astype(v.dtype), v], 1)[:, None]
    qpos = (past_len + jnp.arange(t))[None, :]
    kpos = jnp.concatenate([past_len - lc + jnp.arange(lc), past_len + jnp.arange(t)])[None, :]
    o = _local_attn(q.reshape(bsz, 1, t, hkv, hq // hkv, hd), kk, vv, qpos, kpos, rel_table, sink)
    return o.reshape(bsz, t, hq, hd)

def _cross(q, mk, mv):
    s = jnp.einsum('bqhd,bmhd->bhqm', q, mk.astype(q.dtype)).astype(jnp.float32) * (q.shape[-1] ** -0.5)
    p = jax.nn.softmax(s, -1).astype(q.dtype)
    return jnp.einsum('bhqm,bmhd->bqhd', p, mv.astype(q.dtype))

def _merge(x, outs, gate, w_out, g, b):
    bsz, t = x.shape[0], x.shape[1]
    o = jnp.concatenate([a.reshape(bsz, t, -1) for a in outs], -1) * jax.nn.silu(gate)
    y = jnp.einsum('btd,de->bte', o, w_out)
    return _layer_norm(ALPHA * x + y, g, b)

def setup_inputs(seed: int = 0) -> dict:
    key = jax.random.key(seed)
    ks = jax.random.split(key, 24)
    nrm = lambda k, shape, s=1.0: s * jax.random.normal(k, shape, jnp.float32)
    band_len = min(BAND_CTX, PAST_LEN)
    swa_len = min(SWA_WINDOW, PAST_LEN)
    col_scale = jnp.concatenate([
        jnp.ones((2 * FOX_W,)), jnp.full((FOX_W,), BETA), jnp.ones((H_FOX + 2 * BAND_W,)),
        jnp.full((BAND_W,), BETA), jnp.ones((SWA_Q_W + SWA_KV_W,)), jnp.full((SWA_KV_W,), BETA),
        jnp.ones((MEM_W + D_MODEL,))])
    mem_scale = jnp.concatenate([jnp.ones((MEM_W,)), jnp.full((MEM_W,), BETA)])
    return {
        'x_prompt': nrm(ks[0], (BATCH, SEQ, D_MODEL)),
        'x_sample': nrm(ks[1], (DEC_BATCH, DEC_SEQ, D_MODEL)),
        'cache_fox_k': nrm(ks[2], (DEPTH, DEC_BATCH, PAST_LEN, H_FOX, HEAD_DIM)),
        'cache_fox_v': nrm(ks[3], (DEPTH, DEC_BATCH, PAST_LEN, H_FOX, HEAD_DIM), BETA),
        'cache_fox_logf': jax.nn.log_sigmoid(FORGET_BIAS_INIT + nrm(ks[4], (DEPTH, DEC_BATCH, PAST_LEN, H_FOX))),
        'cache_band_k': nrm(ks[5], (DEPTH, DEC_BATCH, band_len, H_BAND, HEAD_DIM)),
        'cache_band_v': nrm(ks[6], (DEPTH, DEC_BATCH, band_len, H_BAND, HEAD_DIM), BETA),
        'cache_swa_k': nrm(ks[7], (DEPTH, DEC_BATCH, swa_len, H_SWA_KV, HEAD_DIM)),
        'cache_swa_v': nrm(ks[8], (DEPTH, DEC_BATCH, swa_len, H_SWA_KV, HEAD_DIM), BETA),
        'cache_mem_k': nrm(ks[9], (DEPTH, DEC_BATCH, N_MEM, H_MEM, MEM_HD)),
        'cache_mem_v': nrm(ks[10], (DEPTH, DEC_BATCH, N_MEM, H_MEM, MEM_HD), BETA),
        'mem_prompt': nrm(ks[11], (BATCH, N_MEM, D_MODEL)),
        'ln_in_g': 1.0 + nrm(ks[12], (D_MODEL,), 0.02),
        'ln_in_b': nrm(ks[13], (D_MODEL,), 0.02),
        'w_in': nrm(ks[14], (DEPTH, D_MODEL, IN_TOTAL), D_MODEL ** -0.5) * col_scale,
        'b_f': FORGET_BIAS_INIT + nrm(ks[15], (DEPTH, H_FOX), 0.5),
        'rel_bias': nrm(ks[16], (DEPTH, H_BAND, 2 * REL_CLIP + 1), 0.5),
        'sinks': nrm(ks[17], (DEPTH, H_SWA_Q), 0.5),
        'w_mem_kv': nrm(ks[18], (DEPTH, D_MODEL, 2 * MEM_W), D_MODEL ** -0.5) * mem_scale,
        'w_out': nrm(ks[19], (DEPTH, D_MODEL, D_MODEL), BETA * D_MODEL ** -0.5),
        'ln_g': 1.0 + nrm(ks[20], (DEPTH, D_MODEL), 0.02),
        'ln_b': nrm(ks[21], (DEPTH, D_MODEL), 0.02),
    }

def reference(x_prompt, x_sample, cache_fox_k, cache_fox_v, cache_fox_logf, cache_band_k, cache_band_v,
              cache_swa_k, cache_swa_v, cache_mem_k, cache_mem_v, mem_prompt, ln_in_g, ln_in_b, w_in, b_f,
              rel_bias, sinks, w_mem_kv, w_out, ln_g, ln_b):
    seq = x_prompt.shape[1]
    dec_seq = x_sample.shape[1]
    past = cache_fox_k.shape[2]
    pos_p = jnp.arange(seq)
    pos_s = past + jnp.arange(dec_seq)
    band_keep = min(BAND_CTX, seq)
    swa_keep = min(SWA_WINDOW, seq)
    xp = _layer_norm(x_prompt, ln_in_g, ln_in_b)
    xs = _layer_norm(x_sample, ln_in_g, ln_in_b)
    fk_p, fv_p, fl_p, bk_p, bv_p, sk_p, sv_p, mk_p, mv_p = [], [], [], [], [], [], [], [], []
    fk_s, fv_s, fl_s, bk_s, bv_s, sk_s, sv_s = [], [], [], [], [], [], []
    for l in range(DEPTH):
        fq, fk, fv, ff, bq, bk, bv, sq, sk, sv, mq, gate = _in_proj(xp, w_in[l])
        logf = jax.nn.log_sigmoid((ff + b_f[l]).astype(jnp.float32))
        sq, sk = _rope(sq, pos_p), _rope(sk, pos_p)
        mk, mv = _mem_kv(mem_prompt, w_mem_kv[l])
        outs = (_fox_prompt(fq, fk, fv, logf),
                _band_prompt(bq, bk, bv, BAND_PREV, rel_bias[l], None),
                _band_prompt(sq, sk, sv, SWA_PREV, None, sinks[l]),
                _cross(mq, mk, mv))
        xp = _merge(xp, outs, gate, w_out[l], ln_g[l], ln_b[l])
        fk_p.append(fk); fv_p.append(fv); fl_p.append(logf)
        bk_p.append(bk[:, seq - band_keep:]); bv_p.append(bv[:, seq - band_keep:])
        sk_p.append(sk[:, seq - swa_keep:]); sv_p.append(sv[:, seq - swa_keep:])
        mk_p.append(mk); mv_p.append(mv)
        fq, fk, fv, ff, bq, bk, bv, sq, sk, sv, mq, gate = _in_proj(xs, w_in[l])
        logf = jax.nn.log_sigmoid((ff + b_f[l]).astype(jnp.float32))
        sq, sk = _rope(sq, pos_s), _rope(sk, pos_s)
        outs = (_fox_sample(fq, fk, fv, logf, cache_fox_k[l], cache_fox_v[l], cache_fox_logf[l]),
                _band_sample(bq, bk, bv, cache_band_k[l], cache_band_v[l], past, rel_bias[l], None),
                _band_sample(sq, sk, sv, cache_swa_k[l], cache_swa_v[l], past, None, sinks[l]),
                _cross(mq, cache_mem_k[l], cache_mem_v[l]))
        xs = _merge(xs, outs, gate, w_out[l], ln_g[l], ln_b[l])
        fk_s.append(fk); fv_s.append(fv); fl_s.append(logf)
        bk_s.append(bk); bv_s.append(bv)
        sk_s.append(sk); sv_s.append(sv)
    return (xp, xs,
            jnp.stack(fk_p), jnp.stack(fv_p), jnp.stack(fl_p),
            jnp.stack(bk_p), jnp.stack(bv_p),
            jnp.stack(sk_p), jnp.stack(sv_p),
            jnp.stack(mk_p), jnp.stack(mv_p),
            jnp.stack(fk_s), jnp.stack(fv_s), jnp.stack(fl_s),
            jnp.stack(bk_s), jnp.stack(bv_s),
            jnp.stack(sk_s), jnp.stack(sv_s))


_drawn_inputs = setup_inputs


def setup_inputs(seed=0):
    import zlib

    import numpy as np

    out = dict(_drawn_inputs(seed))
    spreads = {}
    factors = {'cache_fox_k': 7.302,
     'cache_fox_v': 5.516,
     'cache_fox_logf': 8.0,
     'cache_band_k': 8.0,
     'cache_band_v': 7.892,
     'cache_swa_k': 8.0,
     'cache_swa_v': 6.843,
     'cache_mem_k': 8.0,
     'cache_mem_v': 7.282,
     'ln_in_g': 2.87,
     'rel_bias': 8.0,
     'sinks': 64.0}
    for name, (base, spread) in spreads.items():
        noise = np.random.default_rng([zlib.crc32(name.encode()), seed]).standard_normal(out[name].shape)
        drawn = base * np.exp(spread * noise) if base else spread * noise
        out[name] = __import__('jax').numpy.asarray(drawn.astype(out[name].dtype))
    for name, factor in factors.items():
        out[name] = (out[name] * factor).astype(out[name].dtype)
    return out
```

```python
from contextlib import ExitStack

import concourse.bass as bass
from concourse import mybir

ALU = mybir.AluOpType
ACT = mybir.ActivationFunctionType
F32 = mybir.dt.float32
F32R = mybir.dt.float32r
AX_X = mybir.AxisListType.X

P = 128
DM = 2048
KC = DM // P
SEQ, DEC, PAST = 512, 32, 256
TOK = SEQ + DEC
HALF = TOK // 2
DEPTH = 2
NMEM = 256
HD = 128
GH = 4
HEADS = 4 * GH
ALPHA = (2 * DEPTH) ** 0.25
EPS = 1e-5
SCALE = HD ** -0.5
NEG = -1e30
RELW = SEQ + P
TILES = [(i * P, P) for i in range(SEQ // P)] + [(SEQ, DEC)]
NT = len(TILES)

MEM_TILES = 2 * GH
HEAD_TILES = 4
PAIR_TILES = 10
PAIRS = 2
A0 = MEM_TILES
B0 = A0 + HEAD_TILES * GH
C0 = B0 + HEAD_TILES * GH
O0 = C0 + PAIR_TILES * PAIRS
LT = O0 + KC

V_UNITS = 2 * GH + PAIRS
K_LOADS = 2 * GH + PAIRS + GH

class Group:
    def __init__(self, blocks, cached, own, place, sink=False):
        self.blocks, self.cached, self.own, self.place, self.sink = blocks, cached, own, place, sink
        self.width = [P * len(b) for b in blocks] + [P * cached + own]
        self.at = [sum(w + 1 for w in self.width[:i]) for i in range(NT)]
        self.order = [i for _, _, i in place]


CAUSAL = [list(range(i + 1)) for i in range(4)]
FOX = Group(CAUSAL, 2, DEC, [(1, 0, 2), (1, 384, 0), (2, 0, 1), (0, 0, 3), (3, 0, 4)])
BAND = Group(CAUSAL, 2, DEC, [(1, 0, 2), (1, 384, 0), (2, 0, 1), (0, 0, 3), (3, 0, 4)])
SWA = Group([[0], [0, 1], [1, 2], [2, 3]], 1, DEC, [(0, 0, 1), (0, 256, 2), (1, 0, 3), (1, 256, 0), (2, 0, 4)], sink=True)
MEM = Group([[0, 1]] * 4, 2, 0, [(0, 0, 0), (0, 256, 1), (1, 0, 2), (1, 256, 3), (2, 0, 4)])
SW = sum(w + 1 for w in FOX.width)
PTW = 10 * P + 3 * DEC

LN_PLAN = [("in", 0), ("mem", 0), ("out", 0), ("in", 1), ("mem", 1), ("mem", 2), ("out", 1), ("in", 2),
           ("mem", 3), ("mem", 4), ("out", 2), ("in", 3), ("mem", 5), ("mv", 4), ("out", 3), ("in", 4),
           ("mem", 6), ("mv", 5), ("out", 4), ("mem", 7), ("mv", 6), ("mv", 7)]
FILLS = [(k, i, b) for k, i in LN_PLAN if k in ("out", "mv") for b in (range(4) if k == "out" else [0])]
NF = len(FILLS)
LNF = 4 * NT


def own(eng, *values):
    out = []
    for v in values:
        if isinstance(v, int):
            out.append(v)
            continue
        NAMES.append(f"held{len(NAMES)}")
        reg = eng.alloc_register(NAMES[-1])
        eng.reg_mov(reg, v)
        out.append(eng.snap(reg, min_val=0, max_val=v.max_val))
    return out


NAMES = []


class Chain:

    def __init__(self, eng, sem):
        self.eng, self.sem, self.base, self.k = eng, sem, 0, 0

    def start(self, base):
        self.base, self.k = own(self.eng, base)[0], 0

    def step(self, ins):
        ins.then_inc(self.sem, 1)
        self.k += 1

    def wait(self):
        self.eng.wait_ge(self.sem, self.base + self.k)

    def link(self, ins):
        self.step(ins)
        self.wait()


def encoder_step(nc, wt, wff, bff, x_t, mem_t, fox_k, fox_v, fox_logf, band_k, band_v, swa_k, swa_v, mem_k, mem_v,
                 rel_pad, sinks, ln_gt, ln_bt, g_row, b_row, ident_d, causal_d, swa_mask_d, cos_d, sin_d,
                 y_o, fk_o, fv_o, fl_o, bk_o, bv_o, sk_o, sv_o, mk_o, mv_o):
    with ExitStack() as ctx:
        top = [nc.sbuf_base]
        top[0] += -top[0] % 64

        def sb_at(name, shape, off, dt=F32):
            return nc.alloc_sbuf_tensor_at(name, shape, dt, offset=off)

        def sb(name, shape, dt=F32):
            size = 4
            for s in shape[1:]:
                size *= s
            off = top[0]
            top[0] += size + -size % 64
            return sb_at(name, shape, off, dt)

        def sem(name):
            return ctx.enter_context(nc.semaphore(name))

        GB = ctx.enter_context(nc.psum_tensor("GB", [P, 4, 512], F32))
        AB = ctx.enter_context(nc.psum_tensor("AB", [P, 4, 512], F32))

        XH = sb("XH", [P, KC, TOK], F32R)
        XL = sb("XL", [P, KC, TOK], F32R)
        OY = sb("OY", [P, KC, TOK])
        WR = sb("WR", [P, 2, KC, P])
        WH = sb("WH", [P, 2, KC, P], F32R)
        WL = sb("WL", [P, 2, KC, P], F32R)
        XN = sb("XN", [P, DM])
        arena = top[0]
        MTH = sb("MTH", [P, KC, NMEM], F32R)
        MTL = sb("MTL", [P, KC, NMEM], F32R)
        FIN = sb_at("FIN", [P, 4, DM], arena)
        arena_end, top[0] = top[0], arena
        KT = sb("KT", [P, TOK])
        QT = sb("QT", [P, TOK])
        VT = sb("VT", [P, TOK])
        ES = sb("ES", [P, TOK])
        GA = sb("GA", [P, TOK])
        V = sb("V", [P, NT, HD])
        S = sb("S", [P, SW])
        PT = sb("PT", [P, PTW])
        KTC = sb("KTC", [P, PAST])
        VC = sb("VC", [P, 2, HD])
        BI = sb("BI", [P, SEQ + PAST + DEC])
        BD = sb("BD", [P, TOK])
        assert top[0] <= arena_end, (top[0], arena_end)
        top[0] = arena_end
        STG = sb_at("STG", [P, 2, 4, P], top[0])
        XR = sb("XR", [P, 2, TOK])
        MT = sb("MT", [P, 2, NMEM])
        MVN = sb("MVN", [P, 2, NMEM])
        ident = sb("ident", [P, P])
        causal = sb("causal", [P, P])
        swam = sb("swam", [P, 2 * P])
        cos = sb("cos", [P, TOK])
        sin = sb("sin", [P, TOK])
        snk = sb("snk", [P, DEPTH * GH])
        gT = sb("gT", [P, (DEPTH + 1) * KC])
        bT = sb("bT", [P, (DEPTH + 1) * KC])
        bF = sb("bF", [GH, DEPTH])
        WFR = sb("WFR", [P, KC, GH])
        WFF = sb("WFF", [P, KC, 2 * GH], F32R)
        CL = sb("CL", [GH, PAST])
        FFN = sb("FFN", [P, NT, GH])
        bst = sb("bst", [P, NT, 24])
        sml = sb("sml", [P, NT, 8])
        nmx = sb("nmx", [P, 8])
        esum = sb("esum", [P, 8])
        rsum = sb("rsum", [P, 8])
        one = sb("one", [P, 1])
        assert top[0] <= nc.sbuf_usable_end, (top[0], nc.sbuf_usable_end)
        LF, T1, NR = XN[0:GH, 0:TOK], XN[0:GH, TOK:2 * TOK], XN[0:GH, 2 * TOK:2 * TOK + SEQ + PAST + DEC]
        GROW, BROW = WR[:, 0, :, :].rearrange("p k c -> p (k c)"), WR[:, 1, :, :].rearrange("p k c -> p (k c)")

        x_res = nc.dram_tensor("x_res", (KC, P, TOK), F32, kind="Internal").ap()
        nc_rows = nc.dram_tensor("nc_rows", (GH, SEQ + PAST + DEC), F32, kind="Internal").ap()
        rel_rows = nc.dram_tensor("rel_rows", (DEPTH * GH, P, RELW), F32, kind="Internal").ap()
        toep = bass.AP(rel_rows.tensor, P - 1, [[P * RELW, DEPTH * GH], [RELW - 1, P], [1, SEQ]])

        s_const = sem("s_const")
        s_toep = sem("s_toep")
        s_x = sem("s_x")
        raw = [sem("raw0"), sem("raw1")]
        ld_mem = sem("ld_mem")
        ld_kc = sem("ld_kc")
        ld_vc = sem("ld_vc")
        ld_km = sem("ld_km")
        ld_vm = sem("ld_vm")
        ld_bias = sem("ld_bias")
        ld_ff = sem("ld_ff")
        ld_xr = [sem("ld_xr0"), sem("ld_xr1")]
        ld_rows = sem("ld_rows")
        o_k = sem("o_k")
        o_v = sem("o_v")
        o_mk = [sem("o_mk0"), sem("o_mk1")]
        o_mv = [sem("o_mv0"), sem("o_mv1")]
        o_x = [sem("o_x0"), sem("o_x1")]
        o_fl = sem("o_fl")
        o_rows = sem("o_rows")
        o_y0 = sem("o_y0")
        o_y = sem("o_y")
        hi = sem("hi")
        lo = sem("lo")
        zd = sem("zd")
        zf = [sem("zf0"), sem("zf1")]
        m_hi = sem("m_hi")
        m_lo = sem("m_lo")
        ti = sem("ti")
        vr = sem("vr")
        sd = sem("sd")
        bs = sem("bs")
        nrm = sem("nrm")
        to = sem("to")
        tf = sem("tf")
        xh = sem("xh")
        xl = sem("xl")
        ffh = sem("ffh")
        ffl = sem("ffl")
        ffd = sem("ffd")
        ffn = sem("ffn")
        fft = sem("fft")
        ffe = sem("ffe")
        ffa = sem("ffa")
        flr = sem("flr")
        ncr = sem("ncr")
        bdr = sem("bdr")
        bmr = sem("bmr")
        sc = [sem(f"sc{b}") for b in range(4)]
        mk = sem("mk")
        ex = sem("ex")
        pr = sem("pr")
        pt = sem("pt")
        pte = sem("pte")
        vt = sem("vt")
        ve = sem("ve")
        vse = sem("vse")
        pv = sem("pv")
        oe = sem("oe")
        eg = sem("eg")
        gd = sem("gd")
        oh = sem("oh")
        ol = sem("ol")
        c_dl = sem("c_dl")
        c_df = sem("c_df")
        c_da = sem("c_da")
        c_db = sem("c_db")
        c_dc = sem("c_dc")
        c_al = sem("c_al")
        f_ti = sem("f_ti")
        f_vr = sem("f_vr")
        f_sd = sem("f_sd")
        f_bs = sem("f_bs")
        f_nrm = sem("f_nrm")
        f_g = sem("f_g")
        f_y = sem("f_y")
        c_fin = sem("c_fin")
        s_rowg = sem("s_rowg")
        s_one = sem("s_one")

        block = ctx.enter_context(nc.Block())
        N_CONST = 9

        def z2(slot):
            return GB[:, 2 * slot:2 * slot + 2, 0:HALF]

        def split2(t):
            return t.rearrange("p (h c) -> p h c", h=2)

        def pt_col(j):
            return PT[:, P * j:P * (j + 1)]

        def wait_apart(eng, sem, count):
            held, = own(eng, count)
            eng.wait_ge(s_one, 1)
            eng.wait_ge(sem, held)

        @block.sync
        def _(sp):
            for n in range(2):
                sp.dma_start(WR[:, n, :, :], wt[n]).then_inc(raw[n], 16)
            with sp.Fori(1, DEPTH * LT // 2) as m:
                nc.cur_bb.disable_value_cache()
                for s in range(2):
                    sp.wait_ge(lo, m * 2 + s - 1)
                    sp.dma_start(WR[:, s, :, :], wt[m * 2 + s]).then_inc(raw[s], 16)
            sp.wait_ge(lo, DEPTH * LT)
            sp.dma_start(GROW, g_row.partition_broadcast(P)).then_inc(s_rowg, 16)
            sp.dma_start(BROW, b_row.partition_broadcast(P)).then_inc(s_rowg, 16)
            sp.wait_ge(s_rowg, 32)

        @block.tensor
        def _(pe):
            def gemm_half(n, s, hf, first=None):
                if hf == 0:
                    pe.wait_ge(lo, n + 1)
                    pe.wait_ge(zf[s], first[0])
                for k in range(KC):
                    if hf == 0 and first[1] is not None:
                        pe.wait_ge(ol, first[1] + k + 1)
                    for i, (w, x) in enumerate(((WH, XH), (WL, XH), (WH, XL))):
                        mm = pe.matmul(GB[:, 2 * s + hf, 0:HALF], w[:, s, k, :],
                                       x[:, k, hf * HALF:(hf + 1) * HALF],
                                       start=(k == 0 and i == 0), stop=(k == KC - 1 and i == 2))
                if hf == 1:
                    mm.then_inc(zd, 1)

            def gemm(n, m, j, hf=None, split=None):
                for h in (range(2) if hf is None else [hf]):
                    gemm_half(n + j, j % 2, h, (m + j // 2, split))

            def scores(g, u, dm=None, fl=None):
                if g is FOX:
                    pe.wait_ge(flr, fl)
                if g is MEM:
                    pe.wait_ge(ld_km, 16 * (dm + 1))
                for j, (b, col, i) in enumerate(g.place):
                    t0, r = TILES[i]
                    if b >= 2:
                        pe.wait_ge(oe, 2 * u)
                    if i < 4:
                        ks = g.blocks[i][0] * P
                        mm = pe.matmul(AB[:, b, col:col + g.width[i]], QT[:, t0:t0 + r], KT[:, ks:ks + g.width[i]],
                                       start=True, stop=True)
                    else:
                        w = P * g.cached
                        mm = pe.matmul(AB[0:DEC, b, col:col + w], QT[:, t0:t0 + r], KTC[:, 0:w],
                                       start=True, stop=True)
                        if g.own:
                            mm = pe.matmul(AB[0:DEC, b, col + w:col + w + DEC], QT[:, t0:t0 + r], KT[:, SEQ:TOK],
                                           start=True, stop=True)
                    if j == len(g.place) - 1 or g.place[j + 1][0] != b:
                        mm.then_inc(sc[b], 1)

            def turn_probs(g, u):
                pe.wait_ge(pr, 5 * u + 5)
                j = 0
                blocks = [(i, b) for i in range(4) for b in range(len(g.blocks[i]))]
                for j, (i, b) in enumerate(blocks):
                    at = g.at[i] + P * b
                    mm = pe.transpose(AB[:, j // 4, P * (j % 4):P * (j % 4 + 1)], S[:, at:at + P], ident[:, :])
                    if j in (3, 7) or (j == len(blocks) - 1 and j < 7):
                        mm.then_inc(pt, 1)
                for b in range(g.cached):
                    mm = pe.transpose(AB[:, 2, 256 + DEC * b:256 + DEC * (b + 1)],
                                      S[0:DEC, g.at[4] + P * b:g.at[4] + P * (b + 1)], ident[0:DEC, 0:DEC])
                if g.own:
                    at = g.at[4] + P * g.cached
                    mm = pe.transpose(AB[0:DEC, 2, 320:320 + DEC], S[0:DEC, at:at + DEC], ident[0:DEC, 0:DEC])
                return mm

            def turn_v(m):
                pe.wait_ge(zf[0], m)
                mm = pe.transpose(AB[0:DEC, 2, 352:352 + P], VT[:, SEQ:TOK], ident[:, :])
                mm.then_inc(pt, 1)
                for i in range(4):
                    mm = pe.transpose(AB[:, 3, P * i:P * (i + 1)], VT[:, P * i:P * (i + 1)], ident[:, :])
                mm.then_inc(vt, 1)

            def mix(g, u, kl, vu=None, dm=None):
                pe.wait_ge(pte, 3 * u + 3)
                pe.wait_ge(ld_vc, 16 * (kl + 1))
                if vu is not None:
                    pe.wait_ge(ve, vu + 1)
                    pe.wait_ge(vse, vu + 1)
                if dm is not None:
                    pe.wait_ge(ld_vm, 16 * (dm + 1))
                j = 0
                for i in range(4):
                    for b, kb in enumerate(g.blocks[i]):
                        mm = pe.matmul(AB[:, 3, P * i:P * (i + 1)], V[:, kb, :], pt_col(j),
                                       start=(b == 0), stop=(b == len(g.blocks[i]) - 1))
                        j += 1
                mm.then_inc(pv, 1)
                for b in range(g.cached):
                    mm = pe.matmul(AB[:, 2, 0:DEC], VC[:, b, :], PT[:, 10 * P + DEC * b:10 * P + DEC * (b + 1)],
                                   start=(b == 0), stop=(b == g.cached - 1 and not g.own))
                if g.own:
                    mm = pe.matmul(AB[:, 2, 0:DEC], V[0:DEC, 4, :], PT[0:DEC, 10 * P + 2 * DEC:10 * P + 3 * DEC],
                                   start=False, stop=True)
                mm.then_inc(pv, 1)

            def head(g, n, m, u, kl, vu, fl):
                n, m, u, kl, vu, fl = own(pe, n, m, u, kl, vu, fl)
                gemm(n, m, 0)
                gemm(n, m, 1)
                gemm(n, m, 2, 0)
                pe.wait_ge(zf[0], m + 1)
                pe.wait_ge(zf[1], m + 1)
                pe.wait_ge(ld_kc, 16 * (kl + 1))
                scores(g, u, fl=fl)
                gemm(n, m, 2, 1)
                gemm(n, m, 3, 0)
                turn_probs(g, u)
                turn_v(m + 2)
                gemm(n, m, 3, 1)
                mix(g, u, kl, vu)

            def pair(n, m, u, kl, vu, dm):
                n, m, u, kl, vu, dm = own(pe, n, m, u, kl, vu, dm)
                gemm(n, m, 0)
                gemm(n, m, 1)
                gemm(n, m, 2, 0)
                pe.wait_ge(zf[0], m + 1)
                pe.wait_ge(zf[1], m + 1)
                pe.wait_ge(ld_kc, 16 * (kl + 1))
                scores(SWA, u)
                gemm(n, m, 2, 1)
                gemm(n, m, 3, 0)
                turn_probs(SWA, u)
                turn_v(m + 2)
                gemm(n, m, 3, 1)
                mix(SWA, u, kl, vu)
                gemm(n, m, 4, 0)
                pe.wait_ge(zf[1], m + 2)
                scores(SWA, u + 1)
                gemm(n, m, 4, 1)
                gemm(n, m, 5, 0)
                turn_probs(SWA, u + 1).then_inc(pt, 1)
                gemm(n, m, 5, 1)
                mix(SWA, u + 1, kl, vu)
                pe.wait_ge(zf[0], m + 3)
                pe.wait_ge(ld_kc, 16 * (kl + 2))
                scores(MEM, u + 2, dm)
                gemm(n, m, 6)
                turn_probs(MEM, u + 2).then_inc(pt, 1)
                gemm(n, m, 7, 0)
                mix(MEM, u + 2, kl + 1, dm=dm)
                pe.wait_ge(zf[1], m + 3)
                pe.wait_ge(ld_kc, 16 * (kl + 3))
                scores(MEM, u + 3, dm + 1)
                gemm(n, m, 7, 1)
                gemm(n, m, 8, 0)
                turn_probs(MEM, u + 3).then_inc(pt, 1)
                gemm(n, m, 8, 1)
                mix(MEM, u + 3, kl + 2, dm=dm + 1)
                gemm(n, m, 9)

            def turn_in(t, base, done):
                t0, r = TILES[t]
                for c in range(KC):
                    mm = pe.transpose(AB[0:r, c // 4, P * (c % 4):P * (c % 4 + 1)], OY[:, c, t0:t0 + r], ident[:, :])
                    if c % 4 == 3:
                        mm.then_inc(done, 1)

            def mem_tile(l, j):
                s, n = j % 2, l * LT + j
                pe.wait_ge(lo, n + 1)
                pe.wait_ge(zf[s], l * (LT // 2) + j // 2)
                if j == 0:
                    pe.wait_ge(m_lo, 2 * (l + 1))
                for k in range(KC):
                    for i, (w, x) in enumerate(((WH, MTH), (WL, MTH), (WH, MTL))):
                        mm = pe.matmul(GB[:, 2 * s, 0:NMEM], w[:, s, k, :], x[:, k, :],
                                       start=(k == 0 and i == 0), stop=(k == KC - 1 and i == 2))
                mm.then_inc(zd, 1)

            pe.wait_ge(s_const, 16 * N_CONST)
            pe.wait_ge(s_x, 16)
            with pe.Fori(0, DEPTH) as layer:
                nc.cur_bb.disable_value_cache()
                l, = own(pe, layer)
                f = 0
                for s in range(2):
                    pe.wait_ge(zf[s], l * (LT // 2))
                for kind, i in LN_PLAN:
                    if kind == "in":
                        turn_in(i, l, ti)
                    elif kind == "mem":
                        mem_tile(l, i)
                    else:
                        for b in (range(4) if kind == "out" else [0]):
                            if f >= 2:
                                pe.wait_ge(tf, l * NF + f - 1)
                            else:
                                pe.wait_ge(tf, l * NF)
                            bank = GB[:, 1 + 2 * (f % 2), :]
                            if kind == "out":
                                t0, r = TILES[i]
                                wait_apart(pe, nrm, l * LNF + 4 * i + b + 1)
                                for c in range(4):
                                    at = 512 * b + P * c
                                    mm = pe.transpose(bank[:, r * c:r * (c + 1)], XN[0:r, at:at + P], ident[0:r, 0:r])
                            else:
                                pe.wait_ge(zf[i % 2], l * (LT // 2) + i // 2 + 1)
                                for c in range(2):
                                    mm = pe.transpose(bank[:, P * c:P * (c + 1)], MT[:, i % 2, P * c:P * (c + 1)],
                                                      ident[:, :])
                            mm.then_inc(to, 1)
                            f += 1
                pe.wait_ge(xl, LNF * (l + 1))
                pe.wait_ge(ffl, l + 1)
                pe.wait_ge(tf, (l + 1) * NF)
                for t, (t0, r) in enumerate(TILES):
                    for k in range(KC):
                        at = 2 * GH * t
                        pe.matmul(AB[0:r, 0, at:at + 2 * GH], XH[:, k, t0:t0 + r], WFF[:, k, :],
                                  start=(k == 0), stop=False, skip_group_check=True)
                        mm = pe.matmul(AB[0:r, 0, at:at + GH], XL[:, k, t0:t0 + r], WFF[:, k, 0:GH],
                                       start=False, stop=(k == KC - 1), skip_group_check=True)
                mm.then_inc(ffd, 1)
                pe.wait_ge(ffn, l + 1)
                for t, (t0, r) in enumerate(TILES):
                    mm = pe.transpose(AB[0:GH, 1 + t // 4, P * (t % 4):P * (t % 4) + r], FFN[0:r, t, :], ident[0:r, 0:r])
                mm.then_inc(fft, 1)
                l, = own(pe, layer)
                for gi, (g, first) in enumerate(((FOX, A0), (BAND, B0))):
                    with pe.Fori(0, GH) as h:
                        nc.cur_bb.disable_value_cache()
                        head(g, l * LT + first + h * HEAD_TILES, l * (LT // 2) + first // 2 + h * 2,
                             l * HEADS + GH * gi + h, l * K_LOADS + GH * gi + h, l * V_UNITS + GH * gi + h, l + 1)
                with pe.Fori(0, PAIRS) as j:
                    nc.cur_bb.disable_value_cache()
                    pair(l * LT + C0 + j * PAIR_TILES, l * (LT // 2) + C0 // 2 + j * (PAIR_TILES // 2),
                         l * HEADS + 2 * GH + j * 4, l * K_LOADS + 2 * GH + j * 3, l * V_UNITS + 2 * GH + j,
                         l * GH + 2 * j)
                n, m = l * LT + O0, l * (LT // 2) + O0 // 2
                gemm(n, m, 0, split=l * KC)
                gemm(n, m, 1)
                with pe.Fori(1, KC // 2) as q:
                    nc.cur_bb.disable_value_cache()
                    gemm(n + q * 2, m + q, 0)
                    gemm(n + q * 2, m + q, 1)
            for s in range(2):
                pe.wait_ge(zf[s], DEPTH * (LT // 2))
            for t in range(NT):
                if t:
                    pe.wait_ge(f_nrm, 4 * t)
                turn_in(t, 0, f_ti)

        @block.scalar
        def _(act):
            chain = Chain(act, c_al)

            def w_hi(n, s, m):
                act.wait_ge(raw[s], 16 * (m + 1))
                act.copy(WH[:, s, :, :], WR[:, s, :, :]).then_inc(hi, 1)

            def tile_done(n, m, j, ahead=True):
                act.wait_ge(zd, n + j + 1)
                if ahead:
                    w_hi(n + j + 2, j % 2, m + j // 2 + 1)

            def exps(g, u, kl=None):
                for j, i in enumerate(g.order):
                    act.wait_ge(mk, 5 * u + j + 1)
                    r, w = TILES[i][1], g.width[i] + g.sink
                    s = S[0:r, g.at[i]:g.at[i] + w]
                    act.activation(s, s, ACT.Exp, bias=nmx[0:r, i:i + 1],
                                   accum_out=esum[0:r, i:i + 1]).then_inc(ex, 1)

            def take_v(vu):
                act.wait_ge(vt, vu + 1)
                act.copy(V[:, 0:4, :], AB[:, 3, :].rearrange("p (b d) -> p b d", b=4)).then_inc(ve, 1)

            def take_o(u, c):
                act.wait_ge(pv, 2 * u + 1)
                act.copy(OY[:, c, 0:SEQ], AB[:, 3, :]).then_inc(oe, 1)
                act.wait_ge(pv, 2 * u + 2)
                act.copy(OY[:, c, SEQ:TOK], AB[:, 2, 0:DEC]).then_inc(oe, 1)

            def gate_exp(s, u):
                act.wait_ge(gd, u)
                act.activation(split2(ES[:, :]), z2(s), ACT.Exp, scale=-1.0).then_inc(eg, 1)

            def take_v_tile(vu):
                act.wait_ge(o_v, 16 * vu)
                act.copy(split2(VT[:, :]), z2(0)).then_inc(zf[0], 1)

            def head(g, n, m, u, vu, c):
                n, m, u, vu = own(act, n, m, u, vu)
                tile_done(n, m, 0)
                act.wait_ge(o_k, 16 * vu)
                act.copy(split2(KT[:, :]), z2(0)).then_inc(zf[0], 1)
                tile_done(n, m, 1)
                act.mul(split2(QT[:, :]), z2(1), SCALE).then_inc(zf[1], 1)
                exps(g, u)
                tile_done(n, m, 2)
                take_v_tile(vu)
                take_v(vu)
                tile_done(n, m, 3)
                gate_exp(1, u)
                take_o(u, c)

            def pair(n, m, u, vu, j):
                n, m, u, vu = own(act, n, m, u, vu)
                tile_done(n, m, 0)
                tile_done(n, m, 1)
                exps(SWA, u)
                tile_done(n, m, 2)
                take_v_tile(vu)
                take_v(vu)
                tile_done(n, m, 3)
                take_o(u, 2 * GH + j * 2)
                exps(SWA, u + 1)
                tile_done(n, m, 4)
                act.mul(split2(QT[:, :]), z2(0), SCALE).then_inc(zf[0], 1)
                tile_done(n, m, 5)
                take_o(u + 1, 2 * GH + 1 + j * 2)
                act.wait_ge(sc[2], u + 3)
                act.mul(split2(QT[:, :]), z2(1), SCALE).then_inc(zf[1], 1)
                exps(MEM, u + 2)
                tile_done(n, m, 6)
                gate_exp(0, u)
                take_o(u + 2, 3 * GH + j * 2)
                exps(MEM, u + 3)
                tile_done(n, m, 7)
                gate_exp(1, u + 1)
                tile_done(n, m, 8)
                gate_exp(0, u + 2)
                take_o(u + 3, 3 * GH + 1 + j * 2)
                tile_done(n, m, 9)
                gate_exp(1, u + 3)

            def mem_hi(q):
                for p in range(2):
                    act.wait_ge(ld_mem, 16 * (2 * q + p + 1))
                    act.copy(MTH[:, 8 * p:8 * p + 8, :], XN[:, :].rearrange("p (k c) -> p k c", k=8)).then_inc(m_hi, 1)

            def seed(t, var_ready, at, out):
                r = TILES[t][1]
                act.wait_ge(var_ready, at + t + 1)
                chain.link(act.activation(sml[0:r, t, 6:7], sml[0:r, t, 2:3], ACT.Ln))
                act.activation(sml[0:r, t, 3:4], sml[0:r, t, 6:7], ACT.Exp, scale=-0.5).then_inc(out, 1)

            def norm(t, ready, at, done):
                r = TILES[t][1]
                act.wait_ge(ready, at + t + 1)
                for b in range(4):
                    act.activation(XN[0:r, 512 * b:512 * (b + 1)], AB[0:r, b, :], ACT.Identity,
                                   bias=sml[0:r, t, 5:6], scale=sml[0:r, t, 4:5]).then_inc(done, 1)

            def mem_done(l, j):
                n, s = l * LT + j, j % 2
                act.wait_ge(zd, n + 1)
                w_hi(n + 2, s, l * (LT // 2) + j // 2 + 1)
                if j >= 2:
                    if j - 2 < GH:
                        act.wait_ge(o_mk[s], 16 * (l * (GH // 2) + (j - 2) // 2 + 1))
                    else:
                        act.wait_ge(to, l * NF + FILLS.index(("mv", j - 2, 0)) + 1)
                act.copy(MT[:, s, :], GB[:, 2 * s, 0:NMEM]).then_inc(zf[s], 1)
                if j < GH:
                    act.wait_ge(zf[s], l * (LT // 2) + j // 2 + 1)
                    act.dma_start(mk_o[l, j], MT[:, s, :]).then_inc(o_mk[s], 16)

            def split_x(l, t):
                t0, r = TILES[t]
                for b in range(4):
                    f = 4 * t + b
                    act.wait_ge(tf, l * NF + FILLS.index(("out", t, b)) + 1)
                    act.copy(XH[:, 4 * b:4 * b + 4, t0:t0 + r], STG[:, f % 2, :, 0:r]).then_inc(xh, 1)
                    act.dma_start(x_res[4 * b:4 * b + 4, :, t0:t0 + r].rearrange("c p t -> p c t"),
                                  STG[:, f % 2, :, 0:r]).then_inc(o_x[f % 2], 16)

            act.wait_ge(s_one, 1)
            mem_hi(0)
            with act.Fori(0, DEPTH) as layer:
                nc.cur_bb.disable_value_cache()
                l, = own(act, layer)
                chain.start(l * (NT + 1))
                act.wait_ge(zd, l * LT)
                for s in range(2):
                    w_hi(l * LT + s, s, l * (LT // 2))
                act.wait_ge(ld_ff, 32 * (l + 1))
                act.copy(WFF[:, :, 0:GH], WFR[:, :, :]).then_inc(ffh, 1)
                seed(0, vr, l * NT, sd)
                norm(0, bs, l * NT, nrm)
                for kind, i in LN_PLAN[1:]:
                    if kind == "in":
                        split_x(l, i - 1)
                        seed(i, vr, l * NT, sd)
                        norm(i, bs, l * NT, nrm)
                    elif kind == "mem":
                        if i == MEM_TILES - 1:
                            split_x(l, NT - 1)
                        mem_done(l, i)
                act.wait_ge(ffa, l + 1)
                chain.link(act.activation(T1, T1, ACT.Exp, scale=-1.0))
                act.activation(T1, T1, ACT.Ln, bias=1.0).then_inc(ffe, 1)
                assert chain.k == NT + 1, chain.k
                l, = own(act, layer)
                for gi, (g, first) in enumerate(((FOX, A0), (BAND, B0))):
                    with act.Fori(0, GH) as h:
                        nc.cur_bb.disable_value_cache()
                        head(g, l * LT + first + h * HEAD_TILES, l * (LT // 2) + first // 2 + h * 2,
                             l * HEADS + GH * gi + h, l * V_UNITS + GH * gi + h, h + GH * gi)
                with act.Fori(0, PAIRS) as j:
                    nc.cur_bb.disable_value_cache()
                    pair(l * LT + C0 + j * PAIR_TILES, l * (LT // 2) + C0 // 2 + j * (PAIR_TILES // 2),
                         l * HEADS + 2 * GH + j * 4, l * V_UNITS + 2 * GH + j, j)
                act.wait_ge(gd, HEADS * (l + 1))
                for c in range(KC):
                    act.copy(XH[:, c, :], OY[:, c, :]).then_inc(oh, 1)
                mem_hi(l + 1)
                n, m = l * LT + O0, l * (LT // 2) + O0 // 2
                with act.Fori(0, KC // 2 - 1) as q:
                    nc.cur_bb.disable_value_cache()
                    tile_done(n + q * 2, m + q, 0)
                    tile_done(n + q * 2, m + q, 1)
            chain.start(DEPTH * (NT + 1))
            for t in range(NT):
                seed(t, f_vr, 0, f_sd)
                if t:
                    act.wait_ge(f_g, 4 * t)
                norm(t, f_bs, 0, f_nrm)

        @block.vector
        def _(dve):
            chain = Chain(dve, c_dl)

            def w_lo(n, s):
                dve.wait_ge(hi, n + 1)
                dve.tensor_tensor(WL[:, s, :, :], WR[:, s, :, :], WH[:, s, :, :].bitcast(F32),
                                  ALU.subtract).then_inc(lo, 1)

            def soft_in(g, u, l=None, j=None, k=0):
                if g is FOX:
                    dve.wait_ge(bdr, 2 * (l * GH + j + 1))
                if g is BAND:
                    dve.wait_ge(bmr, l * GH + j + 1)
                for b, col, i in g.place:
                    t0, r = TILES[i]
                    w, at = g.width[i], g.at[i]
                    dve.wait_ge(sc[b], (l * 2 * GH + (GH if g is BAND else 0) + j if b == 3 else u) + 1)
                    src, dst = AB[0:r, b, col:col + w], S[0:r, at:at + w]

                    def add(c0, c1, bias, ):
                        chain.step(dve.tensor_tensor(dst[:, c0:c1], src[:, c0:c1], bias, ALU.add))
                    if g is FOX:
                        if i == 4:
                            add(0, PAST, BI[0:r, SEQ:SEQ + PAST])
                            add(PAST, w, BD[0:r, SEQ:TOK])
                        else:
                            if i:
                                add(0, P * i, BI[:, 0:P * i])
                            add(P * i, w, BD[:, P * i:P * (i + 1)])
                    elif g is BAND:
                        if i == 4:
                            add(0, w, BI[0:r, P:P + w])
                        else:
                            add(0, w, BI[:, SEQ - w:SEQ])
                    elif g is SWA and i < 4:
                        add(0, w, swam[:, 2 * P - w:2 * P])
                    else:
                        chain.step(dve.tensor_copy(dst, src))
                    if g.sink:
                        at_s = l * GH + j * 2 + k
                        chain.step(dve.tensor_copy(S[0:r, at + w:at + w + 1], snk[0:r, bass.ds(at_s, 1)]))
                    chain.wait()
                    dve.tensor_reduce(nmx[0:r, i:i + 1], S[0:r, at:at + w + g.sink], AX_X, ALU.max,
                                      negate=True).then_inc(mk, 1)

            def soft_out(g, u):
                dve.wait_ge(ex, 5 * u + 5)
                chain.link(dve.reciprocal(rsum[:, 0:NT], esum[:, 0:NT]))
                for i in g.order:
                    r, w = TILES[i][1], g.width[i]
                    s = S[0:r, g.at[i]:g.at[i] + w]
                    dve.tensor_scalar(s, s, rsum[0:r, i:i + 1], None, ALU.mult).then_inc(pr, 1)

            def take_probs(g, u, vu=None):
                n = sum(len(b) for b in g.blocks)
                for b in range(2):
                    dve.wait_ge(pt, 3 * u + b + 1)
                    w = P * min(4, n - 4 * b)
                    dve.tensor_copy(PT[:, 512 * b:512 * b + w], AB[:, b, 0:w]).then_inc(pte, 1)
                dve.wait_ge(pt, 3 * u + 3)
                if n > 8:
                    dve.tensor_copy(PT[:, 8 * P:n * P], AB[:, 2, 0:(n - 8) * P])
                ins = dve.tensor_copy(PT[:, 10 * P:10 * P + DEC * g.cached], AB[:, 2, 256:256 + DEC * g.cached])
                if g.own:
                    ins = dve.tensor_copy(PT[0:DEC, 10 * P + 2 * DEC:PTW], AB[0:DEC, 2, 320:320 + DEC])
                ins.then_inc(pte, 1)
                if vu is not None:
                    dve.tensor_copy(V[0:DEC, 4, :], AB[0:DEC, 2, 352:352 + P]).then_inc(vse, 1)

            def gate(s, u, c, zf_n):
                dve.wait_ge(eg, u + 1)
                chain.link(dve.tensor_scalar(ES[:, :], ES[:, :], 1.0, None, ALU.add))
                chain.link(dve.reciprocal(ES[:, :], ES[:, :]))
                dve.tensor_tensor(split2(GA[:, :]), z2(s), split2(ES[:, :]), ALU.mult).then_inc(zf[s], 1)
                dve.wait_ge(zf[s], zf_n)
                dve.wait_ge(oe, 2 * u + 2)
                dve.tensor_tensor(OY[:, c, :], OY[:, c, :], GA[:, :], ALU.mult).then_inc(gd, 1)

            def rope(s, dst, sw, scale, k_before=None):
                h = HD // 2
                chain.step(dve.tensor_copy(split2(sw[0:h, :]), z2(s)[h:HD]))
                chain.step(dve.tensor_copy(split2(sw[h:HD, :]), z2(s)[0:h]))
                chain.wait()
                chain.step(dve.tensor_tensor(sw[:, :], sw[:, :], sin[:, :], ALU.mult))
                if k_before is not None:
                    dve.wait_ge(o_k, 16 * k_before)
                chain.link(dve.tensor_tensor(split2(dst[:, :]), z2(s), split2(cos[:, :]), ALU.mult))
                if scale is None:
                    dve.tensor_tensor(dst[:, :], dst[:, :], sw[:, :], ALU.add).then_inc(zf[s], 1)
                else:
                    chain.link(dve.tensor_tensor(dst[:, :], dst[:, :], sw[:, :], ALU.add))
                    dve.tensor_scalar(dst[:, :], dst[:, :], scale, None, ALU.mult).then_inc(zf[s], 1)

            def head(g, n, m, u, vu, l, h, c):
                n, m, u, vu, l = own(dve, n, m, u, vu, l)
                w_lo(n + 2, 0)
                w_lo(n + 3, 1)
                soft_in(g, u, l, h)
                soft_out(g, u)
                w_lo(n + 4, 0)
                take_probs(g, u, vu)
                w_lo(n + 5, 1)
                gate(1, u, c, m + 2)

            def pair(n, m, u, vu, l, j):
                n, m, u, vu, l = own(dve, n, m, u, vu, l)
                dve.wait_ge(zd, n + 1)
                w_lo(n + 2, 0)
                dve.wait_ge(gd, u)
                rope(0, KT, GA, None, vu)
                w_lo(n + 3, 1)
                rope(1, QT, ES, SCALE)
                soft_in(SWA, u, l, j, 0)
                soft_out(SWA, u)
                w_lo(n + 4, 0)
                take_probs(SWA, u, vu)
                w_lo(n + 5, 1)
                rope(1, QT, ES, SCALE)
                soft_in(SWA, u + 1, l, j, 1)
                soft_out(SWA, u + 1)
                w_lo(n + 6, 0)
                take_probs(SWA, u + 1)
                w_lo(n + 7, 1)
                soft_in(MEM, u + 2)
                soft_out(MEM, u + 2)
                take_probs(MEM, u + 2)
                w_lo(n + 8, 0)
                gate(0, u, 2 * GH + j * 2, m + 4)
                soft_in(MEM, u + 3)
                soft_out(MEM, u + 3)
                w_lo(n + 9, 1)
                gate(1, u + 1, 2 * GH + 1 + j * 2, m + 4)
                take_probs(MEM, u + 3)
                w_lo(n + 10, 0)
                gate(0, u + 2, 3 * GH + j * 2, m + 5)
                w_lo(n + 11, 1)
                gate(1, u + 3, 3 * GH + 1 + j * 2, m + 5)

            def mem_lo(q):
                for p in range(2):
                    dve.wait_ge(m_hi, 2 * q + p + 1)
                    mh = MTH[:, 8 * p:8 * p + 8, :]
                    dve.tensor_tensor(MTL[:, 8 * p:8 * p + 8, :], XN[:, :].rearrange("p (k c) -> p k c", k=8),
                                      mh.bitcast(F32), ALU.subtract).then_inc(m_lo, 1)

            def stats(t, banks, at, var_ready, seeded, ready):
                r = TILES[t][1]
                for b in range(4):
                    dve.wait_ge(banks, 4 * (at + t) + b + 1)
                    chain.step(dve.bn_stats(bst[0:r, t, 6 * b:6 * b + 6], AB[0:r, b, :]))
                wait_apart(dve, chain.sem, chain.base + chain.k)
                s = sml[0:r, t, :]
                chain.link(dve.bn_aggr(s[:, 0:2], bst[0:r, t, :]))
                dve.tensor_scalar(s[:, 2:3], s[:, 1:2], EPS, None, ALU.add).then_inc(var_ready, 1)
                dve.wait_ge(seeded, at + t + 1)
                chain.link(dve.scalar_tensor_tensor(s[:, 7:8], s[:, 3:4], s[:, 2:3], s[:, 3:4], ALU.mult, ALU.mult))
                chain.link(dve.tensor_scalar(s[:, 7:8], s[:, 7:8], -0.5, 1.5, ALU.mult, ALU.add))
                chain.link(dve.tensor_tensor(s[:, 4:5], s[:, 3:4], s[:, 7:8], ALU.mult))
                dve.scalar_tensor_tensor(s[:, 5:6], s[:, 0:1], -1.0, s[:, 4:5], ALU.mult, ALU.mult).then_inc(ready, 1)

            def take_fill(l, f):
                kind, i, b = FILLS[f]
                bank = GB[:, 1 + 2 * (f % 2), :]
                dve.wait_ge(to, l * NF + f + 1)
                if kind == "out":
                    r = TILES[i][1]
                    q = 4 * i + b
                    dve.wait_ge(xl, l * LNF + q - 1 if q >= 2 else l * LNF)
                    dve.wait_ge(o_x[q % 2], 16 * (l * (LNF // 2) + q // 2))
                    for c in range(4):
                        at = l * KC + 4 * b + c
                        ins = dve.tensor_scalar(STG[:, q % 2, c, 0:r], bank[:, r * c:r * (c + 1)],
                                                gT[:, bass.ds(at, 1)], bT[:, bass.ds(at, 1)], ALU.mult, ALU.add)
                        if c == 3:
                            ins.then_inc(tf, 1)
                else:
                    dve.wait_ge(o_mv[i % 2], 16 * (l * (GH // 2) + (i - GH) // 2))
                    dve.tensor_copy(MVN[:, i % 2, :], bank[:, 0:NMEM]).then_inc(tf, 1)

            dve.memset(esum[:, :], 1.0)
            dve.memset(one[:, :], 1.0).then_inc(s_one, 1)
            dve.wait_ge(s_one, 1)
            mem_lo(0)
            dve.wait_ge(s_const, 16 * N_CONST)
            with dve.Fori(0, DEPTH) as layer:
                nc.cur_bb.disable_value_cache()
                l, = own(dve, layer)
                chain.sem = c_dl
                chain.start(l * CH["ln"])
                for s in range(2):
                    w_lo(l * LT + s, s)
                dve.wait_ge(ffh, l + 1)
                dve.tensor_tensor(WFF[:, :, GH:2 * GH], WFR[:, :, :], WFF[:, :, 0:GH].bitcast(F32),
                                  ALU.subtract).then_inc(ffl, 1)
                stats(0, ti, l * NT, vr, sd, bs)
                f = 0
                for kind, i in LN_PLAN[1:]:
                    if kind == "in":
                        stats(i, ti, l * NT, vr, sd, bs)
                    elif kind == "mem":
                        w_lo(l * LT + i + 2, i % 2)
                    else:
                        for b in range(4 if kind == "out" else 1):
                            take_fill(l, f)
                            f += 1
                assert chain.k == CH["ln"], ("ln", chain.k)
                chain.sem = c_df
                chain.start(l * CH["ff"])
                dve.wait_ge(ffd, l + 1)
                dve.tensor_reduce(FFN[:, 0:4, :], AB[:, 0, 0:32].rearrange("p (t s h) -> p t h s", t=4, s=2),
                                  AX_X, ALU.add)
                dve.tensor_reduce(FFN[0:DEC, 4, :], AB[0:DEC, 0, 32:40].rearrange("p (s h) -> p h s", s=2),
                                  AX_X, ALU.add).then_inc(ffn, 1)
                dve.wait_ge(fft, l + 1)
                bf = bF[:, bass.ds(l, 1)]
                chain.step(dve.tensor_scalar(LF[:, 0:SEQ], AB[0:GH, 1, :], bf, None, ALU.add))
                chain.link(dve.tensor_scalar(LF[:, SEQ:TOK], AB[0:GH, 2, 0:DEC], bf, None, ALU.add))
                dve.scalar_tensor_tensor(T1, LF, -1.0, LF, ALU.mult, ALU.max).then_inc(ffa, 1)
                dve.wait_ge(ffe, l + 1)
                dve.scalar_tensor_tensor(LF, LF, 0.0, T1, ALU.min, ALU.subtract).then_inc(flr, 1)
                dve.wait_ge(flr, l + 1)
                ones = one[0:GH, 0:1]
                chain.step(dve.tensor_tensor_scan(NR[:, 0:SEQ], ones.broadcast_to([GH, SEQ]), LF[:, 0:SEQ], 0.0,
                                                  ALU.mult, ALU.subtract))
                chain.link(dve.tensor_tensor_scan(NR[:, SEQ:SEQ + PAST], ones.broadcast_to([GH, PAST]), CL[:, :], 0.0,
                                                  ALU.mult, ALU.subtract))
                dve.tensor_tensor_scan(NR[:, SEQ + PAST:], ones.broadcast_to([GH, DEC]), LF[:, SEQ:TOK],
                                       NR[:, SEQ + PAST - 1:SEQ + PAST], ALU.mult, ALU.subtract).then_inc(ncr, 1)
                assert chain.k == CH["ff"], ("ff", chain.k)
                l, = own(dve, layer)
                for gi, (g, first, key, csem) in enumerate(((FOX, A0, "fox", c_da), (BAND, B0, "band", c_db))):
                    with dve.Fori(0, GH) as h:
                        nc.cur_bb.disable_value_cache()
                        chain.sem = csem
                        chain.start((l * GH + h) * CH[key])
                        head(g, l * LT + first + h * HEAD_TILES, l * (LT // 2) + first // 2 + h * 2,
                             l * HEADS + GH * gi + h,
                             l * V_UNITS + GH * gi + h, l, h, h + GH * gi)
                        assert chain.k == CH[key], (key, chain.k)
                with dve.Fori(0, PAIRS) as j:
                    nc.cur_bb.disable_value_cache()
                    chain.sem = c_dc
                    chain.start((l * PAIRS + j) * CH["pair"])
                    pair(l * LT + C0 + j * PAIR_TILES, l * (LT // 2) + C0 // 2 + j * (PAIR_TILES // 2), l * HEADS + 2 * GH + j * 4, l * V_UNITS + 2 * GH + j, l, j)
                    assert chain.k == CH["pair"], ("pair", chain.k)
                for c in range(KC):
                    dve.wait_ge(oh, l * KC + c + 1)
                    dve.tensor_tensor(XL[:, c, :], OY[:, c, :], XH[:, c, :].bitcast(F32), ALU.subtract).then_inc(ol, 1)
                mem_lo(l + 1)

                def residual(c, s, count, xr):
                    dve.wait_ge(zd, count)
                    dve.wait_ge(ld_xr[s], xr)
                    dve.scalar_tensor_tensor(split2(OY[:, c, :]), split2(XR[:, s, :]), ALPHA, z2(s),
                                             ALU.mult, ALU.add).then_inc(zf[s], 1)

                n = l * LT + O0
                with dve.Fori(0, KC // 2 - 1) as q:
                    nc.cur_bb.disable_value_cache()
                    for s in range(2):
                        w_lo(n + q * 2 + s + 2, s)
                        residual(q * 2 + s, s, n + q * 2 + s + 1, 16 * (l * (KC // 2) + q + 1))
                for s in range(2):
                    residual(KC - 2 + s, s, n + KC - 2 + s + 1, 16 * (l * (KC // 2) + KC // 2))
            chain.sem = c_fin
            chain.start(0)
            dve.wait_ge(s_rowg, 32)
            for t, (t0, r) in enumerate(TILES):
                stats(t, f_ti, 0, f_vr, f_sd, f_bs)
                if t == 4:
                    dve.wait_ge(o_y0, 16)
                for b in range(4):
                    dve.wait_ge(f_nrm, 4 * t + b + 1)
                    cols = slice(512 * b, 512 * (b + 1))
                    dve.tensor_tensor(FIN[0:r, t % 4, cols], XN[0:r, cols], GROW[0:r, cols], ALU.mult).then_inc(f_g, 1)

        @block.gpsimd
        def _(pool):
            def mem_load(q):
                for p in range(2):
                    if p:
                        wait_apart(pool, m_lo, 2 * q + 1)
                    pool.dma_start(XN[:, :], mem_t[:, 8 * p:8 * p + 8, :].rearrange("p k c -> p (k c)")) \
                        .then_inc(ld_mem, 16)

            mem_load(0)
            pool.dma_start(OY[:, :, :], x_t).then_inc(s_x, 16)
            for dst, src in ((ident, ident_d), (causal, causal_d), (swam, swa_mask_d), (cos, cos_d), (sin, sin_d),
                             (gT, ln_gt), (bT, ln_bt)):
                pool.dma_start(dst[:, :], src).then_inc(s_const, 16)
            pool.dma_start(snk[:, :], sinks.partition_broadcast(P)).then_inc(s_const, 16)
            pool.dma_start(bF[:, :], bff).then_inc(s_const, 16)
            for i in range(DEPTH):
                src = bass.AP(rel_pad.tensor, i * GH * RELW, [[RELW, GH], [0, P], [1, RELW]])
                pool.dma_start(rel_rows[i * GH:(i + 1) * GH], src).then_inc(s_toep, 16)
            pool.wait_ge(s_toep, 16 * DEPTH)

            with pool.Fori(0, DEPTH) as layer:
                nc.cur_bb.disable_value_cache()
                l, = own(pool, layer)
                pool.dma_start(WFR[:, :, :], wff[l]).then_inc(ld_ff, 16)
                pool.dma_start(CL[:, :], fox_logf[l]).then_inc(ld_ff, 16)
                q = 0
                mv = 0
                for kind, i, b in FILLS:
                    if kind == "out":
                        t0, r = TILES[i]
                        pool.wait_ge(xh, l * LNF + q + 1)
                        pool.tensor_tensor(XL[:, 4 * b:4 * b + 4, t0:t0 + r], STG[:, q % 2, :, 0:r],
                                           XH[:, 4 * b:4 * b + 4, t0:t0 + r].bitcast(F32), ALU.subtract) \
                            .then_inc(xl, 1)
                        q += 1
                    else:
                        wait_apart(pool, tf, l * NF + FILLS.index((kind, i, b)) + 1)
                        pool.dma_start(mv_o[l, i - GH], MVN[:, i % 2, :].rearrange("p (b d) -> p b d", b=2)) \
                            .then_inc(o_mv[i % 2], 16)
                wait_apart(pool, flr, l + 1)
                pool.dma_start(fl_o[l], LF).then_inc(o_fl, 16)
                wait_apart(pool, ncr, l + 1)
                pool.dma_start(nc_rows, NR).then_inc(o_rows, 16)
                pool.wait_ge(o_rows, 16 * (l + 1))
                for s in range(2):
                    pool.wait_ge(o_mk[s], 16 * (GH // 2) * (l + 1))
                    pool.wait_ge(o_mv[s], 16 * (GH // 2) * (l + 1))

                l, = own(pool, layer)
                for gi, (g, first) in enumerate(((FOX, A0), (BAND, B0))):
                    with pool.Fori(0, GH) as h:
                        nc.cur_bb.disable_value_cache()
                        u, vu = l * HEADS + GH * gi + h, l * V_UNITS + GH * gi + h
                        m = l * (LT // 2) + first // 2 + h * 2
                        pool.wait_ge(pv, 2 * u)
                        kc, vc = (fox_k, fox_v) if g is FOX else (band_k, band_v)
                        ko, vo = (fk_o, fv_o) if g is FOX else (bk_o, bv_o)
                        pool.dma_start(KTC[:, :], kc[l, h]).then_inc(ld_kc, 16)
                        if g is FOX:
                            pool.dma_start(BI[:, :], nc_rows[h].partition_broadcast(P)).then_inc(ld_bias, 16)
                        else:
                            pool.dma_start(BI[:, 0:SEQ], toep[l * GH + h]).then_inc(ld_bias, 16)
                        pool.dma_start(VC[:, :, :], vc[l, h]).then_inc(ld_vc, 16)
                        wait_apart(pool, ld_bias, 16 * (l * 2 * GH + GH * gi + h + 1))
                        if g is FOX:
                            pool.tensor_tensor(BD[:, 0:SEQ].rearrange("p (b c) -> p b c", b=4),
                                               BI[:, 0:SEQ].rearrange("p (b c) -> p b c", b=4),
                                               causal[:, :].unsqueeze(1).broadcast_to([P, 4, P]), ALU.add) \
                                .then_inc(bdr, 1)
                            pool.tensor_tensor(BD[0:DEC, SEQ:TOK], BI[0:DEC, SEQ + PAST:], causal[0:DEC, 0:DEC],
                                               ALU.add).then_inc(bdr, 1)
                        else:
                            pool.memset(BI[0:P // 2, SEQ - P // 2:SEQ], NEG).then_inc(bmr, 1)
                        wait_apart(pool, zf[0], m + 1)
                        pool.dma_start(ko[l, h], KT[:, :]).then_inc(o_k, 16)
                        wait_apart(pool, zf[0], m + 2)
                        pool.dma_start(vo[l, h], VT[:, :]).then_inc(o_v, 16)
                with pool.Fori(0, PAIRS) as j:
                    nc.cur_bb.disable_value_cache()
                    u, vu, dm = l * HEADS + 2 * GH + j * 4, l * V_UNITS + 2 * GH + j, l * GH + 2 * j
                    m = l * (LT // 2) + C0 // 2 + j * (PAIR_TILES // 2)
                    wait_apart(pool, pv, 2 * u)
                    pool.dma_start(KTC[:, 0:P], swa_k[l, j]).then_inc(ld_kc, 16)
                    pool.dma_start(VC[:, 0, :], swa_v[l, j]).then_inc(ld_vc, 16)
                    wait_apart(pool, zf[0], m + 1)
                    pool.dma_start(sk_o[l, j], KT[:, TOK - P - DEC:TOK]).then_inc(o_k, 16)
                    wait_apart(pool, zf[0], m + 2)
                    pool.dma_start(sv_o[l, j], VT[:, TOK - P - DEC:TOK]).then_inc(o_v, 16)
                    for k in range(2):
                        pool.wait_ge(sc[2], u + k + 2)
                        wait_apart(pool, o_k, 16 * (vu + 1))
                        pool.dma_start(KT[:, 0:NMEM], mk_o[l, j * 2 + k]).then_inc(ld_km, 16)
                        pool.dma_start(KTC[:, :], mem_k[l, j * 2 + k]).then_inc(ld_kc, 16)
                        wait_apart(pool, pv, 2 * (u + k + 2))
                        pool.dma_start(V[:, 0:2, :], mv_o[l, j * 2 + k]).then_inc(ld_vm, 16)
                        pool.dma_start(VC[:, :, :], mem_v[l, j * 2 + k]).then_inc(ld_vc, 16)
                for s in range(2):
                    wait_apart(pool, o_x[s], 16 * (LNF // 2) * (l + 1))
                for s in range(2):
                    pool.dma_start(XR[:, s, :], x_res[s]).then_inc(ld_xr[s], 16)
                pool.wait_ge(o_fl, 16 * (l + 1))
                pool.wait_ge(o_v, 16 * V_UNITS * (l + 1))
                wait_apart(pool, gd, HEADS * (l + 1))
                mem_load(l + 1)
                with pool.Fori(1, KC // 2) as q:
                    nc.cur_bb.disable_value_cache()
                    for s in range(2):
                        wait_apart(pool, zf[s], l * (LT // 2) + O0 // 2 + q)
                        pool.dma_start(XR[:, s, :], x_res[q * 2 + s]).then_inc(ld_xr[s], 16)
            pool.wait_ge(s_rowg, 32)
            for t, (t0, r) in enumerate(TILES):
                for b in range(4):
                    pool.wait_ge(f_g, 4 * t + b + 1)
                    cols = slice(512 * b, 512 * (b + 1))
                    pool.tensor_tensor(FIN[0:r, t % 4, cols], FIN[0:r, t % 4, cols], BROW[0:r, cols], ALU.add) \
                        .then_inc(f_y, 1)
                wait_apart(pool, f_y, 4 * (t + 1))
                pool.dma_start(y_o[t0:t0 + r, :], FIN[0:r, t % 4, :]).then_inc(o_y if t else o_y0, 16)
            pool.wait_ge(o_y, 16 * (NT - 1))
            pool.wait_ge(o_y0, 16)
            pool.wait_ge(o_k, 16 * V_UNITS * DEPTH)


CH = {"ln": 8 * NT, "ff": 4, "fox": 12, "band": 8, "pair": 56}

_OUTS = [((TOK, DM)), ((DEPTH, GH, P, TOK)), ((DEPTH, GH, P, TOK)), ((DEPTH, GH, TOK)),
         ((DEPTH, GH, P, TOK)), ((DEPTH, GH, P, TOK)), ((DEPTH, PAIRS, P, P + DEC)), ((DEPTH, PAIRS, P, P + DEC)),
         ((DEPTH, GH, P, NMEM)), ((DEPTH, GH, P, 2, HD))]


def kernel(**inputs):
    import numpy as np
    import concourse.bacc as bacc
    from concourse.bass_utils import run_bass_kernel_spmd as run

    f32 = np.float32
    a = {k: np.asarray(v) for k, v in inputs.items()}

    def cols(w, c, n=P):
        return w[:, c:c + n].reshape(KC, P, n).transpose(1, 0, 2)

    fq, fk, fv, ff = 0, 512, 1024, 1536
    bq = ff + GH
    bk, bv = bq + 512, bq + 1024
    sq = bq + 1536
    sk, sv = sq + 512, sq + 768
    mq = sq + 1024
    gate = mq + 512
    layers = []
    for l in range(DEPTH):
        wi, wm, wo = a["w_in"][l], a["w_mem_kv"][l], a["w_out"][l]
        t = [cols(wm, P * j) for j in range(MEM_TILES)]
        for g, (k0, q0, v0) in enumerate(((fk, fq, fv), (bk, bq, bv))):
            for h in range(GH):
                t += [cols(wi, c + P * h) for c in (k0, q0, v0)] + [cols(wi, gate + P * (GH * g + h))]
        for j in range(PAIRS):
            t += [cols(wi, sk + P * j), cols(wi, sq + 2 * P * j), cols(wi, sv + P * j), cols(wi, sq + 2 * P * j + P)]
            t += [cols(wi, mq + 2 * P * j + P * k) for k in range(2)]
            t += [cols(wi, gate + P * (2 * GH + 2 * j + k)) for k in range(2)]
            t += [cols(wi, gate + P * (3 * GH + 2 * j + k)) for k in range(2)]
        t += [cols(wo, P * j) for j in range(KC)]
        layers += t
    def keys(x):
        return x[:, 0].transpose(0, 2, 3, 1)

    def values(x):
        d, _, n, h, f = x.shape
        return x[:, 0].reshape(d, n // P, P, h, f).transpose(0, 3, 2, 1, 4)

    x_all = np.concatenate([a["x_prompt"][0], a["x_sample"][0]], 0)
    gs = np.concatenate([a["ln_in_g"][None], a["ln_g"]], 0)
    bs = np.concatenate([a["ln_in_b"][None], a["ln_b"]], 0)
    pos = np.concatenate([np.arange(SEQ), PAST + np.arange(DEC)]).astype(f32)
    half = HD // 2
    inv = (10000.0 ** (-np.arange(half) / half)).astype(f32)
    ang = inv[:, None] * pos[None, :]
    cos = np.concatenate([np.cos(ang), np.cos(ang)], 0)
    sin = np.concatenate([-np.sin(ang), np.sin(ang)], 0)
    r = np.arange(P)
    causal = np.where(r[None, :] <= r[:, None], 0.0, NEG)
    ahead = np.arange(2 * P)[None, :] // 64 - r[:, None] // 64
    swa = np.where((ahead >= 0) & (ahead <= 2), 0.0, NEG)

    arrays = {
        "wt": np.stack(layers).reshape(DEPTH * LT, P, KC, P),
        "wff": np.stack([cols(a["w_in"][l], ff, GH) for l in range(DEPTH)]),
        "bff": a["b_f"].T,
        "x_t": x_all.T.reshape(KC, P, TOK).transpose(1, 0, 2),
        "mem_t": a["mem_prompt"][0].T.reshape(KC, P, NMEM).transpose(1, 0, 2),
        "fox_k": keys(a["cache_fox_k"]), "fox_v": values(a["cache_fox_v"]),
        "fox_logf": a["cache_fox_logf"][:, 0].transpose(0, 2, 1),
        "band_k": keys(a["cache_band_k"]), "band_v": values(a["cache_band_v"]),
        "swa_k": keys(a["cache_swa_k"]), "swa_v": values(a["cache_swa_v"]).reshape(DEPTH, PAIRS, P, HD),
        "mem_k": keys(a["cache_mem_k"]), "mem_v": values(a["cache_mem_v"]),
        "rel_pad": np.pad(a["rel_bias"], ((0, 0), (0, 0), (SEQ + P - 257, 0)), mode="edge"),
        "sinks": a["sinks"].reshape(1, -1)[0],
        "ln_gt": gs.reshape(-1, KC, P).transpose(2, 0, 1).reshape(P, -1),
        "ln_bt": bs.reshape(-1, KC, P).transpose(2, 0, 1).reshape(P, -1),
        "g_row": gs[DEPTH], "b_row": bs[DEPTH],
        "ident": np.eye(P), "causal": causal, "swa_mask": swa, "cos": cos, "sin": sin,
    }
    nc = bacc.Bacc("TRN2", target_bir_lowering=False, num_devices=1)
    feed, args = {}, []
    for name, v in arrays.items():
        v = np.ascontiguousarray(v, dtype=f32)
        feed[f"in_{name}"] = v
        args.append(nc.dram_tensor(f"in_{name}", v.shape, F32, kind="ExternalInput").ap())
    for i, shape in enumerate(_OUTS):
        args.append(nc.dram_tensor(f"out_{i}", shape, F32, kind="ExternalOutput").ap())
    encoder_step(nc, *args)
    res = run(nc, [feed], core_ids=[0]).results[0]
    y, fk_, fv_, fl_, bk_, bv_, sk_, sv_, mk_, mv_ = (res[f"out_{i}"] for i in range(len(_OUTS)))

    def heads(x, lo, hi):
        return np.ascontiguousarray(x[:, :, :, lo:hi].transpose(0, 3, 1, 2)[:, None])

    def logf(lo, hi):
        return np.ascontiguousarray(fl_[:, :, lo:hi].transpose(0, 2, 1)[:, None])

    mem_v = np.ascontiguousarray(mv_.transpose(0, 3, 2, 1, 4).reshape(DEPTH, NMEM, GH, HD)[:, None])
    return (y[None, :SEQ], y[None, SEQ:],
            heads(fk_, 0, SEQ), heads(fv_, 0, SEQ), logf(0, SEQ),
            heads(bk_, 0, SEQ), heads(bv_, 0, SEQ),
            heads(sk_, 0, P), heads(sv_, 0, P),
            heads(mk_, 0, NMEM), mem_v,
            heads(fk_, SEQ, TOK), heads(fv_, SEQ, TOK), logf(SEQ, TOK),
            heads(bk_, SEQ, TOK), heads(bv_, SEQ, TOK),
            heads(sk_, P, P + DEC), heads(sv_, P, P + DEC))
```

```python
from contextlib import ExitStack

import concourse.bass as bass
from concourse import mybir

ALU = mybir.AluOpType
ACT = mybir.ActivationFunctionType
F32 = mybir.dt.float32
F32R = mybir.dt.float32r
AX_X = mybir.AxisListType.X

P = 128
DM = 2048
KC = DM // P
SEQ, DEC, PAST = 512, 32, 256
TOK = SEQ + DEC
HALF = TOK // 2
DEPTH = 2
NMEM = 256
HD = 128
GH = 4
HEADS = 4 * GH
ALPHA = (2 * DEPTH) ** 0.25
EPS = 1e-5
SCALE = HD ** -0.5
NEG = -1e30
RELW = SEQ + P
TILES = [(i * P, P) for i in range(SEQ // P)] + [(SEQ, DEC)]
NT = len(TILES)

MEM_TILES = 2 * GH
HEAD_TILES = 4
PAIR_TILES = 10
PAIRS = 2
A0 = MEM_TILES
B0 = A0 + HEAD_TILES * GH
C0 = B0 + HEAD_TILES * GH
O0 = C0 + PAIR_TILES * PAIRS
LT = O0 + KC

V_UNITS = 2 * GH + PAIRS
K_LOADS = 2 * GH + PAIRS + GH

class Group:
    def __init__(self, blocks, cached, own, place, sink=False):
        self.blocks, self.cached, self.own, self.place, self.sink = blocks, cached, own, place, sink
        self.width = [P * len(b) for b in blocks] + [P * cached + own]
        self.at = [sum(w + 1 for w in self.width[:i]) for i in range(NT)]
        self.order = [i for _, _, i in place]


CAUSAL = [list(range(i + 1)) for i in range(4)]
FOX = Group(CAUSAL, 2, DEC, [(1, 0, 2), (1, 384, 0), (2, 0, 1), (0, 0, 3), (3, 0, 4)])
BAND = Group(CAUSAL, 2, DEC, [(1, 0, 2), (1, 384, 0), (2, 0, 1), (0, 0, 3), (3, 0, 4)])
SWA = Group([[0], [0, 1], [1, 2], [2, 3]], 1, DEC, [(0, 0, 1), (0, 256, 2), (1, 0, 3), (1, 256, 0), (2, 0, 4)], sink=True)
MEM = Group([[0, 1]] * 4, 2, 0, [(0, 0, 0), (0, 256, 1), (1, 0, 2), (1, 256, 3), (2, 0, 4)])
SW = sum(w + 1 for w in FOX.width)
PTW = 10 * P + 3 * DEC

LN_PLAN = [("mem", 0), ("mem", 1), ("mem", 2), ("stat", 0), ("mem", 3), ("mem", 4), ("mem", 5), ("mv", 4),
           ("mem", 6), ("mv", 5), ("mem", 7), ("mv", 6), ("mv", 7)]
NORMED_BEFORE = {4: 4, 5: 4, 6: 4, 7: 4}
NQ = 4


def own(eng, *values):
    out = []
    for v in values:
        if isinstance(v, int):
            out.append(v)
            continue
        NAMES.append(f"held{len(NAMES)}")
        reg = eng.alloc_register(NAMES[-1])
        eng.reg_mov(reg, v)
        out.append(eng.snap(reg, min_val=0, max_val=v.max_val))
    return out


NAMES = []


class Chain:

    def __init__(self, eng, sem):
        self.eng, self.sem, self.base, self.k = eng, sem, 0, 0

    def start(self, base):
        self.base, self.k = own(self.eng, base)[0], 0

    def step(self, ins):
        ins.then_inc(self.sem, 1)
        self.k += 1

    def wait(self):
        self.eng.wait_ge(self.sem, self.base + self.k)

    def link(self, ins):
        self.step(ins)
        self.wait()


def encoder_step(nc, wt, wff, bff, x_t, mem_t, fox_k, fox_v, fox_logf, band_k, band_v, swa_k, swa_v, mem_k, mem_v,
                 rel_pad, sinks, ln_gt, ln_bt, ident_d, causal_d, swa_mask_d, cos_d, sin_d,
                 y_o, fk_o, fv_o, fl_o, bk_o, bv_o, sk_o, sv_o, mk_o, mv_o):
    with ExitStack() as ctx:
        top = [nc.sbuf_base]
        top[0] += -top[0] % 64

        def sb_at(name, shape, off, dt=F32):
            return nc.alloc_sbuf_tensor_at(name, shape, dt, offset=off)

        def sb(name, shape, dt=F32):
            size = 4
            for s in shape[1:]:
                size *= s
            off = top[0]
            top[0] += size + -size % 64
            return sb_at(name, shape, off, dt)

        def sem(name):
            return ctx.enter_context(nc.semaphore(name))

        GB = ctx.enter_context(nc.psum_tensor("GB", [P, 4, 512], F32))
        AB = ctx.enter_context(nc.psum_tensor("AB", [P, 4, 512], F32))

        XH = sb("XH", [P, KC, TOK], F32R)
        XL = sb("XL", [P, KC, TOK], F32R)
        OY = sb("OY", [P, KC, TOK])
        WR = sb("WR", [P, 2, KC, P])
        WH = sb("WH", [P, 2, KC, P], F32R)
        WL = sb("WL", [P, 2, KC, P], F32R)
        LNB = sb("LNB", [P, 5, TOK])
        ones = sb("ones", [P, P])
        arena = top[0]
        MTH = sb("MTH", [P, KC, NMEM], F32R)
        MTR = sb_at("MTR", [P, KC, NMEM], top[0])
        MTL = sb("MTL", [P, KC, NMEM], F32R)
        arena_end, top[0] = top[0], arena
        KT = sb("KT", [P, TOK])
        QT = sb("QT", [P, TOK])
        VT = sb("VT", [P, TOK])
        ES = sb("ES", [P, TOK])
        GA = sb("GA", [P, TOK])
        V = sb("V", [P, NT, HD])
        S = sb("S", [P, SW])
        PT = sb("PT", [P, PTW])
        KTC = sb("KTC", [P, PAST])
        VC = sb("VC", [P, 2, HD])
        BI = sb("BI", [P, SEQ + PAST + DEC])
        BD = sb("BD", [P, TOK])
        assert top[0] <= arena_end, (top[0], arena_end)
        top[0] = arena_end
        MT = sb_at("MT", [P, 2, NMEM], top[0])
        MVN = sb_at("MVN", [P, 2, NMEM], top[0] + 8 * NMEM)
        XR = sb("XR", [P, 2, TOK])
        ident = sb("ident", [P, P])
        causal = sb("causal", [P, P])
        swam = sb("swam", [P, 2 * P])
        cos = sb("cos", [P, TOK])
        sin = sb("sin", [P, TOK])
        snk = sb("snk", [P, DEPTH * GH])
        gT = sb("gT", [P, (DEPTH + 1) * KC])
        bT = sb("bT", [P, (DEPTH + 1) * KC])
        bF = sb("bF", [GH, DEPTH])
        WFR = sb("WFR", [P, KC, GH])
        WFF = sb("WFF", [P, KC, 2 * GH], F32R)
        CL = sb("CL", [GH, PAST])
        nmx = sb("nmx", [P, 8])
        esum = sb("esum", [P, 8])
        rsum = sb("rsum", [P, 8])
        one = sb("one", [P, 1])
        assert top[0] <= nc.sbuf_usable_end, (top[0], nc.sbuf_usable_end)
        SUM1, SUM2, SHIFT, SQ = LNB[:, 0, :], LNB[:, 1, :], LNB[:, 2, :], [LNB[:, 3, :], LNB[:, 4, :]]
        RSTD, NMR, VE, SCR = LNB[:, 0, :], LNB[:, 1, :], LNB[:, 3, :], LNB[:, 4, :]
        NR = LNB[0:GH, 0:2, :].rearrange("p s c -> p (s c)")[:, 0:SEQ + PAST + DEC]
        LF, T1 = LNB[0:GH, 3, :], LNB[0:GH, 4, :]

        x_res = nc.dram_tensor("x_res", (KC, P, TOK), F32, kind="Internal").ap()
        nc_rows = nc.dram_tensor("nc_rows", (GH, SEQ + PAST + DEC), F32, kind="Internal").ap()
        rel_rows = nc.dram_tensor("rel_rows", (DEPTH * GH, P, RELW), F32, kind="Internal").ap()
        toep = bass.AP(rel_rows.tensor, P - 1, [[P * RELW, DEPTH * GH], [RELW - 1, P], [1, SEQ]])

        s_const = sem("s_const")
        s_toep = sem("s_toep")
        s_x0 = sem("s_x0")
        s_x = [sem(f"s_x{p + 1}") for p in range(NQ)]
        raw = [sem("raw0"), sem("raw1")]
        ld_mem = [sem(f"ld_mem{p}") for p in range(NQ)]
        ld_kc = sem("ld_kc")
        ld_vc = sem("ld_vc")
        ld_km = sem("ld_km")
        ld_vm = sem("ld_vm")
        ld_bias = sem("ld_bias")
        ld_ff = sem("ld_ff")
        ld_xr = [sem("ld_xr0"), sem("ld_xr1")]
        ld_rows = sem("ld_rows")
        o_k = sem("o_k")
        o_v = sem("o_v")
        o_mk = [sem("o_mk0"), sem("o_mk1")]
        o_mv = [sem("o_mv0"), sem("o_mv1")]
        o_x = sem("o_x")
        o_fl = sem("o_fl")
        o_rows = sem("o_rows")
        o_y = sem("o_y")
        hi = sem("hi")
        lo = sem("lo")
        zd = sem("zd")
        zf = [sem("zf0"), sem("zf1")]
        m_hi = sem("m_hi")
        m_lo = sem("m_lo")
        mu0 = sem("mu0")
        sh = sem("sh")
        zero = sem("zero")
        cen = sem("cen")
        sqr = sem("sqr")
        sm1 = sem("sm1")
        sm2 = sem("sm2")
        st = sem("st")
        m2 = sem("m2")
        vr = sem("vr")
        sd = sem("sd")
        bs = sem("bs")
        n1 = sem("n1")
        n2 = sem("n2")
        nx = sem("nx")
        to = sem("to")
        tf = sem("tf")
        xh = sem("xh")
        xl = sem("xl")
        ffh = sem("ffh")
        ffl = sem("ffl")
        ffd = sem("ffd")
        ffe = sem("ffe")
        ffa = sem("ffa")
        flr = sem("flr")
        ncr = sem("ncr")
        bdr = sem("bdr")
        bmr = sem("bmr")
        sc = [sem(f"sc{b}") for b in range(4)]
        mk = sem("mk")
        ex = sem("ex")
        pr = sem("pr")
        pt = sem("pt")
        pte = sem("pte")
        vt = sem("vt")
        ve = sem("ve")
        vse = sem("vse")
        pv = sem("pv")
        oe = sem("oe")
        eg = sem("eg")
        gd = sem("gd")
        oh = [sem("oh0"), sem("oh1")]
        ol = [sem("ol0"), sem("ol1")]
        c_dl = sem("c_dl")
        c_df = sem("c_df")
        c_da = sem("c_da")
        c_db = sem("c_db")
        c_dc = sem("c_dc")
        c_al = sem("c_al")
        s_one = sem("s_one")

        block = ctx.enter_context(nc.Block())
        N_CONST = 9

        def z2(slot):
            return GB[:, 2 * slot:2 * slot + 2, 0:HALF]

        def split2(t):
            return t.rearrange("p (h c) -> p h c", h=2)

        def oy2(c):
            return split2(OY[:, c, :])

        def pt_col(j):
            return PT[:, P * j:P * (j + 1)]

        def wait_apart(eng, sem, count):
            held, = own(eng, count)
            eng.wait_ge(s_one, 1)
            eng.wait_ge(sem, held)

        @block.sync
        def _(sp):
            for n in range(2):
                sp.dma_start(WR[:, n, :, :], wt[n]).then_inc(raw[n], 16)
            with sp.Fori(1, DEPTH * LT // 2) as m:
                nc.cur_bb.disable_value_cache()
                for s in range(2):
                    sp.wait_ge(lo, m * 2 + s - 1)
                    sp.dma_start(WR[:, s, :, :], wt[m * 2 + s]).then_inc(raw[s], 16)
            sp.wait_ge(lo, DEPTH * LT)
            sp.sem_inc(raw[0], 16)

        @block.tensor
        def _(pe):
            def gemm_half(n, s, hf, free, split):
                if hf == 0:
                    pe.wait_ge(lo, n + 1)
                    pe.wait_ge(zf[s], free)
                for k in range(KC):
                    if split is not None:
                        pe.wait_ge(ol[hf], split + k + 1)
                    for i, (w, x) in enumerate(((WH, XH), (WL, XH), (WH, XL))):
                        mm = pe.matmul(GB[:, 2 * s + hf, 0:HALF], w[:, s, k, :],
                                       x[:, k, hf * HALF:(hf + 1) * HALF],
                                       start=(k == 0 and i == 0), stop=(k == KC - 1 and i == 2))
                if hf == 1:
                    mm.then_inc(zd, 1)

            def gemm(n, m, j, hf=None, split=None):
                for h in (range(2) if hf is None else [hf]):
                    gemm_half(n + j, j % 2, h, m + j // 2, split)

            def scores(g, u, dm=None, fl=None):
                if g is FOX:
                    pe.wait_ge(flr, fl)
                if g is MEM:
                    pe.wait_ge(ld_km, 16 * (dm + 1))
                for j, (b, col, i) in enumerate(g.place):
                    t0, r = TILES[i]
                    if b >= 2:
                        pe.wait_ge(oe, 2 * u + 2)
                    if i < 4:
                        ks = g.blocks[i][0] * P
                        mm = pe.matmul(AB[:, b, col:col + g.width[i]], QT[:, t0:t0 + r], KT[:, ks:ks + g.width[i]],
                                       start=True, stop=True)
                    else:
                        w = P * g.cached
                        mm = pe.matmul(AB[0:DEC, b, col:col + w], QT[:, t0:t0 + r], KTC[:, 0:w],
                                       start=True, stop=True)
                        if g.own:
                            mm = pe.matmul(AB[0:DEC, b, col + w:col + w + DEC], QT[:, t0:t0 + r], KT[:, SEQ:TOK],
                                           start=True, stop=True)
                    if j == len(g.place) - 1 or g.place[j + 1][0] != b:
                        mm.then_inc(sc[b], 1)

            def turn_probs(g, u):
                pe.wait_ge(pr, 5 * u + 5)
                j = 0
                blocks = [(i, b) for i in range(4) for b in range(len(g.blocks[i]))]
                for j, (i, b) in enumerate(blocks):
                    at = g.at[i] + P * b
                    mm = pe.transpose(AB[:, j // 4, P * (j % 4):P * (j % 4 + 1)], S[:, at:at + P], ident[:, :])
                    if j in (3, 7) or (j == len(blocks) - 1 and j < 7):
                        mm.then_inc(pt, 1)
                for b in range(g.cached):
                    mm = pe.transpose(AB[:, 2, 256 + DEC * b:256 + DEC * (b + 1)],
                                      S[0:DEC, g.at[4] + P * b:g.at[4] + P * (b + 1)], ident[0:DEC, 0:DEC])
                if g.own:
                    at = g.at[4] + P * g.cached
                    mm = pe.transpose(AB[0:DEC, 2, 320:320 + DEC], S[0:DEC, at:at + DEC], ident[0:DEC, 0:DEC])
                return mm

            def turn_v(m):
                pe.wait_ge(zf[0], m)
                mm = pe.transpose(AB[0:DEC, 2, 352:352 + P], VT[:, SEQ:TOK], ident[:, :])
                mm.then_inc(pt, 1)
                for i in range(4):
                    mm = pe.transpose(AB[:, 3, P * i:P * (i + 1)], VT[:, P * i:P * (i + 1)], ident[:, :])
                mm.then_inc(vt, 1)

            def mix(g, u, kl, vu=None, dm=None):
                pe.wait_ge(pte, 3 * u + 3)
                pe.wait_ge(ld_vc, 16 * (kl + 1))
                if vu is not None:
                    pe.wait_ge(ve, vu + 1)
                    pe.wait_ge(vse, vu + 1)
                if dm is not None:
                    pe.wait_ge(ld_vm, 16 * (dm + 1))
                j = 0
                for i in range(4):
                    for b, kb in enumerate(g.blocks[i]):
                        mm = pe.matmul(AB[:, 3, P * i:P * (i + 1)], V[:, kb, :], pt_col(j),
                                       start=(b == 0), stop=(b == len(g.blocks[i]) - 1))
                        j += 1
                mm.then_inc(pv, 1)
                for b in range(g.cached):
                    mm = pe.matmul(AB[:, 2, 0:DEC], VC[:, b, :], PT[:, 10 * P + DEC * b:10 * P + DEC * (b + 1)],
                                   start=(b == 0), stop=(b == g.cached - 1 and not g.own))
                if g.own:
                    mm = pe.matmul(AB[:, 2, 0:DEC], V[0:DEC, 4, :], PT[0:DEC, 10 * P + 2 * DEC:10 * P + 3 * DEC],
                                   start=False, stop=True)
                mm.then_inc(pv, 1)

            def head(g, n, m, u, kl, vu, fl):
                n, m, u, kl, vu, fl = own(pe, n, m, u, kl, vu, fl)
                gemm(n, m, 0)
                gemm(n, m, 1)
                gemm(n, m, 2, 0)
                pe.wait_ge(zf[0], m + 1)
                pe.wait_ge(zf[1], m + 1)
                pe.wait_ge(ld_kc, 16 * (kl + 1))
                scores(g, u, fl=fl)
                gemm(n, m, 2, 1)
                gemm(n, m, 3, 0)
                turn_probs(g, u)
                turn_v(m + 2)
                gemm(n, m, 3, 1)
                mix(g, u, kl, vu)

            def pair(n, m, u, kl, vu, dm):
                n, m, u, kl, vu, dm = own(pe, n, m, u, kl, vu, dm)
                gemm(n, m, 0)
                gemm(n, m, 1)
                gemm(n, m, 2, 0)
                pe.wait_ge(zf[0], m + 1)
                pe.wait_ge(zf[1], m + 1)
                pe.wait_ge(ld_kc, 16 * (kl + 1))
                scores(SWA, u)
                gemm(n, m, 2, 1)
                gemm(n, m, 3, 0)
                turn_probs(SWA, u)
                turn_v(m + 2)
                gemm(n, m, 3, 1)
                mix(SWA, u, kl, vu)
                gemm(n, m, 4, 0)
                pe.wait_ge(zf[1], m + 2)
                scores(SWA, u + 1)
                gemm(n, m, 4, 1)
                gemm(n, m, 5, 0)
                turn_probs(SWA, u + 1).then_inc(pt, 1)
                gemm(n, m, 5, 1)
                mix(SWA, u + 1, kl, vu)
                pe.wait_ge(zf[0], m + 3)
                pe.wait_ge(ld_kc, 16 * (kl + 2))
                scores(MEM, u + 2, dm)
                gemm(n, m, 6)
                turn_probs(MEM, u + 2).then_inc(pt, 1)
                gemm(n, m, 7, 0)
                mix(MEM, u + 2, kl + 1, dm=dm)
                pe.wait_ge(zf[1], m + 3)
                pe.wait_ge(ld_kc, 16 * (kl + 3))
                scores(MEM, u + 3, dm + 1)
                gemm(n, m, 7, 1)
                gemm(n, m, 8, 0)
                turn_probs(MEM, u + 3).then_inc(pt, 1)
                gemm(n, m, 8, 1)
                mix(MEM, u + 3, kl + 2, dm=dm + 1)
                gemm(n, m, 9)

            def mean_of_first():
                for h in range(2):
                    mm = pe.matmul(AB[:, h, 0:HALF], ones[:, :], OY[:, 0, h * HALF:(h + 1) * HALF],
                                   start=True, stop=True)
                mm.then_inc(mu0, 1)

            def statistics(r):
                pe.wait_ge(sm1, KC * (r + 1) + 1)
                pe.wait_ge(sm2, KC * (r + 1) + 2)
                for i, total in enumerate((SUM1, SUM2)):
                    for h in range(2):
                        mm = pe.matmul(AB[:, 2 * i + h, 0:HALF], ones[:, :], total[:, h * HALF:(h + 1) * HALF],
                                       start=True, stop=True)
                mm.then_inc(st, 1)

            def mem_tile(l, j):
                s, n = j % 2, l * LT + j
                pe.wait_ge(lo, n + 1)
                pe.wait_ge(zf[s], l * (LT // 2) + j // 2 + 1)
                for k in range(KC):
                    if j == 0 and k % (KC // NQ) == 0:
                        pe.wait_ge(m_lo, NQ * l + k // (KC // NQ) + 1)
                    for i, (w, x) in enumerate(((WH, MTH), (WL, MTH), (WH, MTL))):
                        mm = pe.matmul(GB[:, 2 * s, 0:NMEM], w[:, s, k, :], x[:, k, :],
                                       start=(k == 0 and i == 0), stop=(k == KC - 1 and i == 2))
                mm.then_inc(zd, 1)

            pe.wait_ge(s_one, 1)
            pe.wait_ge(s_x0, 16)
            mean_of_first()
            with pe.Fori(0, DEPTH) as layer:
                nc.cur_bb.disable_value_cache()
                l, = own(pe, layer)
                for kind, i in LN_PLAN:
                    if kind == "mem":
                        mem_tile(l, i)
                    elif kind == "stat":
                        statistics(l)
                    else:
                        f = i - GH
                        pe.wait_ge(tf, l * GH + max(f, 1))
                        pe.wait_ge(zf[i % 2], l * (LT // 2) + i // 2 + 2)
                        if f == 0:
                            pe.wait_ge(s_const, 16 * N_CONST)
                        for c in range(2):
                            mm = pe.transpose(GB[:, 1 + 2 * (f % 2), P * c:P * (c + 1)],
                                              MT[:, i % 2, P * c:P * (c + 1)], ident[:, :])
                        mm.then_inc(to, 1)
                pe.wait_ge(xl, KC * (l + 1))
                pe.wait_ge(ffl, l + 1)
                for h in range(2):
                    for k in range(KC):
                        for i, (w, x) in enumerate(((0, XH), (GH, XH), (0, XL))):
                            mm = pe.matmul(AB[0:GH, h, 0:HALF], WFF[:, k, w:w + GH], x[:, k, h * HALF:(h + 1) * HALF],
                                           start=(k == 0 and i == 0), stop=(k == KC - 1 and i == 2))
                mm.then_inc(ffd, 1)
                pe.wait_ge(tf, (l + 1) * GH + 1)
                l, = own(pe, layer)
                for gi, (g, first) in enumerate(((FOX, A0), (BAND, B0))):
                    with pe.Fori(0, GH) as h:
                        nc.cur_bb.disable_value_cache()
                        head(g, l * LT + first + h * HEAD_TILES, l * (LT // 2) + first // 2 + h * 2 + 1,
                             l * HEADS + GH * gi + h, l * K_LOADS + GH * gi + h, l * V_UNITS + GH * gi + h, l + 1)
                with pe.Fori(0, PAIRS) as j:
                    nc.cur_bb.disable_value_cache()
                    pair(l * LT + C0 + j * PAIR_TILES, l * (LT // 2) + C0 // 2 + j * (PAIR_TILES // 2) + 1,
                         l * HEADS + 2 * GH + j * 4, l * K_LOADS + 2 * GH + j * 3, l * V_UNITS + 2 * GH + j,
                         l * GH + 2 * j)
                n, m = l * LT + O0, l * (LT // 2) + O0 // 2 + 1
                gemm(n, m, 0, split=l * KC)
                gemm(n, m, 1, 0)
                pe.wait_ge(zf[0], m + 1)
                mean_of_first()
                gemm(n, m, 1, 1)
                with pe.Fori(1, KC // 2) as q:
                    nc.cur_bb.disable_value_cache()
                    gemm(n + q * 2, m + q, 0)
                    gemm(n + q * 2, m + q, 1)
            statistics(DEPTH)

        @block.scalar
        def _(act):
            chain = Chain(act, c_al)

            def w_hi(n, s, m):
                act.wait_ge(raw[s], 16 * m)
                act.copy(WH[:, s, :, :], WR[:, s, :, :]).then_inc(hi, 1)

            def tile_done(n, m, j, ahead=True):
                act.wait_ge(zd, n + j + 2)
                if ahead:
                    w_hi(n + j + 2, j % 2, m + j // 2 + 1)

            def exps(g, u, kl=None):
                for j, i in enumerate(g.order):
                    act.wait_ge(mk, 5 * u + j + 1)
                    r, w = TILES[i][1], g.width[i] + g.sink
                    s = S[0:r, g.at[i]:g.at[i] + w]
                    act.activation(s, s, ACT.Exp, bias=nmx[0:r, i:i + 1],
                                   accum_out=esum[0:r, i:i + 1]).then_inc(ex, 1)

            def take_v(vu):
                act.wait_ge(vt, vu + 1)
                act.copy(V[:, 0:4, :], AB[:, 3, :].rearrange("p (b d) -> p b d", b=4)).then_inc(ve, 1)

            def take_o(u, c):
                act.wait_ge(pv, 2 * u + 3)
                act.copy(OY[:, c, 0:SEQ], AB[:, 3, :]).then_inc(oe, 1)
                act.wait_ge(pv, 2 * u + 4)
                act.copy(OY[:, c, SEQ:TOK], AB[:, 2, 0:DEC]).then_inc(oe, 1)

            def gate_exp(s, u):
                act.wait_ge(gd, u + 1)
                act.activation(split2(ES[:, :]), z2(s), ACT.Exp, scale=-1.0).then_inc(eg, 1)

            def take_v_tile(vu):
                act.wait_ge(o_v, 16 * (vu + 1))
                act.copy(split2(VT[:, :]), z2(0)).then_inc(zf[0], 1)

            def head(g, n, m, u, vu, c):
                n, m, u, vu = own(act, n, m, u, vu)
                tile_done(n, m, 0)
                act.wait_ge(o_k, 16 * (vu + 1))
                act.copy(split2(KT[:, :]), z2(0)).then_inc(zf[0], 1)
                tile_done(n, m, 1)
                act.mul(split2(QT[:, :]), z2(1), SCALE).then_inc(zf[1], 1)
                exps(g, u)
                tile_done(n, m, 2)
                take_v_tile(vu)
                take_v(vu)
                tile_done(n, m, 3)
                gate_exp(1, u)
                take_o(u, c)

            def pair(n, m, u, vu, j):
                n, m, u, vu = own(act, n, m, u, vu)
                tile_done(n, m, 0)
                tile_done(n, m, 1)
                exps(SWA, u)
                tile_done(n, m, 2)
                take_v_tile(vu)
                take_v(vu)
                tile_done(n, m, 3)
                take_o(u, 2 * GH + j * 2)
                exps(SWA, u + 1)
                tile_done(n, m, 4)
                act.mul(split2(QT[:, :]), z2(0), SCALE).then_inc(zf[0], 1)
                tile_done(n, m, 5)
                take_o(u + 1, 2 * GH + 1 + j * 2)
                act.wait_ge(sc[2], u + 3)
                act.mul(split2(QT[:, :]), z2(1), SCALE).then_inc(zf[1], 1)
                exps(MEM, u + 2)
                tile_done(n, m, 6)
                gate_exp(0, u)
                take_o(u + 2, 3 * GH + j * 2)
                exps(MEM, u + 3)
                tile_done(n, m, 7)
                gate_exp(1, u + 1)
                tile_done(n, m, 8)
                gate_exp(0, u + 2)
                take_o(u + 3, 3 * GH + 1 + j * 2)
                tile_done(n, m, 9)
                gate_exp(1, u + 3)

            def mem_load():
                for p in range(NQ):
                    cs = slice(p * KC // NQ, (p + 1) * KC // NQ)
                    act.dma_start(MTR[:, cs, :], mem_t[:, cs, :]).then_inc(ld_mem[p], 16)

            def mem_hi(r):
                for p in range(NQ):
                    cs = slice(p * KC // NQ, (p + 1) * KC // NQ)
                    act.wait_ge(ld_mem[p], 16 * (r + 1))
                    act.copy(MTH[:, cs, :], MTR[:, cs, :]).then_inc(m_hi, 1)

            def take_shift(r):
                act.wait_ge(mu0, r + 1)
                act.mul(split2(SHIFT), AB[:, 0:2, 0:HALF], KC).then_inc(sh, 1)

            def square(r, c, s):
                act.wait_ge(cen, r * KC + c + 1)
                act.wait_ge(sm2, r * KC + c + 1)
                act.activation(SQ[s], OY[:, c, :], ACT.Square).then_inc(sqr, 1)

            def seed(r):
                act.wait_ge(st, r + 1)
                act.activation(split2(SCR), AB[:, 0:2, 0:HALF], ACT.Square).then_inc(m2, 1)
                act.wait_ge(vr, r + 1)
                chain.link(act.activation(SCR, VE, ACT.Ln))
                act.activation(RSTD, SCR, ACT.Exp, scale=-0.5).then_inc(sd, 1)

            def affine(r, c):
                act.wait_ge(n2, r * KC + c + 1)
                at = r * KC + c
                act.activation(OY[:, c, :], OY[:, c, :], ACT.Identity, bias=bT[:, bass.ds(at, 1)],
                               scale=gT[:, bass.ds(at, 1)]).then_inc(nx, 1)

            def x_hi(l, c):
                affine(l, c)
                act.wait_ge(nx, l * KC + c + 1)
                act.copy(XH[:, c, :], OY[:, c, :]).then_inc(xh, 1)
                if (c + 1) % (KC // NQ) == 0:
                    cs = slice(c + 1 - KC // NQ, c + 1)
                    act.dma_start(x_res[cs].rearrange("c p t -> p c t"), OY[:, cs, :]).then_inc(o_x, 16)

            def mem_done(l, j):
                n, s = l * LT + j, j % 2
                act.wait_ge(zd, n + 2)
                w_hi(n + 2, s, l * (LT // 2) + j // 2 + 2)
                if j >= 2:
                    if j - 2 < GH:
                        act.wait_ge(o_mk[s], 16 * (l * (GH // 2) + (j - 2) // 2 + 1))
                    else:
                        act.wait_ge(to, l * GH + j - 2 - GH + 1)
                act.copy(MT[:, s, :], GB[:, 2 * s, 0:NMEM]).then_inc(zf[s], 1)
                if j < GH:
                    act.wait_ge(zf[s], l * (LT // 2) + j // 2 + 2)
                    act.dma_start(mk_o[l, j], MT[:, s, :]).then_inc(o_mk[s], 16)

            w_hi(0, 0, 1)
            mem_load()
            mem_hi(0)
            take_shift(0)
            for p in range(NQ):
                with act.Fori(p * KC // NQ // 2, (p + 1) * KC // NQ // 2) as q:
                    nc.cur_bb.disable_value_cache()
                    for s in range(2):
                        square(0, q * 2 + s, s)
            with act.Fori(0, DEPTH) as layer:
                nc.cur_bb.disable_value_cache()
                l, = own(act, layer)
                chain.start(l * 2)
                act.wait_ge(zd, l * LT + 1)
                w_hi(l * LT + 1, 1, l * (LT // 2) + 1)
                act.wait_ge(ld_ff, 32 * (l + 1))
                act.copy(WFF[:, :, 0:GH], WFR[:, :, :]).then_inc(ffh, 1)
                c = 0
                for kind, i in LN_PLAN:
                    if kind == "stat":
                        seed(l)
                    elif kind == "mem":
                        for _ in range(NORMED_BEFORE.get(i, 0)):
                            x_hi(l, c)
                            c += 1
                        mem_done(l, i)
                act.wait_ge(ffa, l + 1)
                chain.link(act.activation(T1, T1, ACT.Exp, scale=-1.0))
                act.activation(T1, T1, ACT.Ln, bias=1.0).then_inc(ffe, 1)
                assert chain.k == 2, chain.k
                l, = own(act, layer)
                act.wait_ge(o_x, 16 * NQ * (l + 1))
                for gi, (g, first) in enumerate(((FOX, A0), (BAND, B0))):
                    with act.Fori(0, GH) as h:
                        nc.cur_bb.disable_value_cache()
                        head(g, l * LT + first + h * HEAD_TILES, l * (LT // 2) + first // 2 + h * 2 + 1,
                             l * HEADS + GH * gi + h, l * V_UNITS + GH * gi + h, h + GH * gi)
                with act.Fori(0, PAIRS) as j:
                    nc.cur_bb.disable_value_cache()
                    pair(l * LT + C0 + j * PAIR_TILES, l * (LT // 2) + C0 // 2 + j * (PAIR_TILES // 2) + 1,
                         l * HEADS + 2 * GH + j * 4, l * V_UNITS + 2 * GH + j, j)
                act.wait_ge(gd, HEADS * (l + 1))
                for h in range(2):
                    cols = slice(h * HALF, (h + 1) * HALF)
                    for c in range(KC):
                        if h == 0 and c == KC - 1:
                            act.wait_ge(gd, HEADS * (l + 1) + 1)
                        act.copy(XH[:, c, cols], OY[:, c, cols]).then_inc(oh[h], 1)
                act.wait_ge(o_k, 16 * (V_UNITS * (l + 1) + 1))
                act.wait_ge(o_v, 16 * (V_UNITS * (l + 1) + 1))
                mem_load()
                n, m = l * LT + O0, l * (LT // 2) + O0 // 2 + 1
                r, = own(act, layer + 1)
                tile_done(n, m, 0)
                take_shift(r)
                tile_done(n, m, 1)
                act.wait_ge(o_fl, 16 * r)
                square(r, 0, 0)
                square(r, 1, 1)
                mem_hi(r)
                with act.Fori(1, KC // 2 - 1) as q:
                    nc.cur_bb.disable_value_cache()
                    for s in range(2):
                        tile_done(n + q * 2, m + q, s)
                        square(r, q * 2 + s, s)
                tile_done(n + KC - 2, m + KC // 2 - 1, 0)
                square(r, KC - 2, 0)
                square(r, KC - 1, 1)
            chain.start(DEPTH * 2)
            seed(DEPTH)
            for c in range(KC):
                affine(DEPTH, c)
                if c % 2:
                    act.wait_ge(nx, DEPTH * KC + c + 1)
                    act.dma_start(y_o[c - 1:c + 1].rearrange("c p t -> p c t"), OY[:, c - 1:c + 1, :]).then_inc(o_y, 16)
            act.wait_ge(o_y, 16 * (KC // 2))
            for s in range(2):
                act.wait_ge(o_mk[s], 16 * (GH // 2) * DEPTH)

        @block.vector
        def _(dve):
            chain = Chain(dve, c_dl)

            def w_lo(n, s):
                dve.wait_ge(hi, n + 1)
                dve.tensor_tensor(WL[:, s, :, :], WR[:, s, :, :], WH[:, s, :, :].bitcast(F32),
                                  ALU.subtract).then_inc(lo, 1)

            def soft_in(g, u, l=None, j=None, k=0):
                if g is FOX:
                    dve.wait_ge(bdr, 2 * (l * GH + j + 1))
                if g is BAND:
                    dve.wait_ge(bmr, l * GH + j + 1)
                for b, col, i in g.place:
                    t0, r = TILES[i]
                    w, at = g.width[i], g.at[i]
                    dve.wait_ge(sc[b], (l * 2 * GH + (GH if g is BAND else 0) + j if b == 3 else u) + 1)
                    src, dst = AB[0:r, b, col:col + w], S[0:r, at:at + w]

                    def add(c0, c1, bias, ):
                        chain.step(dve.tensor_tensor(dst[:, c0:c1], src[:, c0:c1], bias, ALU.add))
                    if g is FOX:
                        if i == 4:
                            add(0, PAST, BI[0:r, SEQ:SEQ + PAST])
                            add(PAST, w, BD[0:r, SEQ:TOK])
                        else:
                            if i:
                                add(0, P * i, BI[:, 0:P * i])
                            add(P * i, w, BD[:, P * i:P * (i + 1)])
                    elif g is BAND:
                        if i == 4:
                            add(0, w, BI[0:r, P:P + w])
                        else:
                            add(0, w, BI[:, SEQ - w:SEQ])
                    elif g is SWA and i < 4:
                        add(0, w, swam[:, 2 * P - w:2 * P])
                    else:
                        chain.step(dve.tensor_copy(dst, src))
                    if g.sink:
                        at_s = l * GH + j * 2 + k
                        chain.step(dve.tensor_copy(S[0:r, at + w:at + w + 1], snk[0:r, bass.ds(at_s, 1)]))
                    chain.wait()
                    dve.tensor_reduce(nmx[0:r, i:i + 1], S[0:r, at:at + w + g.sink], AX_X, ALU.max,
                                      negate=True).then_inc(mk, 1)

            def soft_out(g, u):
                dve.wait_ge(ex, 5 * u + 5)
                chain.link(dve.reciprocal(rsum[:, 0:NT], esum[:, 0:NT]))
                for i in g.order:
                    r, w = TILES[i][1], g.width[i]
                    s = S[0:r, g.at[i]:g.at[i] + w]
                    dve.tensor_scalar(s, s, rsum[0:r, i:i + 1], None, ALU.mult).then_inc(pr, 1)

            def take_probs(g, u, vu=None):
                n = sum(len(b) for b in g.blocks)
                for b in range(2):
                    dve.wait_ge(pt, 3 * u + b + 1)
                    w = P * min(4, n - 4 * b)
                    dve.tensor_copy(PT[:, 512 * b:512 * b + w], AB[:, b, 0:w]).then_inc(pte, 1)
                dve.wait_ge(pt, 3 * u + 3)
                if n > 8:
                    dve.tensor_copy(PT[:, 8 * P:n * P], AB[:, 2, 0:(n - 8) * P])
                ins = dve.tensor_copy(PT[:, 10 * P:10 * P + DEC * g.cached], AB[:, 2, 256:256 + DEC * g.cached])
                if g.own:
                    ins = dve.tensor_copy(PT[0:DEC, 10 * P + 2 * DEC:PTW], AB[0:DEC, 2, 320:320 + DEC])
                ins.then_inc(pte, 1)
                if vu is not None:
                    dve.tensor_copy(V[0:DEC, 4, :], AB[0:DEC, 2, 352:352 + P]).then_inc(vse, 1)

            def gate(s, u, c, zf_n):
                dve.wait_ge(eg, u + 1)
                chain.link(dve.tensor_scalar(ES[:, :], ES[:, :], 1.0, None, ALU.add))
                chain.link(dve.reciprocal(ES[:, :], ES[:, :]))
                dve.tensor_tensor(split2(GA[:, :]), z2(s), split2(ES[:, :]), ALU.mult).then_inc(zf[s], 1)
                dve.wait_ge(zf[s], zf_n)
                dve.wait_ge(oe, 2 * u + 4)
                dve.tensor_tensor(OY[:, c, :], OY[:, c, :], GA[:, :], ALU.mult).then_inc(gd, 1)

            def rope(s, dst, sw, scale, k_before=None):
                h = HD // 2
                chain.step(dve.tensor_copy(split2(sw[0:h, :]), z2(s)[h:HD]))
                chain.step(dve.tensor_copy(split2(sw[h:HD, :]), z2(s)[0:h]))
                chain.wait()
                chain.step(dve.tensor_tensor(sw[:, :], sw[:, :], sin[:, :], ALU.mult))
                if k_before is not None:
                    dve.wait_ge(o_k, 16 * (k_before + 1))
                chain.link(dve.tensor_tensor(split2(dst[:, :]), z2(s), split2(cos[:, :]), ALU.mult))
                if scale is None:
                    dve.tensor_tensor(dst[:, :], dst[:, :], sw[:, :], ALU.add).then_inc(zf[s], 1)
                else:
                    chain.link(dve.tensor_tensor(dst[:, :], dst[:, :], sw[:, :], ALU.add))
                    dve.tensor_scalar(dst[:, :], dst[:, :], scale, None, ALU.mult).then_inc(zf[s], 1)

            def head(g, n, m, u, vu, l, h, c):
                n, m, u, vu, l = own(dve, n, m, u, vu, l)
                w_lo(n + 2, 0)
                w_lo(n + 3, 1)
                soft_in(g, u, l, h)
                soft_out(g, u)
                w_lo(n + 4, 0)
                take_probs(g, u, vu)
                w_lo(n + 5, 1)
                gate(1, u, c, m + 2)

            def pair(n, m, u, vu, l, j):
                n, m, u, vu, l = own(dve, n, m, u, vu, l)
                dve.wait_ge(zd, n + 2)
                w_lo(n + 2, 0)
                dve.wait_ge(gd, u + 1)
                rope(0, KT, GA, None, vu)
                dve.wait_ge(zd, n + 3)
                rope(1, QT, ES, SCALE)
                w_lo(n + 3, 1)
                soft_in(SWA, u, l, j, 0)
                soft_out(SWA, u)
                w_lo(n + 4, 0)
                take_probs(SWA, u, vu)
                w_lo(n + 5, 1)
                rope(1, QT, ES, SCALE)
                soft_in(SWA, u + 1, l, j, 1)
                soft_out(SWA, u + 1)
                w_lo(n + 6, 0)
                take_probs(SWA, u + 1)
                w_lo(n + 7, 1)
                soft_in(MEM, u + 2)
                soft_out(MEM, u + 2)
                take_probs(MEM, u + 2)
                w_lo(n + 8, 0)
                gate(0, u, 2 * GH + j * 2, m + 4)
                soft_in(MEM, u + 3)
                soft_out(MEM, u + 3)
                w_lo(n + 9, 1)
                gate(1, u + 1, 2 * GH + 1 + j * 2, m + 4)
                take_probs(MEM, u + 3)
                w_lo(n + 10, 0)
                gate(0, u + 2, 3 * GH + j * 2, m + 5)
                w_lo(n + 11, 1)
                gate(1, u + 3, 3 * GH + 1 + j * 2, m + 5)

            def mem_lo(r):
                for p in range(NQ):
                    cs = slice(p * KC // NQ, (p + 1) * KC // NQ)
                    dve.wait_ge(m_hi, NQ * r + p + 1)
                    dve.tensor_tensor(MTL[:, cs, :], MTR[:, cs, :], MTH[:, cs, :].bitcast(F32), ALU.subtract) \
                        .then_inc(m_lo, 1)

            def shift(c):
                dve.tensor_tensor(OY[:, c, :], OY[:, c, :], SHIFT, ALU.subtract).then_inc(cen, 1)

            def rstd(r):
                mean, mean_sq = AB[:, 0:2, 0:HALF], AB[:, 2:4, 0:HALF]
                dve.wait_ge(m2, r + 1)
                dve.scalar_tensor_tensor(split2(VE), mean_sq, EPS, split2(SCR), ALU.add, ALU.subtract).then_inc(vr, 1)
                dve.wait_ge(sd, r + 1)
                chain.link(dve.scalar_tensor_tensor(SCR, RSTD, -0.5, VE, ALU.mult, ALU.mult))
                chain.link(dve.tensor_tensor(SCR, SCR, RSTD, ALU.mult))
                chain.link(dve.scalar_tensor_tensor(RSTD, SCR, 1.5, RSTD, ALU.add, ALU.mult))
                dve.scalar_tensor_tensor(split2(NMR), mean, -1.0, split2(RSTD), ALU.mult, ALU.mult).then_inc(bs, 1)

            def times_rstd(c):
                dve.tensor_tensor(OY[:, c, :], OY[:, c, :], RSTD, ALU.mult).then_inc(n1, 1)

            def take_turned(l, f):
                dve.wait_ge(to, l * GH + f + 1)
                dve.wait_ge(o_mv[f % 2], 16 * (l * (GH // 2) + f // 2 + 1))
                dve.tensor_copy(MVN[:, f % 2, :], GB[:, 1 + 2 * (f % 2), 0:NMEM]).then_inc(tf, 1)

            dve.memset(esum[:, :], 1.0)
            for released, count in ((zd, 1), (zf[0], 1), (zf[1], 1), (tf, 1), (gd, 1), (oe, 2), (pv, 2), (sm1, 1),
                                    (sm2, 2)):
                dve.sem_inc(released, count)
            dve.memset(one[:, :], 1.0)
            dve.memset(ones[:, :], 1.0 / DM).then_inc(s_one, 1)
            dve.wait_ge(s_one, 1)
            w_lo(0, 0)
            mem_lo(0)
            dve.wait_ge(sh, 1)
            for p in range(NQ):
                dve.wait_ge(s_x[p], 16)
                with dve.Fori(p * KC // NQ, (p + 1) * KC // NQ) as c:
                    nc.cur_bb.disable_value_cache()
                    shift(c)
            dve.wait_ge(s_const, 16 * N_CONST)
            with dve.Fori(0, DEPTH) as layer:
                nc.cur_bb.disable_value_cache()
                l, = own(dve, layer)
                chain.sem = c_dl
                chain.start(l * CH["ln"])
                w_lo(l * LT + 1, 1)
                dve.wait_ge(ffh, l + 1)
                dve.tensor_tensor(WFF[:, :, GH:2 * GH], WFR[:, :, :], WFF[:, :, 0:GH].bitcast(F32),
                                  ALU.subtract).then_inc(ffl, 1)
                c = 0
                for kind, i in LN_PLAN:
                    if kind == "stat":
                        rstd(l)
                    elif kind == "mem":
                        for _ in range(NORMED_BEFORE.get(i, 0)):
                            times_rstd(c)
                            c += 1
                        w_lo(l * LT + i + 2, i % 2)
                    else:
                        take_turned(l, i - GH)
                assert chain.k == CH["ln"], ("ln", chain.k)
                chain.sem = c_df
                chain.start(l * CH["ff"])
                dve.wait_ge(ffd, l + 1)
                bf = bF[:, bass.ds(l, 1)]
                chain.link(dve.tensor_scalar(split2(LF), AB[0:GH, 0:2, 0:HALF], bf, None, ALU.add))
                dve.scalar_tensor_tensor(T1, LF, -1.0, LF, ALU.mult, ALU.max).then_inc(ffa, 1)
                dve.wait_ge(ffe, l + 1)
                dve.scalar_tensor_tensor(LF, LF, 0.0, T1, ALU.min, ALU.subtract).then_inc(flr, 1)
                dve.wait_ge(flr, l + 1)
                unit = one[0:GH, 0:1]
                chain.step(dve.tensor_tensor_scan(NR[:, 0:SEQ], unit.broadcast_to([GH, SEQ]), LF[:, 0:SEQ], 0.0,
                                                  ALU.mult, ALU.subtract))
                chain.link(dve.tensor_tensor_scan(NR[:, SEQ:SEQ + PAST], unit.broadcast_to([GH, PAST]), CL[:, :], 0.0,
                                                  ALU.mult, ALU.subtract))
                dve.tensor_tensor_scan(NR[:, SEQ + PAST:], unit.broadcast_to([GH, DEC]), LF[:, SEQ:TOK],
                                       NR[:, SEQ + PAST - 1:SEQ + PAST], ALU.mult, ALU.subtract).then_inc(ncr, 1)
                assert chain.k == CH["ff"], ("ff", chain.k)
                l, = own(dve, layer)
                for gi, (g, first, key, csem) in enumerate(((FOX, A0, "fox", c_da), (BAND, B0, "band", c_db))):
                    with dve.Fori(0, GH) as h:
                        nc.cur_bb.disable_value_cache()
                        chain.sem = csem
                        chain.start((l * GH + h) * CH[key])
                        head(g, l * LT + first + h * HEAD_TILES, l * (LT // 2) + first // 2 + h * 2 + 1,
                             l * HEADS + GH * gi + h,
                             l * V_UNITS + GH * gi + h, l, h, h + GH * gi)
                        assert chain.k == CH[key], (key, chain.k)
                with dve.Fori(0, PAIRS) as j:
                    nc.cur_bb.disable_value_cache()
                    chain.sem = c_dc
                    chain.start((l * PAIRS + j) * CH["pair"])
                    pair(l * LT + C0 + j * PAIR_TILES, l * (LT // 2) + C0 // 2 + j * (PAIR_TILES // 2) + 1, l * HEADS + 2 * GH + j * 4, l * V_UNITS + 2 * GH + j, l, j)
                    assert chain.k == CH["pair"], ("pair", chain.k)
                for c in range(KC):
                    dve.wait_ge(oh[1], l * KC + c + 1)
                    dve.tensor_tensor(XL[:, c, HALF:TOK], OY[:, c, HALF:TOK], XH[:, c, HALF:TOK].bitcast(F32),
                                      ALU.subtract).then_inc(ol[1], 1)

                def residual(c, s, count, xr):
                    dve.wait_ge(zd, count + 1)
                    dve.wait_ge(ld_xr[s], xr)
                    dve.scalar_tensor_tensor(split2(OY[:, c, :]), split2(XR[:, s, :]), ALPHA, z2(s),
                                             ALU.mult, ALU.add).then_inc(zf[s], 1)

                def summed(c, s, q):
                    residual(c, s, n + c + 1, 16 * (l * (KC // 2) + q + 1))
                    dve.wait_ge(zf[s], m + q + 1)
                    shift(c)

                n, m = l * LT + O0, l * (LT // 2) + O0 // 2 + 1
                w_lo(n + 2, 0)
                residual(0, 0, n + 1, 16 * (l * (KC // 2) + 1))
                w_lo(n + 3, 1)
                dve.wait_ge(sh, l + 2)
                dve.wait_ge(zf[0], m + 1)
                shift(0)
                summed(1, 1, 0)
                mem_lo(l + 1)
                with dve.Fori(1, KC // 2 - 1) as q:
                    nc.cur_bb.disable_value_cache()
                    for s in range(2):
                        w_lo(n + q * 2 + s + 2, s)
                        summed(q * 2 + s, s, q)
                summed(KC - 2, 0, KC // 2 - 1)
                w_lo(n + KC, 0)
                summed(KC - 1, 1, KC // 2 - 1)
            chain.sem = c_dl
            chain.start(DEPTH * CH["ln"])
            rstd(DEPTH)
            for c in range(KC):
                times_rstd(c)

        @block.gpsimd
        def _(pool):
            def sum_up(r, c, s):
                pool.wait_ge(cen, r * KC + c + 1)
                pool.wait_ge(sm1, r * KC + c + 1)
                pool.tensor_tensor(SUM1, SUM1, OY[:, c, :], ALU.add).then_inc(sm1, 1)
                pool.wait_ge(sqr, r * KC + c + 1)
                pool.wait_ge(sm2, r * KC + c + 2)
                pool.tensor_tensor(SUM2, SUM2, SQ[s], ALU.add).then_inc(sm2, 1)

            def less_mean(r, c):
                pool.wait_ge(n1, r * KC + c + 1)
                pool.tensor_tensor(OY[:, c, :], OY[:, c, :], NMR, ALU.add).then_inc(n2, 1)

            def x_lo(l, c):
                pool.wait_ge(xh, l * KC + c + 1)
                pool.tensor_tensor(XL[:, c, :], OY[:, c, :], XH[:, c, :].bitcast(F32), ALU.subtract).then_inc(xl, 1)

            pool.memset(LNB[:, 0:2, :], 0.0).then_inc(zero, 1)
            pool.dma_start(OY[:, 0, :], x_t[:, 0, :]).then_inc(s_x0, 16)
            for p in range(NQ):
                cs = slice(max(p * KC // NQ, 1), (p + 1) * KC // NQ)
                pool.dma_start(OY[:, cs, :], x_t[:, cs, :]).then_inc(s_x[p], 16)
            for dst, src in ((ident, ident_d), (causal, causal_d), (swam, swa_mask_d), (cos, cos_d), (sin, sin_d),
                             (gT, ln_gt), (bT, ln_bt)):
                pool.dma_start(dst[:, :], src).then_inc(s_const, 16)
            pool.dma_start(snk[:, :], sinks.partition_broadcast(P)).then_inc(s_const, 16)
            pool.dma_start(bF[:, :], bff).then_inc(s_const, 16)
            for i, done in enumerate((o_k, o_v, o_mv[0], o_mv[1])):
                pool.dma_start(rsum[i:i + 1, NT:NT + 1], ident_d[0:1, 0:1]).then_inc(done, 16)
            for i in range(DEPTH):
                src = bass.AP(rel_pad.tensor, i * GH * RELW, [[RELW, GH], [0, P], [1, RELW]])
                pool.dma_start(rel_rows[i * GH:(i + 1) * GH], src).then_inc(s_toep, 16)
            pool.wait_ge(zero, 1)
            for p in range(NQ):
                with pool.Fori(p * KC // NQ // 2, (p + 1) * KC // NQ // 2) as q:
                    nc.cur_bb.disable_value_cache()
                    for s in range(2):
                        sum_up(0, q * 2 + s, s)
            pool.wait_ge(s_toep, 16 * DEPTH)

            with pool.Fori(0, DEPTH) as layer:
                nc.cur_bb.disable_value_cache()
                l, = own(pool, layer)
                pool.dma_start(WFR[:, :, :], wff[l]).then_inc(ld_ff, 16)
                pool.dma_start(CL[:, :], fox_logf[l]).then_inc(ld_ff, 16)
                wait_apart(pool, bs, l + 1)
                c = 0
                for kind, i in LN_PLAN:
                    if kind == "mem":
                        for _ in range(NORMED_BEFORE.get(i, 0)):
                            less_mean(l, c)
                            if c:
                                x_lo(l, c - 1)
                            c += 1
                        if i == MEM_TILES - 1:
                            x_lo(l, KC - 1)
                    elif kind == "mv":
                        wait_apart(pool, tf, l * GH + i - GH + 2)
                        pool.dma_start(mv_o[l, i - GH], MVN[:, i % 2, :].rearrange("p (b d) -> p b d", b=2)) \
                            .then_inc(o_mv[i % 2], 16)
                wait_apart(pool, flr, l + 1)
                pool.dma_start(fl_o[l], LF).then_inc(o_fl, 16)
                wait_apart(pool, ncr, l + 1)
                pool.dma_start(nc_rows, NR).then_inc(o_rows, 16)
                pool.wait_ge(o_rows, 16 * (l + 1))
                for s in range(2):
                    pool.wait_ge(o_mk[s], 16 * (GH // 2) * (l + 1))
                    pool.wait_ge(o_mv[s], 16 * ((GH // 2) * (l + 1) + 1))
                wait_apart(pool, o_x, 16 * NQ * (l + 1))
                for s in range(2):
                    pool.dma_start(XR[:, s, :], x_res[s]).then_inc(ld_xr[s], 16)
                pool.memset(LNB[:, 0:2, :], 0.0).then_inc(zero, 1)

                l, = own(pool, layer)
                for gi, (g, first) in enumerate(((FOX, A0), (BAND, B0))):
                    with pool.Fori(0, GH) as h:
                        nc.cur_bb.disable_value_cache()
                        u, vu = l * HEADS + GH * gi + h, l * V_UNITS + GH * gi + h
                        m = l * (LT // 2) + first // 2 + h * 2 + 1
                        pool.wait_ge(pv, 2 * u + 2)
                        kc, vc = (fox_k, fox_v) if g is FOX else (band_k, band_v)
                        ko, vo = (fk_o, fv_o) if g is FOX else (bk_o, bv_o)
                        pool.dma_start(KTC[:, :], kc[l, h]).then_inc(ld_kc, 16)
                        if g is FOX:
                            pool.dma_start(BI[:, :], nc_rows[h].partition_broadcast(P)).then_inc(ld_bias, 16)
                        else:
                            pool.dma_start(BI[:, 0:SEQ], toep[l * GH + h]).then_inc(ld_bias, 16)
                        pool.dma_start(VC[:, :, :], vc[l, h]).then_inc(ld_vc, 16)
                        wait_apart(pool, ld_bias, 16 * (l * 2 * GH + GH * gi + h + 1))
                        if g is FOX:
                            pool.tensor_tensor(BD[:, 0:SEQ].rearrange("p (b c) -> p b c", b=4),
                                               BI[:, 0:SEQ].rearrange("p (b c) -> p b c", b=4),
                                               causal[:, :].unsqueeze(1).broadcast_to([P, 4, P]), ALU.add) \
                                .then_inc(bdr, 1)
                            pool.tensor_tensor(BD[0:DEC, SEQ:TOK], BI[0:DEC, SEQ + PAST:], causal[0:DEC, 0:DEC],
                                               ALU.add).then_inc(bdr, 1)
                        else:
                            pool.memset(BI[0:P // 2, SEQ - P // 2:SEQ], NEG).then_inc(bmr, 1)
                        wait_apart(pool, zf[0], m + 1)
                        pool.dma_start(ko[l, h], KT[:, :]).then_inc(o_k, 16)
                        wait_apart(pool, zf[0], m + 2)
                        pool.dma_start(vo[l, h], VT[:, :]).then_inc(o_v, 16)
                with pool.Fori(0, PAIRS) as j:
                    nc.cur_bb.disable_value_cache()
                    u, vu, dm = l * HEADS + 2 * GH + j * 4, l * V_UNITS + 2 * GH + j, l * GH + 2 * j
                    m = l * (LT // 2) + C0 // 2 + j * (PAIR_TILES // 2) + 1
                    wait_apart(pool, pv, 2 * u + 2)
                    pool.dma_start(KTC[:, 0:P], swa_k[l, j]).then_inc(ld_kc, 16)
                    pool.dma_start(VC[:, 0, :], swa_v[l, j]).then_inc(ld_vc, 16)
                    wait_apart(pool, zf[0], m + 1)
                    pool.dma_start(sk_o[l, j], KT[:, TOK - P - DEC:TOK]).then_inc(o_k, 16)
                    wait_apart(pool, zf[0], m + 2)
                    pool.dma_start(sv_o[l, j], VT[:, TOK - P - DEC:TOK]).then_inc(o_v, 16)
                    for k in range(2):
                        pool.wait_ge(sc[2], u + k + 2)
                        wait_apart(pool, o_k, 16 * (vu + 2))
                        pool.dma_start(KT[:, 0:NMEM], mk_o[l, j * 2 + k]).then_inc(ld_km, 16)
                        pool.dma_start(KTC[:, :], mem_k[l, j * 2 + k]).then_inc(ld_kc, 16)
                        wait_apart(pool, pv, 2 * (u + k + 3))
                        pool.dma_start(V[:, 0:2, :], mv_o[l, j * 2 + k]).then_inc(ld_vm, 16)
                        pool.dma_start(VC[:, :, :], mem_v[l, j * 2 + k]).then_inc(ld_vc, 16)
                pool.wait_ge(zero, l + 2)
                for c in range(KC):
                    pool.wait_ge(oh[0], l * KC + c + 1)
                    pool.tensor_tensor(XL[:, c, 0:HALF], OY[:, c, 0:HALF], XH[:, c, 0:HALF].bitcast(F32),
                                       ALU.subtract).then_inc(ol[0], 1)
                r, = own(pool, layer + 1)

                def load_residual(q, s):
                    wait_apart(pool, zf[s], l * (LT // 2) + O0 // 2 + q + 1)
                    pool.dma_start(XR[:, s, :], x_res[q * 2 + s]).then_inc(ld_xr[s], 16)

                with pool.Fori(0, KC // 2 - 1) as q:
                    nc.cur_bb.disable_value_cache()
                    for s in range(2):
                        load_residual(q + 1, s)
                        sum_up(r, q * 2 + s, s)
                for s in range(2):
                    sum_up(r, KC - 2 + s, s)
            wait_apart(pool, bs, DEPTH + 1)
            for c in range(KC):
                less_mean(DEPTH, c)
            pool.wait_ge(o_k, 16 * (V_UNITS * DEPTH + 1))


CH = {"ln": 3, "ff": 3, "fox": 12, "band": 8, "pair": 56}

_OUTS = [(KC, P, TOK), ((DEPTH, GH, P, TOK)), ((DEPTH, GH, P, TOK)), ((DEPTH, GH, TOK)),
         ((DEPTH, GH, P, TOK)), ((DEPTH, GH, P, TOK)), ((DEPTH, PAIRS, P, P + DEC)), ((DEPTH, PAIRS, P, P + DEC)),
         ((DEPTH, GH, P, NMEM)), ((DEPTH, GH, P, 2, HD))]


def kernel(**inputs):
    import numpy as np
    import concourse.bacc as bacc
    from concourse.bass_utils import run_bass_kernel_spmd as run

    f32 = np.float32
    a = {k: np.asarray(v) for k, v in inputs.items()}

    def cols(w, c, n=P):
        return w[:, c:c + n].reshape(KC, P, n).transpose(1, 0, 2)

    fq, fk, fv, ff = 0, 512, 1024, 1536
    bq = ff + GH
    bk, bv = bq + 512, bq + 1024
    sq = bq + 1536
    sk, sv = sq + 512, sq + 768
    mq = sq + 1024
    gate = mq + 512
    layers = []
    for l in range(DEPTH):
        wi, wm, wo = a["w_in"][l], a["w_mem_kv"][l], a["w_out"][l]
        t = [cols(wm, P * j) for j in range(MEM_TILES)]
        for g, (k0, q0, v0) in enumerate(((fk, fq, fv), (bk, bq, bv))):
            for h in range(GH):
                t += [cols(wi, c + P * h) for c in (k0, q0, v0)] + [cols(wi, gate + P * (GH * g + h))]
        for j in range(PAIRS):
            t += [cols(wi, sk + P * j), cols(wi, sq + 2 * P * j), cols(wi, sv + P * j), cols(wi, sq + 2 * P * j + P)]
            t += [cols(wi, mq + 2 * P * j + P * k) for k in range(2)]
            t += [cols(wi, gate + P * (2 * GH + 2 * j + k)) for k in range(2)]
            t += [cols(wi, gate + P * (3 * GH + 2 * j + k)) for k in range(2)]
        t += [cols(wo, P * j) for j in range(KC)]
        layers += t
    def keys(x):
        return x[:, 0].transpose(0, 2, 3, 1)

    def values(x):
        d, _, n, h, f = x.shape
        return x[:, 0].reshape(d, n // P, P, h, f).transpose(0, 3, 2, 1, 4)

    x_all = np.concatenate([a["x_prompt"][0], a["x_sample"][0]], 0)
    gs = np.concatenate([a["ln_in_g"][None], a["ln_g"]], 0)
    bs = np.concatenate([a["ln_in_b"][None], a["ln_b"]], 0)
    pos = np.concatenate([np.arange(SEQ), PAST + np.arange(DEC)]).astype(f32)
    half = HD // 2
    inv = (10000.0 ** (-np.arange(half) / half)).astype(f32)
    ang = inv[:, None] * pos[None, :]
    cos = np.concatenate([np.cos(ang), np.cos(ang)], 0)
    sin = np.concatenate([-np.sin(ang), np.sin(ang)], 0)
    r = np.arange(P)
    causal = np.where(r[None, :] <= r[:, None], 0.0, NEG)
    ahead = np.arange(2 * P)[None, :] // 64 - r[:, None] // 64
    swa = np.where((ahead >= 0) & (ahead <= 2), 0.0, NEG)

    arrays = {
        "wt": np.stack(layers).reshape(DEPTH * LT, P, KC, P),
        "wff": np.stack([cols(a["w_in"][l], ff, GH) for l in range(DEPTH)]),
        "bff": a["b_f"].T,
        "x_t": x_all.T.reshape(KC, P, TOK).transpose(1, 0, 2),
        "mem_t": a["mem_prompt"][0].T.reshape(KC, P, NMEM).transpose(1, 0, 2),
        "fox_k": keys(a["cache_fox_k"]), "fox_v": values(a["cache_fox_v"]),
        "fox_logf": a["cache_fox_logf"][:, 0].transpose(0, 2, 1),
        "band_k": keys(a["cache_band_k"]), "band_v": values(a["cache_band_v"]),
        "swa_k": keys(a["cache_swa_k"]), "swa_v": values(a["cache_swa_v"]).reshape(DEPTH, PAIRS, P, HD),
        "mem_k": keys(a["cache_mem_k"]), "mem_v": values(a["cache_mem_v"]),
        "rel_pad": np.pad(a["rel_bias"], ((0, 0), (0, 0), (SEQ + P - 257, 0)), mode="edge"),
        "sinks": a["sinks"].reshape(1, -1)[0],
        "ln_gt": gs.reshape(-1, KC, P).transpose(2, 0, 1).reshape(P, -1),
        "ln_bt": bs.reshape(-1, KC, P).transpose(2, 0, 1).reshape(P, -1),
        "ident": np.eye(P), "causal": causal, "swa_mask": swa, "cos": cos, "sin": sin,
    }
    nc = bacc.Bacc("TRN2", target_bir_lowering=False, num_devices=1)
    feed, args = {}, []
    for name, v in arrays.items():
        v = np.ascontiguousarray(v, dtype=f32)
        feed[f"in_{name}"] = v
        args.append(nc.dram_tensor(f"in_{name}", v.shape, F32, kind="ExternalInput").ap())
    for i, shape in enumerate(_OUTS):
        args.append(nc.dram_tensor(f"out_{i}", shape, F32, kind="ExternalOutput").ap())
    encoder_step(nc, *args)
    res = run(nc, [feed], core_ids=[0]).results[0]
    y, fk_, fv_, fl_, bk_, bv_, sk_, sv_, mk_, mv_ = (res[f"out_{i}"] for i in range(len(_OUTS)))

    def heads(x, lo, hi):
        return np.ascontiguousarray(x[:, :, :, lo:hi].transpose(0, 3, 1, 2)[:, None])

    def logf(lo, hi):
        return np.ascontiguousarray(fl_[:, :, lo:hi].transpose(0, 2, 1)[:, None])

    mem_v = np.ascontiguousarray(mv_.transpose(0, 3, 2, 1, 4).reshape(DEPTH, NMEM, GH, HD)[:, None])
    y = np.ascontiguousarray(y.reshape(DM, TOK).T)
    return (y[None, :SEQ], y[None, SEQ:],
            heads(fk_, 0, SEQ), heads(fv_, 0, SEQ), logf(0, SEQ),
            heads(bk_, 0, SEQ), heads(bv_, 0, SEQ),
            heads(sk_, 0, P), heads(sv_, 0, P),
            heads(mk_, 0, NMEM), mem_v,
            heads(fk_, SEQ, TOK), heads(fv_, SEQ, TOK), logf(SEQ, TOK),
            heads(bk_, SEQ, TOK), heads(bv_, SEQ, TOK),
            heads(sk_, P, P + DEC), heads(sv_, P, P + DEC))
```

```python
from contextlib import ExitStack
from itertools import count

import concourse.bass as bass
from concourse import mybir

ALU = mybir.AluOpType
ACT = mybir.ActivationFunctionType
F32 = mybir.dt.float32
F32R = mybir.dt.float32r
AX_X = mybir.AxisListType.X

P = 128
DM = 2048
KC = DM // P
SEQ, DEC, PAST = 512, 32, 256
TOK = SEQ + DEC
HALF = TOK // 2
DEPTH = 2
NMEM = 256
HD = 128
GH = 4
HEADS = 4 * GH
ALPHA = (2 * DEPTH) ** 0.25
EPS = 1e-5
SCALE = HD ** -0.5
NEG = -1e30
RELW = SEQ + P
TILES = [(i * P, P) for i in range(SEQ // P)] + [(SEQ, DEC)]
NT = len(TILES)

MEM_TILES = 2 * GH
HEAD_TILES = 4
PAIR_TILES = 10
PAIRS = 2
A0 = MEM_TILES
B0 = A0 + HEAD_TILES * GH
C0 = B0 + HEAD_TILES * GH
O0 = C0 + PAIR_TILES * PAIRS
LT = O0 + KC

V_UNITS = 2 * GH + PAIRS
K_LOADS = 2 * GH + PAIRS + GH
Q_SPLITS = 3 * GH

class Group:
    def __init__(self, blocks, cached, own, place, sink=False):
        self.blocks, self.cached, self.own, self.place, self.sink = blocks, cached, own, place, sink
        self.width = [P * len(b) for b in blocks] + [P * cached + own]
        self.at = [sum(w + 1 for w in self.width[:i]) for i in range(NT)]
        self.order = [i for _, _, i in place]


CAUSAL = [list(range(i + 1)) for i in range(4)]
FOX = Group(CAUSAL, 2, DEC, [(1, 0, 2), (1, 384, 0), (2, 0, 1), (0, 0, 3), (3, 0, 4)])
BAND = Group(CAUSAL, 2, DEC, [(1, 0, 2), (1, 384, 0), (2, 0, 1), (0, 0, 3), (3, 0, 4)])
SWA = Group([[0], [0, 1], [1, 2], [2, 3]], 1, DEC, [(0, 0, 1), (0, 256, 2), (1, 0, 3), (1, 256, 0), (2, 0, 4)], sink=True)
MEM = Group([[0, 1]] * 4, 2, 0, [(0, 0, 0), (0, 256, 1), (1, 0, 2), (1, 256, 3), (2, 0, 4)])
SW = sum(w + 1 for w in FOX.width)
PTW = 10 * P + 3 * DEC

LN_PLAN = [("mem", 0), ("mem", 1), ("stat", 0), ("mem", 2), ("mem", 3), ("mem", 4), ("mem", 5), ("mv", 4),
           ("mem", 6), ("mv", 5), ("mem", 7), ("mv", 6), ("forget", 0), ("mv", 7)]
NORMED_DVE = {3: 3, 4: 3, 5: 3, 6: 3, 7: 4}
NORMED_ACT = {4: 3, 5: 3, 6: 3, 7: 3}
SHARE = [c for c in range(KC) if c % 4 == 3]
LAST_SHARE = [c for c in range(KC) if c % 3 == 2]
LOW_SHARE = [(0, 1, 2, 3, 4, 5, 8, 11, 14), (0, 3, 6, 9, 12, 15)]
NQ = 4


def own(eng, *values):
    out = []
    for v in values:
        if isinstance(v, int):
            out.append(v)
            continue
        reg = eng.alloc_register(f"held{next(REGISTER_NUMBER)}")
        eng.reg_mov(reg, v)
        out.append(eng.snap(reg, min_val=0, max_val=v.max_val))
    return out


REGISTER_NUMBER = count()


class Chain:

    def __init__(self, eng, sem):
        self.eng, self.sem, self.base, self.k = eng, sem, 0, 0

    def start(self, base):
        self.base, self.k = own(self.eng, base)[0], 0

    def step(self, ins):
        ins.then_inc(self.sem, 1)
        self.k += 1

    def wait(self):
        self.eng.wait_ge(self.sem, self.base + self.k)

    def link(self, ins):
        self.step(ins)
        self.wait()


def encoder_step(nc, wt, wff, bff, x_t, mem_t, fox_k, fox_v, fox_logf, band_k, band_v, swa_k, swa_v, mem_k, mem_v,
                 rel_pad, sinks, ln_gt, ln_bt, ident_d, causal_d, swa_mask_d, cos_d, sin_d,
                 y_o, fk_o, fv_o, fl_o, bk_o, bv_o, sk_o, sv_o, mk_o, mv_o):
    with ExitStack() as ctx:
        top = [nc.sbuf_base]
        top[0] += -top[0] % 64

        def sb_at(name, shape, off, dt=F32):
            return nc.alloc_sbuf_tensor_at(name, shape, dt, offset=off)

        def sb(name, shape, dt=F32):
            size = 4
            for s in shape[1:]:
                size *= s
            off = top[0]
            top[0] += size + -size % 64
            return sb_at(name, shape, off, dt)

        def sem(name):
            return ctx.enter_context(nc.semaphore(name))

        GB = ctx.enter_context(nc.psum_tensor("GB", [P, 4, 512], F32))
        AB = ctx.enter_context(nc.psum_tensor("AB", [P, 4, 512], F32))

        XH = sb("XH", [P, KC, TOK], F32R)
        XL = sb("XL", [P, KC, TOK], F32R)
        OY = sb("OY", [P, KC, TOK])
        WR = sb("WR", [P, 2, KC, P])
        WH = sb("WH", [P, 2, KC, P], F32R)
        WL = sb("WL", [P, 2, KC, P], F32R)
        lnb_at = top[0]
        LNB = sb("LNB", [P, 5, TOK])
        ones = sb("ones", [P, P])
        arena = top[0]
        MTH = sb("MTH", [P, KC, NMEM], F32R)
        MTR = sb_at("MTR", [P, KC, NMEM], top[0])
        MTL = sb("MTL", [P, KC, NMEM], F32R)
        arena_end, top[0] = top[0], arena
        KT = sb("KT", [P, TOK])
        QT = sb("QT", [P, TOK])
        VT = sb("VT", [P, TOK])
        ES = sb("ES", [P, TOK])
        GA = sb("GA", [P, TOK])
        V = sb("V", [P, NT, HD])
        S = sb("S", [P, SW])
        PT = sb("PT", [P, PTW])
        KTC = sb("KTC", [P, PAST])
        VC = sb("VC", [P, 2, HD])
        BI = sb("BI", [P, SEQ + PAST + DEC])
        BD = sb("BD", [P, TOK])
        assert top[0] <= arena_end, (top[0], arena_end)
        top[0] = arena_end
        MT = sb_at("MT", [P, 2, NMEM], top[0])
        MVN = sb_at("MVN", [P, 2, NMEM], top[0] + 8 * NMEM)
        XR = sb("XR", [P, 2, TOK])
        ident = sb("ident", [P, P])
        causal = sb("causal", [P, P])
        swam = sb("swam", [P, 2 * P])
        cos = sb("cos", [P, TOK])
        sin = sb("sin", [P, TOK])
        snk = sb("snk", [P, DEPTH * GH])
        gT = sb("gT", [P, (DEPTH + 1) * KC])
        bT = sb("bT", [P, (DEPTH + 1) * KC])
        bF = sb("bF", [GH, DEPTH])
        WFR = sb("WFR", [P, DEPTH * KC, GH])
        WFF = sb("WFF", [P, KC, 2 * GH], F32R)
        CL = sb("CL", [GH, DEPTH * PAST])
        nmx = sb("nmx", [P, 8])
        esum = sb("esum", [P, 8])
        rsum = sb("rsum", [P, 8])
        one = sb("one", [P, 1])
        assert top[0] <= nc.sbuf_usable_end, (top[0], nc.sbuf_usable_end)
        SPL = sb_at("SPL", [P, 5, TOK], lnb_at, F32R)
        KH, KL, QH, QL, KCH, KCL = (SPL[:, 0, :], SPL[:, 1, :], SPL[:, 2, :], SPL[:, 3, :], SPL[:, 4, 0:PAST],
                                    SPL[:, 4, PAST:2 * PAST])
        SUM1, SUM2, SHIFT, SQ = LNB[:, 0, :], LNB[:, 1, :], LNB[:, 2, :], [LNB[:, 3, :], LNB[:, 4, :]]
        RSTD, NMR, VE, SCR = LNB[:, 0, :], LNB[:, 1, :], LNB[:, 3, :], LNB[:, 4, :]
        NR = LNB[0:GH, 0:2, :].rearrange("p s c -> p (s c)")[:, 0:SEQ + PAST + DEC]
        LF, T1 = LNB[0:GH, 3, :], LNB[0:GH, 4, :]

        x_res = nc.dram_tensor("x_res", (KC, P, TOK), F32, kind="Internal").ap()
        nc_rows = nc.dram_tensor("nc_rows", (GH, SEQ + PAST + DEC), F32, kind="Internal").ap()
        rel_rows = nc.dram_tensor("rel_rows", (DEPTH * GH, P, RELW), F32, kind="Internal").ap()
        toep = bass.AP(rel_rows.tensor, P - 1, [[P * RELW, DEPTH * GH], [RELW - 1, P], [1, SEQ]])

        s_const = sem("s_const")
        s_toep = sem("s_toep")
        s_x0 = sem("s_x0")
        s_x = [sem(f"s_x{p + 1}") for p in range(NQ)]
        raw = [sem("raw0"), sem("raw1")]
        ld_mem = [sem(f"ld_mem{p}") for p in range(NQ)]
        ld_kc = sem("ld_kc")
        ld_vc = sem("ld_vc")
        ld_km = sem("ld_km")
        ld_vm = sem("ld_vm")
        ld_bias = sem("ld_bias")
        ld_xr = [sem("ld_xr0"), sem("ld_xr1")]
        o_k = sem("o_k")
        o_v = sem("o_v")
        o_mk = [sem("o_mk0"), sem("o_mk1")]
        o_mv = [sem("o_mv0"), sem("o_mv1")]
        o_x = sem("o_x")
        o_fl = sem("o_fl")
        o_rows = sem("o_rows")
        o_y = sem("o_y")
        hi = sem("hi")
        lo = sem("lo")
        zd = sem("zd")
        zf = [sem("zf0"), sem("zf1")]
        m_hi = sem("m_hi")
        m_lo = sem("m_lo")
        mu0 = sem("mu0")
        sh = sem("sh")
        zero = sem("zero")
        cen = sem("cen")
        sqr = sem("sqr")
        sm1 = sem("sm1")
        sm2 = sem("sm2")
        st = sem("st")
        m2 = sem("m2")
        vr = sem("vr")
        sd = sem("sd")
        bs = sem("bs")
        n1 = sem("n1")
        n2 = [sem("n2_dve"), sem("n2_pool")]
        n1p = sem("n1p")
        nx = sem("nx")
        to = sem("to")
        tf = sem("tf")
        xh = sem("xh")
        xl = sem("xl")
        ffh = sem("ffh")
        ffl = sem("ffl")
        ffd = sem("ffd")
        ffe = sem("ffe")
        ffa = sem("ffa")
        flr = sem("flr")
        ncr = sem("ncr")
        bdr = sem("bdr")
        bmr = sem("bmr")
        sc = [sem(f"sc{b}") for b in range(4)]
        mk = sem("mk")
        ex = sem("ex")
        pr = sem("pr")
        pt = sem("pt")
        pte = sem("pte")
        vt = sem("vt")
        ve = sem("ve")
        vse = sem("vse")
        pv = sem("pv")
        oe = sem("oe")
        kh = sem("kh")
        k_low = sem("k_low")
        qh = sem("qh")
        eg = sem("eg")
        gd = sem("gd")
        oh = [sem("oh0"), sem("oh1")]
        ol = [[sem(f"ol{h}_{e}") for e in ("dve", "pool")] for h in range(2)]
        c_dl = sem("c_dl")
        c_df = sem("c_df")
        c_da = sem("c_da")
        c_db = sem("c_db")
        c_dc = sem("c_dc")
        c_al = sem("c_al")
        s_one = sem("s_one")

        block = ctx.enter_context(nc.Block())
        N_CONST = 11

        def z2(slot):
            return GB[:, 2 * slot:2 * slot + 2, 0:HALF]

        def split2(t):
            return t.rearrange("p (h c) -> p h c", h=2)

        def normed(r, c):
            share = LAST_SHARE if isinstance(r, int) else SHARE
            by_pool = c in share
            before = sum((k in share) == by_pool for k in range(c))
            each = len(SHARE) if by_pool else KC - len(SHARE)
            return n2[by_pool], r * each + before + 1

        def low_made(l, h, c):
            by_pool = c in LOW_SHARE[h]
            before = sum((k in LOW_SHARE[h]) == by_pool for k in range(c))
            each = len(LOW_SHARE[h]) if by_pool else KC - len(LOW_SHARE[h])
            return ol[h][by_pool], l * each + before + 1

        def make_low(eng, l, h, c):
            cols = slice(h * HALF, (h + 1) * HALF)
            by_pool = c in LOW_SHARE[h]
            eng.wait_ge(oh[h], l * KC + c + 1)
            eng.tensor_tensor(XL[:, c, cols], OY[:, c, cols], XH[:, c, cols].bitcast(F32), ALU.subtract) \
                .then_inc(ol[h][by_pool], 1)

        def pt_col(j):
            return PT[:, P * j:P * (j + 1)]

        def wait_apart(eng, sem, count):
            held, = own(eng, count)
            eng.wait_ge(s_one, 1)
            eng.wait_ge(sem, held)

        @block.sync
        def _(sp):
            sp.dma_start(WR[:, 0, :, :], wt[0]).then_inc(raw[0], 16)
            sp.dma_start(OY[:, 0, :], x_t[:, 0, :]).then_inc(s_x0, 16)
            def load_x(p):
                cs = slice(max(p * KC // NQ, 1), (p + 1) * KC // NQ)
                sp.dma_start(OY[:, cs, :], x_t[:, cs, :]).then_inc(s_x[p], 16)

            load_x(0)
            load_x(1)
            for p in range(NQ):
                cs = slice(p * KC // NQ, (p + 1) * KC // NQ)
                sp.dma_start(MTR[:, cs, :], mem_t[:, cs, :]).then_inc(ld_mem[p], 16)
            sp.dma_start(WR[:, 1, :, :], wt[1]).then_inc(raw[1], 16)
            load_x(2)
            load_x(3)
            for dst, src in ((ident, ident_d), (causal, causal_d), (swam, swa_mask_d), (cos, cos_d), (sin, sin_d),
                             (gT, ln_gt), (bT, ln_bt)):
                sp.dma_start(dst[:, :], src).then_inc(s_const, 16)
            sp.dma_start(snk[:, :], sinks.partition_broadcast(P)).then_inc(s_const, 16)
            sp.dma_start(bF[:, :], bff).then_inc(s_const, 16)
            sp.dma_start(WFR[:, :, :], wff).then_inc(s_const, 16)
            sp.dma_start(CL[:, :], fox_logf).then_inc(s_const, 16)
            with sp.Fori(1, DEPTH * LT // 2) as m:
                nc.cur_bb.disable_value_cache()
                for s in range(2):
                    sp.wait_ge(lo, m * 2 + s - 1)
                    sp.dma_start(WR[:, s, :, :], wt[m * 2 + s]).then_inc(raw[s], 16)
            sp.wait_ge(lo, DEPTH * LT)
            for s in range(2):
                sp.sem_inc(raw[s], 16)
            for c in range(0, KC, 2):
                sp.wait_ge(nx, DEPTH * KC + c + 2)
                sp.dma_start(y_o[c:c + 2].rearrange("c p t -> p c t"), OY[:, c:c + 2, :]).then_inc(o_y, 16)
            sp.wait_ge(o_y, 16 * (KC // 2))

        @block.tensor
        def _(pe):
            def gemm_half(n, s, hf, free, split):
                if hf == 0:
                    pe.wait_ge(lo, n + 1)
                    pe.wait_ge(zf[s], free)
                for k in range(KC):
                    if split is not None:
                        pe.wait_ge(*low_made(split, hf, k))
                    for i, (w, x) in enumerate(((WH, XH), (WL, XH), (WH, XL))):
                        mm = pe.matmul(GB[:, 2 * s + hf, 0:HALF], w[:, s, k, :],
                                       x[:, k, hf * HALF:(hf + 1) * HALF],
                                       start=(k == 0 and i == 0), stop=(k == KC - 1 and i == 2))
                if hf == 1:
                    mm.then_inc(zd, 1)

            def gemm(n, m, j, hf=None, split=None):
                for h in (range(2) if hf is None else [hf]):
                    gemm_half(n + j, j % 2, h, m + j // 2, split)

            def scores(g, u, fl=None):
                if g is FOX:
                    pe.wait_ge(flr, fl)
                for j, (b, col, i) in enumerate(g.place):
                    t0, r = TILES[i]
                    if b >= 2:
                        pe.wait_ge(oe, 2 * u + 2)
                    parts = []
                    if i < 4:
                        ks = g.blocks[i][0] * P
                        parts.append((col, g.width[i], KH[:, ks:ks + g.width[i]], KL[:, ks:ks + g.width[i]]))
                    else:
                        w = P * g.cached
                        parts.append((col, w, KCH[:, 0:w], KCL[:, 0:w]))
                        if g.own:
                            parts.append((col + w, DEC, KH[:, SEQ:TOK], KL[:, SEQ:TOK]))
                    for at, w, k_hi, k_lo in parts:
                        for p, (q, k) in enumerate(((QH, k_hi), (QH, k_lo), (QL, k_hi))):
                            mm = pe.matmul(AB[0:r, b, at:at + w], q[:, t0:t0 + r], k, start=(p == 0), stop=(p == 2))
                    if j == len(g.place) - 1 or g.place[j + 1][0] != b:
                        mm.then_inc(sc[b], 1)

            def turn_probs(g, u):
                pe.wait_ge(pr, 5 * u + 5)
                j = 0
                blocks = [(i, b) for i in range(4) for b in range(len(g.blocks[i]))]
                for j, (i, b) in enumerate(blocks):
                    at = g.at[i] + P * b
                    mm = pe.transpose(AB[:, j // 4, P * (j % 4):P * (j % 4 + 1)], S[:, at:at + P], ident[:, :])
                    if j in (3, 7) or (j == len(blocks) - 1 and j < 7):
                        mm.then_inc(pt, 1)
                for b in range(g.cached):
                    mm = pe.transpose(AB[:, 2, 256 + DEC * b:256 + DEC * (b + 1)],
                                      S[0:DEC, g.at[4] + P * b:g.at[4] + P * (b + 1)], ident[0:DEC, 0:DEC])
                if g.own:
                    at = g.at[4] + P * g.cached
                    mm = pe.transpose(AB[0:DEC, 2, 320:320 + DEC], S[0:DEC, at:at + DEC], ident[0:DEC, 0:DEC])
                return mm

            def turn_v(m):
                pe.wait_ge(zf[0], m)
                mm = pe.transpose(AB[0:DEC, 2, 352:352 + P], VT[:, SEQ:TOK], ident[:, :])
                mm.then_inc(pt, 1)
                for i in range(4):
                    mm = pe.transpose(AB[:, 3, P * i:P * (i + 1)], VT[:, P * i:P * (i + 1)], ident[:, :])
                mm.then_inc(vt, 1)

            def mix(g, u, kl, vu=None, dm=None):
                pe.wait_ge(pte, 3 * u + 3)
                pe.wait_ge(ld_vc, 16 * (kl + 1))
                if vu is not None:
                    pe.wait_ge(ve, vu + 1)
                    pe.wait_ge(vse, vu + 1)
                if dm is not None:
                    pe.wait_ge(ld_vm, 16 * (dm + 1))
                j = 0
                for i in range(4):
                    for b, kb in enumerate(g.blocks[i]):
                        mm = pe.matmul(AB[:, 3, P * i:P * (i + 1)], V[:, kb, :], pt_col(j),
                                       start=(b == 0), stop=(b == len(g.blocks[i]) - 1))
                        j += 1
                mm.then_inc(pv, 1)
                for b in range(g.cached):
                    mm = pe.matmul(AB[:, 2, 0:DEC], VC[:, b, :], PT[:, 10 * P + DEC * b:10 * P + DEC * (b + 1)],
                                   start=(b == 0), stop=(b == g.cached - 1 and not g.own))
                if g.own:
                    mm = pe.matmul(AB[:, 2, 0:DEC], V[0:DEC, 4, :], PT[0:DEC, 10 * P + 2 * DEC:10 * P + 3 * DEC],
                                   start=False, stop=True)
                mm.then_inc(pv, 1)

            def head(g, n, m, u, kl, vu, fl):
                n, m, u, kl, vu, fl = own(pe, n, m, u, kl, vu, fl)
                gemm(n, m, 0)
                gemm(n, m, 1)
                gemm(n, m, 2, 0)
                pe.wait_ge(k_low, kl + 1)
                pe.wait_ge(zf[1], m + 1)
                scores(g, u, fl=fl)
                gemm(n, m, 2, 1)
                gemm(n, m, 3, 0)
                turn_probs(g, u)
                turn_v(m + 2)
                gemm(n, m, 3, 1)
                mix(g, u, kl, vu)

            def pair(n, m, u, kl, vu, dm):
                n, m, u, kl, vu, dm = own(pe, n, m, u, kl, vu, dm)
                gemm(n, m, 0)
                gemm(n, m, 1)
                gemm(n, m, 2, 0)
                pe.wait_ge(k_low, kl + 1)
                pe.wait_ge(zf[1], m + 1)
                scores(SWA, u)
                gemm(n, m, 2, 1)
                gemm(n, m, 3, 0)
                turn_probs(SWA, u)
                turn_v(m + 2)
                gemm(n, m, 3, 1)
                mix(SWA, u, kl, vu)
                gemm(n, m, 4, 0)
                pe.wait_ge(zf[1], m + 2)
                scores(SWA, u + 1)
                gemm(n, m, 4, 1)
                gemm(n, m, 5, 0)
                turn_probs(SWA, u + 1).then_inc(pt, 1)
                gemm(n, m, 5, 1)
                mix(SWA, u + 1, kl, vu)
                pe.wait_ge(zf[0], m + 3)
                pe.wait_ge(k_low, kl + 2)
                scores(MEM, u + 2)
                gemm(n, m, 6)
                turn_probs(MEM, u + 2).then_inc(pt, 1)
                gemm(n, m, 7, 0)
                mix(MEM, u + 2, kl + 1, dm=dm)
                pe.wait_ge(zf[1], m + 3)
                pe.wait_ge(k_low, kl + 3)
                scores(MEM, u + 3)
                gemm(n, m, 7, 1)
                gemm(n, m, 8, 0)
                turn_probs(MEM, u + 3).then_inc(pt, 1)
                gemm(n, m, 8, 1)
                mix(MEM, u + 3, kl + 2, dm=dm + 1)
                gemm(n, m, 9)

            def mean_of_first():
                for h in range(2):
                    mm = pe.matmul(AB[:, h, 0:HALF], ones[:, :], OY[:, 0, h * HALF:(h + 1) * HALF],
                                   start=True, stop=True)
                mm.then_inc(mu0, 1)

            def statistics(r):
                pe.wait_ge(sm1, KC * (r + 1) + 1)
                pe.wait_ge(sm2, KC * (r + 1) + 2)
                for i, total in enumerate((SUM1, SUM2)):
                    for h in range(2):
                        mm = pe.matmul(AB[:, 2 * i + h, 0:HALF], ones[:, :], total[:, h * HALF:(h + 1) * HALF],
                                       start=True, stop=True)
                mm.then_inc(st, 1)

            def mem_tile(l, j):
                s, n = j % 2, l * LT + j
                pe.wait_ge(lo, n + 1)
                pe.wait_ge(zf[s], l * (LT // 2) + j // 2 + 1)
                for k in range(KC):
                    if j == 0 and k % (KC // NQ) == 0:
                        pe.wait_ge(m_lo, NQ * l + k // (KC // NQ) + 1)
                    for i, (w, x) in enumerate(((WH, MTH), (WL, MTH), (WH, MTL))):
                        mm = pe.matmul(GB[:, 2 * s, 0:NMEM], w[:, s, k, :], x[:, k, :],
                                       start=(k == 0 and i == 0), stop=(k == KC - 1 and i == 2))
                mm.then_inc(zd, 1)

            pe.wait_ge(s_one, 1)
            pe.wait_ge(s_x0, 16)
            mean_of_first()
            with pe.Fori(0, DEPTH) as layer:
                nc.cur_bb.disable_value_cache()
                l, = own(pe, layer)
                for kind, i in LN_PLAN:
                    if kind == "mem":
                        mem_tile(l, i)
                    elif kind == "stat":
                        statistics(l)
                    elif kind == "forget":
                        pe.wait_ge(ffl, l + 1)
                        for k in range(KC):
                            pe.wait_ge(xl, KC * l + k + 1)
                            for h in range(2):
                                for i, (w, x) in enumerate(((0, XH), (GH, XH), (0, XL))):
                                    mm = pe.matmul(AB[0:GH, h, 0:HALF], WFF[:, k, w:w + GH],
                                                   x[:, k, h * HALF:(h + 1) * HALF],
                                                   start=(k == 0 and i == 0), stop=(k == KC - 1 and i == 2))
                        mm.then_inc(ffd, 1)
                    else:
                        f = i - GH
                        pe.wait_ge(tf, l * GH + max(f, 1))
                        pe.wait_ge(zf[i % 2], l * (LT // 2) + i // 2 + 2)
                        if f == 0:
                            pe.wait_ge(s_const, 16 * N_CONST)
                        for c in range(2):
                            mm = pe.transpose(GB[:, 1 + 2 * (f % 2), P * c:P * (c + 1)],
                                              MT[:, i % 2, P * c:P * (c + 1)], ident[:, :])
                        mm.then_inc(to, 1)
                pe.wait_ge(tf, (l + 1) * GH + 1)
                l, = own(pe, layer)
                for gi, (g, first) in enumerate(((FOX, A0), (BAND, B0))):
                    with pe.Fori(0, GH) as h:
                        nc.cur_bb.disable_value_cache()
                        head(g, l * LT + first + h * HEAD_TILES, l * (LT // 2) + first // 2 + h * 2 + 1,
                             l * HEADS + GH * gi + h, l * K_LOADS + GH * gi + h, l * V_UNITS + GH * gi + h, l + 1)
                with pe.Fori(0, PAIRS) as j:
                    nc.cur_bb.disable_value_cache()
                    pair(l * LT + C0 + j * PAIR_TILES, l * (LT // 2) + C0 // 2 + j * (PAIR_TILES // 2) + 1,
                         l * HEADS + 2 * GH + j * 4, l * K_LOADS + 2 * GH + j * 3, l * V_UNITS + 2 * GH + j,
                         l * GH + 2 * j)
                n, m = l * LT + O0, l * (LT // 2) + O0 // 2 + 1
                gemm(n, m, 0, split=l)
                gemm(n, m, 1, 0)
                pe.wait_ge(zf[0], m + 1)
                mean_of_first()
                gemm(n, m, 1, 1)
                with pe.Fori(1, KC // 2) as q:
                    nc.cur_bb.disable_value_cache()
                    gemm(n + q * 2, m + q, 0)
                    gemm(n + q * 2, m + q, 1)
            statistics(DEPTH)

        @block.scalar
        def _(act):
            chain = Chain(act, c_al)

            def w_hi(n, s, m):
                act.wait_ge(raw[s], 16 * m)
                act.copy(WH[:, s, :, :], WR[:, s, :, :]).then_inc(hi, 1)

            def tile_done(n, m, j, ahead=True):
                act.wait_ge(zd, n + j + 2)
                if ahead:
                    w_hi(n + j + 2, j % 2, m + j // 2 + 1)

            def exps(g, u, kl=None):
                for j, i in enumerate(g.order):
                    act.wait_ge(mk, 5 * u + j + 1)
                    r, w = TILES[i][1], g.width[i] + g.sink
                    s = S[0:r, g.at[i]:g.at[i] + w]
                    act.activation(s, s, ACT.Exp, bias=nmx[0:r, i:i + 1],
                                   accum_out=esum[0:r, i:i + 1]).then_inc(ex, 1)

            def take_v(vu):
                act.wait_ge(vt, vu + 1)
                act.copy(V[:, 0:4, :], AB[:, 3, :].rearrange("p (b d) -> p b d", b=4)).then_inc(ve, 1)

            def take_o(u, c):
                act.wait_ge(pv, 2 * u + 3)
                act.copy(OY[:, c, 0:SEQ], AB[:, 3, :]).then_inc(oe, 1)
                act.wait_ge(pv, 2 * u + 4)
                act.copy(OY[:, c, SEQ:TOK], AB[:, 2, 0:DEC]).then_inc(oe, 1)

            def gate_exp(s, u):
                act.wait_ge(gd, u + 1)
                act.activation(split2(ES[:, :]), z2(s), ACT.Exp, scale=-1.0).then_inc(eg, 1)

            def take_v_tile(vu):
                act.wait_ge(o_v, 16 * (vu + 1))
                act.copy(split2(VT[:, :]), z2(0)).then_inc(zf[0], 1)

            def k_hi(kl, w, cached):
                act.copy(KH[:, 0:w], KT[:, 0:w])
                act.wait_ge(ld_kc, 16 * (kl + 1))
                act.copy(KCH[:, 0:P * cached], KTC[:, 0:P * cached]).then_inc(kh, 1)

            def head(g, n, m, u, vu, kl, c, rows):
                n, m, u, vu, kl = own(act, n, m, u, vu, kl)
                w_hi(n + 1, 1, m)
                tile_done(n, m, 0)
                act.wait_ge(o_k, 16 * (vu + 1))
                if rows is not None:
                    act.wait_ge(o_fl, 16 * rows)
                    act.wait_ge(o_rows, 16 * rows)
                act.copy(split2(KH), z2(0))
                act.copy(split2(KT[:, :]), z2(0)).then_inc(zf[0], 1)
                act.wait_ge(ld_kc, 16 * (kl + 1))
                act.copy(KCH, KTC[:, :]).then_inc(kh, 1)
                tile_done(n, m, 1)
                act.mul(split2(QH), z2(1), SCALE).then_inc(qh, 1)
                exps(g, u)
                tile_done(n, m, 2)
                take_v_tile(vu)
                take_v(vu)
                tile_done(n, m, 3, ahead=False)
                gate_exp(1, u)
                take_o(u, c)

            def pair(n, m, u, vu, kl, dm, j):
                n, m, u, vu, kl, dm = own(act, n, m, u, vu, kl, dm)
                w_hi(n + 1, 1, m)
                tile_done(n, m, 0)
                act.wait_ge(zf[0], m + 1)
                k_hi(kl, TOK, SWA.cached)
                tile_done(n, m, 1)
                exps(SWA, u)
                tile_done(n, m, 2)
                take_v_tile(vu)
                take_v(vu)
                tile_done(n, m, 3)
                take_o(u, 2 * GH + j * 2)
                exps(SWA, u + 1)
                tile_done(n, m, 4)
                act.mul(split2(QH), z2(0), SCALE).then_inc(qh, 1)
                act.wait_ge(ld_km, 16 * (dm + 1))
                k_hi(kl + 1, NMEM, MEM.cached)
                tile_done(n, m, 5)
                take_o(u + 1, 2 * GH + 1 + j * 2)
                act.wait_ge(sc[2], u + 3)
                act.mul(split2(QH), z2(1), SCALE).then_inc(qh, 1)
                exps(MEM, u + 2)
                act.wait_ge(ld_km, 16 * (dm + 2))
                k_hi(kl + 2, NMEM, MEM.cached)
                tile_done(n, m, 6)
                gate_exp(0, u)
                take_o(u + 2, 3 * GH + j * 2)
                exps(MEM, u + 3)
                tile_done(n, m, 7)
                gate_exp(1, u + 1)
                tile_done(n, m, 8)
                gate_exp(0, u + 2)
                take_o(u + 3, 3 * GH + 1 + j * 2)
                tile_done(n, m, 9, ahead=False)
                gate_exp(1, u + 3)

            def mem_load():
                for p in range(NQ):
                    cs = slice(p * KC // NQ, (p + 1) * KC // NQ)
                    act.dma_start(MTR[:, cs, :], mem_t[:, cs, :]).then_inc(ld_mem[p], 16)

            def mem_hi(r):
                for p in range(NQ):
                    cs = slice(p * KC // NQ, (p + 1) * KC // NQ)
                    act.wait_ge(ld_mem[p], 16 * (r + 1))
                    act.copy(MTH[:, cs, :], MTR[:, cs, :]).then_inc(m_hi, 1)

            def take_shift(r):
                act.wait_ge(mu0, r + 1)
                act.mul(split2(SHIFT), AB[:, 0:2, 0:HALF], KC).then_inc(sh, 1)

            def square(r, c, s):
                act.wait_ge(cen, r * KC + c + 1)
                act.wait_ge(sm2, r * KC + c + 1)
                act.activation(SQ[s], OY[:, c, :], ACT.Square).then_inc(sqr, 1)

            def seed(r):
                act.wait_ge(st, r + 1)
                act.activation(split2(SCR), AB[:, 0:2, 0:HALF], ACT.Square).then_inc(m2, 1)
                act.wait_ge(vr, r + 1)
                chain.link(act.activation(SCR, VE, ACT.Ln))
                act.activation(RSTD, SCR, ACT.Exp, scale=-0.5).then_inc(sd, 1)

            def affine(r, c):
                act.wait_ge(*normed(r, c))
                at = r * KC + c
                act.activation(OY[:, c, :], OY[:, c, :], ACT.Identity, bias=bT[:, bass.ds(at, 1)],
                               scale=gT[:, bass.ds(at, 1)]).then_inc(nx, 1)

            def x_hi(l, c):
                affine(l, c)
                act.wait_ge(nx, l * KC + c + 1)
                act.copy(XH[:, c, :], OY[:, c, :]).then_inc(xh, 1)
                if (c + 1) % (KC // NQ) == 0:
                    cs = slice(c + 1 - KC // NQ, c + 1)
                    act.dma_start(x_res[cs].rearrange("c p t -> p c t"), OY[:, cs, :]).then_inc(o_x, 16)

            def mem_done(l, j):
                n, s = l * LT + j, j % 2
                act.wait_ge(zd, n + 2)
                if j < MEM_TILES - 1:
                    w_hi(n + 2, s, l * (LT // 2) + j // 2 + 2)
                if j >= 2:
                    if j - 2 < GH:
                        act.wait_ge(o_mk[s], 16 * (l * (GH // 2) + (j - 2) // 2 + 1))
                    else:
                        act.wait_ge(to, l * GH + j - 2 - GH + 1)
                act.copy(MT[:, s, :], GB[:, 2 * s, 0:NMEM]).then_inc(zf[s], 1)
                if j < GH:
                    act.wait_ge(zf[s], l * (LT // 2) + j // 2 + 2)
                    act.dma_start(mk_o[l, j], MT[:, s, :]).then_inc(o_mk[s], 16)

            w_hi(0, 0, 1)
            take_shift(0)
            for p in range(NQ):
                if p == 1:
                    mem_hi(0)
                if p == 2:
                    w_hi(1, 1, 1)
                with act.Fori(p * KC // NQ // 2, (p + 1) * KC // NQ // 2) as q:
                    nc.cur_bb.disable_value_cache()
                    for s in range(2):
                        square(0, q * 2 + s, s)
            act.wait_ge(s_const, 16 * N_CONST)
            with act.Fori(0, DEPTH) as layer:
                nc.cur_bb.disable_value_cache()
                l, = own(act, layer)
                chain.start(l * 2)
                act.copy(WFF[:, :, 0:GH], WFR[:, bass.ds(l * KC, KC), :]).then_inc(ffh, 1)
                c = 0
                for kind, i in LN_PLAN:
                    if kind == "stat":
                        seed(l)
                    elif kind == "mem":
                        for _ in range(NORMED_ACT.get(i, 0)):
                            x_hi(l, c)
                            c += 1
                        mem_done(l, i)
                for c in range(c, KC):
                    x_hi(l, c)
                act.wait_ge(ffa, l + 1)
                chain.link(act.activation(T1, T1, ACT.Exp, scale=-1.0))
                act.activation(T1, T1, ACT.Ln, bias=1.0).then_inc(ffe, 1)
                assert chain.k == 2, chain.k
                l, = own(act, layer)
                act.wait_ge(o_x, 16 * NQ * (l + 1))
                for gi, (g, first) in enumerate(((FOX, A0), (BAND, B0))):
                    with act.Fori(0, GH) as h:
                        nc.cur_bb.disable_value_cache()
                        head(g, l * LT + first + h * HEAD_TILES, l * (LT // 2) + first // 2 + h * 2 + 1,
                             l * HEADS + GH * gi + h, l * V_UNITS + GH * gi + h, l * K_LOADS + GH * gi + h,
                             h + GH * gi, l + 1 if g is FOX else None)
                with act.Fori(0, PAIRS) as j:
                    nc.cur_bb.disable_value_cache()
                    pair(l * LT + C0 + j * PAIR_TILES, l * (LT // 2) + C0 // 2 + j * (PAIR_TILES // 2) + 1,
                         l * HEADS + 2 * GH + j * 4, l * V_UNITS + 2 * GH + j, l * K_LOADS + 2 * GH + j * 3,
                         l * GH + 2 * j, j)
                act.wait_ge(gd, HEADS * (l + 1))
                n, m = l * LT + O0, l * (LT // 2) + O0 // 2 + 1
                for h in range(2):
                    cols = slice(h * HALF, (h + 1) * HALF)
                    if h == 1:
                        w_hi(n + 1, 1, m)
                    for c in range(KC):
                        if h == 0 and c == KC - 1:
                            act.wait_ge(gd, HEADS * (l + 1) + 1)
                        act.copy(XH[:, c, cols], OY[:, c, cols]).then_inc(oh[h], 1)
                act.wait_ge(o_k, 16 * (V_UNITS * (l + 1) + 1))
                act.wait_ge(o_v, 16 * (V_UNITS * (l + 1) + 1))
                mem_load()
                r, = own(act, layer + 1)
                tile_done(n, m, 0)
                take_shift(r)
                tile_done(n, m, 1)
                act.wait_ge(o_fl, 16 * r)
                square(r, 0, 0)
                square(r, 1, 1)
                mem_hi(r)
                with act.Fori(1, KC // 2 - 1) as q:
                    nc.cur_bb.disable_value_cache()
                    for s in range(2):
                        tile_done(n + q * 2, m + q, s)
                        square(r, q * 2 + s, s)
                tile_done(n + KC - 2, m + KC // 2 - 1, 0)
                square(r, KC - 2, 0)
                square(r, KC - 1, 1)
                w_hi(n + KC + 1, 1, m + KC // 2)
            chain.start(DEPTH * 2)
            seed(DEPTH)
            for c in range(KC):
                affine(DEPTH, c)
            for s in range(2):
                act.wait_ge(o_mk[s], 16 * (GH // 2) * DEPTH)

        @block.vector
        def _(dve):
            chain = Chain(dve, c_dl)

            def w_lo(n, s):
                dve.wait_ge(hi, n + 1)
                dve.tensor_tensor(WL[:, s, :, :], WR[:, s, :, :], WH[:, s, :, :].bitcast(F32),
                                  ALU.subtract).then_inc(lo, 1)

            def soft_in(g, u, l=None, j=None, k=0):
                if g is FOX:
                    dve.wait_ge(bdr, 2 * (l * GH + j + 1))
                if g is BAND:
                    dve.wait_ge(bmr, l * GH + j + 1)
                for b, col, i in g.place:
                    t0, r = TILES[i]
                    w, at = g.width[i], g.at[i]
                    dve.wait_ge(sc[b], (l * 2 * GH + (GH if g is BAND else 0) + j if b == 3 else u) + 1)
                    src, dst = AB[0:r, b, col:col + w], S[0:r, at:at + w]

                    def add(c0, c1, bias, ):
                        chain.step(dve.tensor_tensor(dst[:, c0:c1], src[:, c0:c1], bias, ALU.add))
                    if g is FOX:
                        if i == 4:
                            add(0, PAST, BI[0:r, SEQ:SEQ + PAST])
                            add(PAST, w, BD[0:r, SEQ:TOK])
                        else:
                            if i:
                                add(0, P * i, BI[:, 0:P * i])
                            add(P * i, w, BD[:, P * i:P * (i + 1)])
                    elif g is BAND:
                        if i == 4:
                            add(0, w, BI[0:r, P:P + w])
                        else:
                            add(0, w, BI[:, SEQ - w:SEQ])
                    elif g is SWA and i < 4:
                        chain.step(dve.scalar_tensor_tensor(dst, src, SCALE, swam[:, 2 * P - w:2 * P],
                                                            ALU.mult, ALU.add))
                    elif g is SWA:
                        chain.step(dve.tensor_scalar(dst, src, SCALE, None, ALU.mult))
                    else:
                        chain.step(dve.tensor_copy(dst, src))
                    if g.sink:
                        at_s = l * GH + j * 2 + k
                        chain.step(dve.tensor_copy(S[0:r, at + w:at + w + 1], snk[0:r, bass.ds(at_s, 1)]))
                    chain.wait()
                    dve.tensor_reduce(nmx[0:r, i:i + 1], S[0:r, at:at + w + g.sink], AX_X, ALU.max,
                                      negate=True).then_inc(mk, 1)

            def soft_out(g, u):
                dve.wait_ge(ex, 5 * u + 5)
                chain.link(dve.reciprocal(rsum[:, 0:NT], esum[:, 0:NT]))
                for i in g.order:
                    r, w = TILES[i][1], g.width[i]
                    s = S[0:r, g.at[i]:g.at[i] + w]
                    dve.tensor_scalar(s, s, rsum[0:r, i:i + 1], None, ALU.mult).then_inc(pr, 1)

            def take_probs(g, u, vu=None):
                n = sum(len(b) for b in g.blocks)
                for b in range(2):
                    dve.wait_ge(pt, 3 * u + b + 1)
                    w = P * min(4, n - 4 * b)
                    dve.tensor_copy(PT[:, 512 * b:512 * b + w], AB[:, b, 0:w]).then_inc(pte, 1)
                dve.wait_ge(pt, 3 * u + 3)
                if n > 8:
                    dve.tensor_copy(PT[:, 8 * P:n * P], AB[:, 2, 0:(n - 8) * P])
                ins = dve.tensor_copy(PT[:, 10 * P:10 * P + DEC * g.cached], AB[:, 2, 256:256 + DEC * g.cached])
                if g.own:
                    ins = dve.tensor_copy(PT[0:DEC, 10 * P + 2 * DEC:PTW], AB[0:DEC, 2, 320:320 + DEC])
                ins.then_inc(pte, 1)
                if vu is not None:
                    dve.tensor_copy(V[0:DEC, 4, :], AB[0:DEC, 2, 352:352 + P]).then_inc(vse, 1)

            def gate(s, u, c, zf_n):
                dve.wait_ge(eg, u + 1)
                chain.link(dve.tensor_scalar(ES[:, :], ES[:, :], 1.0, None, ALU.add))
                chain.link(dve.reciprocal(ES[:, :], ES[:, :]))
                dve.tensor_tensor(split2(GA[:, :]), z2(s), split2(ES[:, :]), ALU.mult).then_inc(zf[s], 1)
                dve.wait_ge(zf[s], zf_n)
                dve.wait_ge(oe, 2 * u + 4)
                dve.tensor_tensor(OY[:, c, :], OY[:, c, :], GA[:, :], ALU.mult).then_inc(gd, 1)

            def rope(s, dst, sw, k_before=None):
                h = HD // 2
                chain.step(dve.tensor_copy(split2(sw[0:h, :]), z2(s)[h:HD]))
                chain.step(dve.tensor_copy(split2(sw[h:HD, :]), z2(s)[0:h]))
                chain.wait()
                chain.step(dve.tensor_tensor(sw[:, :], sw[:, :], sin[:, :], ALU.mult))
                if k_before is not None:
                    dve.wait_ge(o_k, 16 * (k_before + 1))
                chain.link(dve.tensor_tensor(split2(dst[:, :]), z2(s), split2(cos[:, :]), ALU.mult))
                add = dve.tensor_tensor(dst[:, :], dst[:, :], sw[:, :], ALU.add)
                if dst is KT:
                    add.then_inc(zf[s], 1)
                else:
                    chain.link(add)
                    chain.link(dve.tensor_copy(QH, dst[:, :]))
                    dve.tensor_tensor(QL, dst[:, :], QH.bitcast(F32), ALU.subtract).then_inc(zf[s], 1)

            def k_lo(kl, w, cached):
                dve.wait_ge(kh, kl + 1)
                dve.tensor_tensor(KL[:, 0:w], KT[:, 0:w], KH[:, 0:w].bitcast(F32), ALU.subtract)
                dve.tensor_tensor(KCL[:, 0:P * cached], KTC[:, 0:P * cached], KCH[:, 0:P * cached].bitcast(F32),
                                  ALU.subtract).then_inc(k_low, 1)

            def q_lo(s, qn):
                dve.wait_ge(qh, qn + 1)
                dve.scalar_tensor_tensor(split2(QL), z2(s), SCALE, split2(QH.bitcast(F32)), ALU.mult, ALU.subtract) \
                    .then_inc(zf[s], 1)

            def head(g, n, m, u, vu, kl, l, h, c):
                n, m, u, vu, kl, l = own(dve, n, m, u, vu, kl, l)
                w_lo(n + 1, 1)
                w_lo(n + 2, 0)
                k_lo(kl, TOK, g.cached)
                q_lo(1, l * Q_SPLITS + (GH if g is BAND else 0) + h)
                w_lo(n + 3, 1)
                soft_in(g, u, l, h)
                soft_out(g, u)
                w_lo(n + 4, 0)
                take_probs(g, u, vu)
                gate(1, u, c, m + 2)

            def pair(n, m, u, vu, kl, l, j):
                n, m, u, vu, kl, l = own(dve, n, m, u, vu, kl, l)
                qn = l * Q_SPLITS + 2 * GH + j * 2
                w_lo(n + 1, 1)
                dve.wait_ge(zd, n + 2)
                dve.wait_ge(gd, u + 1)
                rope(0, KT, GA, vu)
                w_lo(n + 2, 0)
                k_lo(kl, TOK, SWA.cached)
                dve.wait_ge(zd, n + 3)
                rope(1, QT, ES)
                w_lo(n + 3, 1)
                soft_in(SWA, u, l, j, 0)
                soft_out(SWA, u)
                w_lo(n + 4, 0)
                take_probs(SWA, u, vu)
                dve.wait_ge(zd, n + 5)
                rope(1, QT, ES)
                w_lo(n + 5, 1)
                soft_in(SWA, u + 1, l, j, 1)
                soft_out(SWA, u + 1)
                w_lo(n + 6, 0)
                q_lo(0, qn)
                k_lo(kl + 1, NMEM, MEM.cached)
                take_probs(SWA, u + 1)
                w_lo(n + 7, 1)
                soft_in(MEM, u + 2)
                q_lo(1, qn + 1)
                soft_out(MEM, u + 2)
                k_lo(kl + 2, NMEM, MEM.cached)
                take_probs(MEM, u + 2)
                w_lo(n + 8, 0)
                gate(0, u, 2 * GH + j * 2, m + 4)
                soft_in(MEM, u + 3)
                soft_out(MEM, u + 3)
                w_lo(n + 9, 1)
                gate(1, u + 1, 2 * GH + 1 + j * 2, m + 4)
                take_probs(MEM, u + 3)
                w_lo(n + 10, 0)
                gate(0, u + 2, 3 * GH + j * 2, m + 5)
                gate(1, u + 3, 3 * GH + 1 + j * 2, m + 5)

            def mem_lo(r):
                for p in range(NQ):
                    cs = slice(p * KC // NQ, (p + 1) * KC // NQ)
                    dve.wait_ge(m_hi, NQ * r + p + 1)
                    dve.tensor_tensor(MTL[:, cs, :], MTR[:, cs, :], MTH[:, cs, :].bitcast(F32), ALU.subtract) \
                        .then_inc(m_lo, 1)

            def shift(r, c):
                centre(c)
                add_up(r, c)

            def centre(c):
                dve.tensor_tensor(OY[:, c, :], OY[:, c, :], SHIFT, ALU.subtract).then_inc(cen, 1)

            def add_up(r, c):
                dve.wait_ge(cen, r * KC + c + 1)
                dve.wait_ge(sm1, r * KC + c + 1)
                dve.tensor_tensor(SUM1, SUM1, OY[:, c, :], ALU.add).then_inc(sm1, 1)

            def rstd(r):
                mean, mean_sq = AB[:, 0:2, 0:HALF], AB[:, 2:4, 0:HALF]
                dve.wait_ge(m2, r + 1)
                dve.scalar_tensor_tensor(split2(VE), mean_sq, EPS, split2(SCR), ALU.add, ALU.subtract).then_inc(vr, 1)
                dve.wait_ge(sd, r + 1)
                chain.link(dve.scalar_tensor_tensor(SCR, RSTD, -0.5, VE, ALU.mult, ALU.mult))
                chain.link(dve.tensor_tensor(SCR, SCR, RSTD, ALU.mult))
                chain.link(dve.scalar_tensor_tensor(RSTD, SCR, 1.5, RSTD, ALU.add, ALU.mult))
                dve.scalar_tensor_tensor(split2(NMR), mean, -1.0, split2(RSTD), ALU.mult, ALU.mult).then_inc(bs, 1)

            def normalise(r, c):
                dve.tensor_tensor(OY[:, c, :], OY[:, c, :], RSTD, ALU.mult).then_inc(n1, 1)
                if c not in SHARE or r is None:
                    dve.wait_ge(n1, DEPTH * KC + n1_last.index(c) + 1 if r is None else r * KC + c + 1)
                    if c == 0:
                        dve.wait_ge(bs, (DEPTH if r is None else r) + 1)
                    dve.tensor_tensor(OY[:, c, :], OY[:, c, :], NMR, ALU.add).then_inc(n2[0], 1)

            n1_last = [c for c in range(KC) if c not in LAST_SHARE]

            def take_turned(l, f):
                dve.wait_ge(to, l * GH + f + 1)
                dve.wait_ge(o_mv[f % 2], 16 * (l * (GH // 2) + f // 2 + 1))
                dve.tensor_copy(MVN[:, f % 2, :], GB[:, 1 + 2 * (f % 2), 0:NMEM]).then_inc(tf, 1)

            dve.memset(esum[:, :], 1.0)
            for released, count in ((zd, 1), (zf[0], 1), (zf[1], 1), (tf, 1), (gd, 1), (oe, 2), (pv, 2), (sm1, 1),
                                    (sm2, 2)):
                dve.sem_inc(released, count)
            dve.memset(one[:, :], 1.0)
            dve.memset(ones[:, :], 1.0 / DM).then_inc(s_one, 1)
            dve.wait_ge(s_one, 1)
            w_lo(0, 0)
            dve.wait_ge(zero, 1)
            dve.wait_ge(sh, 1)
            for step, p in (("centre", 0), ("centre", 1), ("mem", 0), ("weights", 1), ("centre", 2), ("centre", 3)):
                if step == "mem":
                    mem_lo(0)
                    continue
                if step == "weights":
                    w_lo(1, 1)
                    continue
                dve.wait_ge(s_x[p], 16)
                with dve.Fori(p * KC // NQ // 2, (p + 1) * KC // NQ // 2) as q:
                    nc.cur_bb.disable_value_cache()
                    for s in range(2):
                        centre(q * 2 + s)
            dve.wait_ge(cen, KC)
            dve.tensor_reduce(SUM1, OY[:, :, :].rearrange("p c t -> p t c"), AX_X, ALU.add).then_inc(sm1, KC)
            dve.wait_ge(s_const, 16 * N_CONST)
            with dve.Fori(0, DEPTH) as layer:
                nc.cur_bb.disable_value_cache()
                l, = own(dve, layer)
                chain.sem = c_dl
                chain.start(l * CH["ln"])
                dve.wait_ge(ffh, l + 1)
                dve.tensor_tensor(WFF[:, :, GH:2 * GH], WFR[:, bass.ds(l * KC, KC), :], WFF[:, :, 0:GH].bitcast(F32),
                                  ALU.subtract).then_inc(ffl, 1)
                c = 0
                for kind, i in LN_PLAN:
                    if kind == "stat":
                        rstd(l)
                    elif kind == "mem":
                        for _ in range(NORMED_DVE.get(i, 0)):
                            normalise(l, c)
                            c += 1
                        if i < MEM_TILES - 1:
                            w_lo(l * LT + i + 2, i % 2)
                    elif kind == "mv":
                        take_turned(l, i - GH)
                assert chain.k == CH["ln"], ("ln", chain.k)
                chain.sem = c_df
                chain.start(l * CH["ff"])
                dve.wait_ge(ffd, l + 1)
                bf = bF[:, bass.ds(l, 1)]
                chain.link(dve.tensor_scalar(split2(LF), AB[0:GH, 0:2, 0:HALF], bf, None, ALU.add))
                dve.scalar_tensor_tensor(T1, LF, -1.0, LF, ALU.mult, ALU.max).then_inc(ffa, 1)
                dve.wait_ge(ffe, l + 1)
                dve.scalar_tensor_tensor(LF, LF, 0.0, T1, ALU.min, ALU.subtract).then_inc(flr, 1)
                dve.wait_ge(flr, l + 1)
                unit = one[0:GH, 0:1]
                chain.step(dve.tensor_tensor_scan(NR[:, 0:SEQ], unit.broadcast_to([GH, SEQ]), LF[:, 0:SEQ], 0.0,
                                                  ALU.mult, ALU.subtract))
                chain.link(dve.tensor_tensor_scan(NR[:, SEQ:SEQ + PAST], unit.broadcast_to([GH, PAST]),
                                                  CL[:, bass.ds(l * PAST, PAST)], 0.0,
                                                  ALU.mult, ALU.subtract))
                dve.tensor_tensor_scan(NR[:, SEQ + PAST:], unit.broadcast_to([GH, DEC]), LF[:, SEQ:TOK],
                                       NR[:, SEQ + PAST - 1:SEQ + PAST], ALU.mult, ALU.subtract).then_inc(ncr, 1)
                assert chain.k == CH["ff"], ("ff", chain.k)
                l, = own(dve, layer)
                for gi, (g, first, key, csem) in enumerate(((FOX, A0, "fox", c_da), (BAND, B0, "band", c_db))):
                    with dve.Fori(0, GH) as h:
                        nc.cur_bb.disable_value_cache()
                        chain.sem = csem
                        chain.start((l * GH + h) * CH[key])
                        head(g, l * LT + first + h * HEAD_TILES, l * (LT // 2) + first // 2 + h * 2 + 1,
                             l * HEADS + GH * gi + h,
                             l * V_UNITS + GH * gi + h, l * K_LOADS + GH * gi + h, l, h, h + GH * gi)
                        assert chain.k == CH[key], (key, chain.k)
                with dve.Fori(0, PAIRS) as j:
                    nc.cur_bb.disable_value_cache()
                    chain.sem = c_dc
                    chain.start((l * PAIRS + j) * CH["pair"])
                    pair(l * LT + C0 + j * PAIR_TILES, l * (LT // 2) + C0 // 2 + j * (PAIR_TILES // 2) + 1,
                         l * HEADS + 2 * GH + j * 4, l * V_UNITS + 2 * GH + j, l * K_LOADS + 2 * GH + j * 3, l, j)
                    assert chain.k == CH["pair"], ("pair", chain.k)
                for h in range(2):
                    if h == 1:
                        w_lo(l * LT + O0 + 1, 1)
                    for c in range(KC):
                        if c not in LOW_SHARE[h]:
                            make_low(dve, l, h, c)

                def residual(c, s, count, xr):
                    dve.wait_ge(zd, count + 1)
                    dve.wait_ge(ld_xr[s], xr)
                    dve.scalar_tensor_tensor(split2(OY[:, c, :]), split2(XR[:, s, :]), ALPHA, z2(s),
                                             ALU.mult, ALU.add).then_inc(zf[s], 1)

                def summed(c, s, q):
                    residual(c, s, n + c + 1, 16 * (l * (KC // 2) + q + 1))
                    dve.wait_ge(zf[s], m + q + 1)
                    shift(r, c)

                n, m = l * LT + O0, l * (LT // 2) + O0 // 2 + 1
                r, = own(dve, layer + 1)
                w_lo(n + 2, 0)
                residual(0, 0, n + 1, 16 * (l * (KC // 2) + 1))
                w_lo(n + 3, 1)
                dve.wait_ge(zero, l + 2)
                dve.wait_ge(sh, l + 2)
                dve.wait_ge(zf[0], m + 1)
                shift(r, 0)
                summed(1, 1, 0)
                mem_lo(l + 1)
                with dve.Fori(1, KC // 2 - 1) as q:
                    nc.cur_bb.disable_value_cache()
                    for s in range(2):
                        w_lo(n + q * 2 + s + 2, s)
                        summed(q * 2 + s, s, q)
                summed(KC - 2, 0, KC // 2 - 1)
                w_lo(n + KC, 0)
                summed(KC - 1, 1, KC // 2 - 1)
                w_lo(n + KC + 1, 1)
            chain.sem = c_dl
            chain.start(DEPTH * CH["ln"])
            rstd(DEPTH)
            for c in n1_last:
                normalise(None, c)

        @block.gpsimd
        def _(pool):
            def sum_up(r, c, s):
                pool.wait_ge(sqr, r * KC + c + 1)
                pool.wait_ge(sm2, r * KC + c + 2)
                pool.tensor_tensor(SUM2, SUM2, SQ[s], ALU.add).then_inc(sm2, 1)

            def less_mean(r, c):
                if r is not None:
                    pool.wait_ge(n1, r * KC + c + 1)
                pool.tensor_tensor(OY[:, c, :], OY[:, c, :], NMR, ALU.add).then_inc(n2[1], 1)

            def x_lo(l, c):
                pool.wait_ge(xh, l * KC + c + 1)
                pool.tensor_tensor(XL[:, c, :], OY[:, c, :], XH[:, c, :].bitcast(F32), ALU.subtract).then_inc(xl, 1)

            pool.memset(LNB[:, 0:2, :], 0.0).then_inc(zero, 1)
            pool.wait_ge(zero, 1)
            for p in range(NQ):
                with pool.Fori(p * KC // NQ // 2, (p + 1) * KC // NQ // 2) as q:
                    nc.cur_bb.disable_value_cache()
                    for s in range(2):
                        sum_up(0, q * 2 + s, s)
            for i, done in enumerate((o_k, o_v, o_mv[0], o_mv[1])):
                pool.dma_start(rsum[i:i + 1, NT:NT + 1], ident_d[0:1, 0:1]).then_inc(done, 16)
            for i in range(DEPTH):
                src = bass.AP(rel_pad.tensor, i * GH * RELW, [[RELW, GH], [0, P], [1, RELW]])
                pool.dma_start(rel_rows[i * GH:(i + 1) * GH], src).then_inc(s_toep, 16)
            with pool.Fori(0, DEPTH) as layer:
                nc.cur_bb.disable_value_cache()
                l, = own(pool, layer)
                wait_apart(pool, bs, l + 1)
                c = 0
                for kind, i in LN_PLAN:
                    if kind == "mem":
                        for _ in range(NORMED_ACT.get(i, 0) if i < MEM_TILES - 1 else KC - c):
                            if c + 3 in SHARE:
                                less_mean(l, c + 3)
                            x_lo(l, c)
                            c += 1
                    elif kind == "mv":
                        wait_apart(pool, tf, l * GH + i - GH + 2)
                        pool.dma_start(mv_o[l, i - GH], MVN[:, i % 2, :].rearrange("p (b d) -> p b d", b=2)) \
                            .then_inc(o_mv[i % 2], 16)
                wait_apart(pool, flr, l + 1)
                pool.dma_start(fl_o[l], LF).then_inc(o_fl, 16)
                wait_apart(pool, ncr, l + 1)
                pool.dma_start(nc_rows, NR).then_inc(o_rows, 16)
                pool.wait_ge(o_rows, 16 * (l + 1))
                for s in range(2):
                    pool.wait_ge(o_mk[s], 16 * (GH // 2) * (l + 1))
                    pool.wait_ge(o_mv[s], 16 * ((GH // 2) * (l + 1) + 1))
                wait_apart(pool, o_x, 16 * NQ * (l + 1))
                for s in range(2):
                    pool.dma_start(XR[:, s, :], x_res[s]).then_inc(ld_xr[s], 16)

                l, = own(pool, layer)
                for gi, (g, first) in enumerate(((FOX, A0), (BAND, B0))):
                    with pool.Fori(0, GH) as h:
                        nc.cur_bb.disable_value_cache()
                        u, vu = l * HEADS + GH * gi + h, l * V_UNITS + GH * gi + h
                        m = l * (LT // 2) + first // 2 + h * 2 + 1
                        pool.wait_ge(pv, 2 * u + 2)
                        kc, vc = (fox_k, fox_v) if g is FOX else (band_k, band_v)
                        ko, vo = (fk_o, fv_o) if g is FOX else (bk_o, bv_o)
                        pool.dma_start(KTC[:, :], kc[l, h]).then_inc(ld_kc, 16)
                        if g is BAND:
                            pool.wait_ge(s_toep, 16 * DEPTH)
                        if g is FOX:
                            pool.dma_start(BI[:, :], nc_rows[h].partition_broadcast(P)).then_inc(ld_bias, 16)
                        else:
                            pool.dma_start(BI[:, 0:SEQ], toep[l * GH + h]).then_inc(ld_bias, 16)
                        pool.dma_start(VC[:, :, :], vc[l, h]).then_inc(ld_vc, 16)
                        wait_apart(pool, ld_bias, 16 * (l * 2 * GH + GH * gi + h + 1))
                        if g is FOX:
                            pool.tensor_tensor(BD[:, 0:SEQ].rearrange("p (b c) -> p b c", b=4),
                                               BI[:, 0:SEQ].rearrange("p (b c) -> p b c", b=4),
                                               causal[:, :].unsqueeze(1).broadcast_to([P, 4, P]), ALU.add) \
                                .then_inc(bdr, 1)
                            pool.tensor_tensor(BD[0:DEC, SEQ:TOK], BI[0:DEC, SEQ + PAST:], causal[0:DEC, 0:DEC],
                                               ALU.add).then_inc(bdr, 1)
                        else:
                            pool.memset(BI[0:P // 2, SEQ - P // 2:SEQ], NEG).then_inc(bmr, 1)
                        wait_apart(pool, zf[0], m + 1)
                        pool.dma_start(ko[l, h], KT[:, :]).then_inc(o_k, 16)
                        wait_apart(pool, zf[0], m + 2)
                        pool.dma_start(vo[l, h], VT[:, :]).then_inc(o_v, 16)
                with pool.Fori(0, PAIRS) as j:
                    nc.cur_bb.disable_value_cache()
                    u, vu, dm = l * HEADS + 2 * GH + j * 4, l * V_UNITS + 2 * GH + j, l * GH + 2 * j
                    m = l * (LT // 2) + C0 // 2 + j * (PAIR_TILES // 2) + 1
                    wait_apart(pool, pv, 2 * u + 2)
                    pool.dma_start(KTC[:, 0:P], swa_k[l, j]).then_inc(ld_kc, 16)
                    pool.dma_start(VC[:, 0, :], swa_v[l, j]).then_inc(ld_vc, 16)
                    wait_apart(pool, zf[0], m + 1)
                    pool.dma_start(sk_o[l, j], KT[:, TOK - P - DEC:TOK]).then_inc(o_k, 16)
                    wait_apart(pool, zf[0], m + 2)
                    pool.dma_start(sv_o[l, j], VT[:, TOK - P - DEC:TOK]).then_inc(o_v, 16)
                    for k in range(2):
                        pool.wait_ge(sc[2], u + k + 2)
                        wait_apart(pool, o_k, 16 * (vu + 2))
                        pool.dma_start(KT[:, 0:NMEM], mk_o[l, j * 2 + k]).then_inc(ld_km, 16)
                        pool.dma_start(KTC[:, :], mem_k[l, j * 2 + k]).then_inc(ld_kc, 16)
                        wait_apart(pool, pv, 2 * (u + k + 3))
                        pool.dma_start(V[:, 0:2, :], mv_o[l, j * 2 + k]).then_inc(ld_vm, 16)
                        pool.dma_start(VC[:, :, :], mem_v[l, j * 2 + k]).then_inc(ld_vc, 16)
                for h in range(2):
                    for c in LOW_SHARE[h]:
                        make_low(pool, l, h, c)
                pool.memset(LNB[:, 0:2, :], 0.0).then_inc(zero, 1)
                r, = own(pool, layer + 1)

                def load_residual(q, s):
                    wait_apart(pool, zf[s], l * (LT // 2) + O0 // 2 + q + 1)
                    pool.dma_start(XR[:, s, :], x_res[q * 2 + s]).then_inc(ld_xr[s], 16)

                with pool.Fori(0, KC // 2 - 1) as q:
                    nc.cur_bb.disable_value_cache()
                    for s in range(2):
                        load_residual(q + 1, s)
                        sum_up(r, q * 2 + s, s)
                for s in range(2):
                    sum_up(r, KC - 2 + s, s)
            wait_apart(pool, bs, DEPTH + 1)
            for i, c in enumerate(LAST_SHARE):
                pool.tensor_tensor(OY[:, c, :], OY[:, c, :], RSTD, ALU.mult).then_inc(n1p, 1)
                pool.wait_ge(n1p, i + 1)
                less_mean(None, c)
            pool.wait_ge(o_k, 16 * (V_UNITS * DEPTH + 1))


CH = {"ln": 3, "ff": 3, "fox": 12, "band": 8, "pair": 58}

_OUTS = [(KC, P, TOK), ((DEPTH, GH, P, TOK)), ((DEPTH, GH, P, TOK)), ((DEPTH, GH, TOK)),
         ((DEPTH, GH, P, TOK)), ((DEPTH, GH, P, TOK)), ((DEPTH, PAIRS, P, P + DEC)), ((DEPTH, PAIRS, P, P + DEC)),
         ((DEPTH, GH, P, NMEM)), ((DEPTH, GH, P, 2, HD))]


def kernel(**inputs):
    import numpy as np
    import concourse.bacc as bacc
    from concourse.bass_utils import run_bass_kernel_spmd as run

    f32 = np.float32
    a = {k: np.asarray(v) for k, v in inputs.items()}

    def cols(w, c, n=P):
        return w[:, c:c + n].reshape(KC, P, n).transpose(1, 0, 2)

    fq, fk, fv, ff = 0, 512, 1024, 1536
    bq = ff + GH
    bk, bv = bq + 512, bq + 1024
    sq = bq + 1536
    sk, sv = sq + 512, sq + 768
    mq = sq + 1024
    gate = mq + 512
    layers = []
    for l in range(DEPTH):
        wi, wm, wo = a["w_in"][l], a["w_mem_kv"][l], a["w_out"][l]
        t = [cols(wm, P * j) for j in range(MEM_TILES)]
        for g, (k0, q0, v0) in enumerate(((fk, fq, fv), (bk, bq, bv))):
            for h in range(GH):
                t += [cols(wi, c + P * h) for c in (k0, q0, v0)] + [cols(wi, gate + P * (GH * g + h))]
        for j in range(PAIRS):
            t += [cols(wi, sk + P * j), cols(wi, sq + 2 * P * j), cols(wi, sv + P * j), cols(wi, sq + 2 * P * j + P)]
            t += [cols(wi, mq + 2 * P * j + P * k) for k in range(2)]
            t += [cols(wi, gate + P * (2 * GH + 2 * j + k)) for k in range(2)]
            t += [cols(wi, gate + P * (3 * GH + 2 * j + k)) for k in range(2)]
        t += [cols(wo, P * j) for j in range(KC)]
        layers += t
    def keys(x):
        return x[:, 0].transpose(0, 2, 3, 1)

    def values(x):
        d, _, n, h, f = x.shape
        return x[:, 0].reshape(d, n // P, P, h, f).transpose(0, 3, 2, 1, 4)

    x_all = np.concatenate([a["x_prompt"][0], a["x_sample"][0]], 0)
    gs = np.concatenate([a["ln_in_g"][None], a["ln_g"]], 0)
    bs = np.concatenate([a["ln_in_b"][None], a["ln_b"]], 0)
    pos = np.concatenate([np.arange(SEQ), PAST + np.arange(DEC)]).astype(f32)
    half = HD // 2
    inv = (10000.0 ** (-np.arange(half) / half)).astype(f32)
    ang = inv[:, None] * pos[None, :]
    cos = np.concatenate([np.cos(ang), np.cos(ang)], 0)
    sin = np.concatenate([-np.sin(ang), np.sin(ang)], 0)
    r = np.arange(P)
    causal = np.where(r[None, :] <= r[:, None], 0.0, NEG)
    ahead = np.arange(2 * P)[None, :] // 64 - r[:, None] // 64
    swa = np.where((ahead >= 0) & (ahead <= 2), 0.0, NEG)

    arrays = {
        "wt": np.stack(layers).reshape(DEPTH * LT, P, KC, P),
        "wff": np.concatenate([cols(a["w_in"][l], ff, GH) for l in range(DEPTH)], 1),
        "bff": a["b_f"].T,
        "x_t": x_all.T.reshape(KC, P, TOK).transpose(1, 0, 2),
        "mem_t": a["mem_prompt"][0].T.reshape(KC, P, NMEM).transpose(1, 0, 2),
        "fox_k": keys(a["cache_fox_k"]), "fox_v": values(a["cache_fox_v"]),
        "fox_logf": a["cache_fox_logf"][:, 0].transpose(2, 0, 1).reshape(GH, -1),
        "band_k": keys(a["cache_band_k"]), "band_v": values(a["cache_band_v"]),
        "swa_k": keys(a["cache_swa_k"]), "swa_v": values(a["cache_swa_v"]).reshape(DEPTH, PAIRS, P, HD),
        "mem_k": keys(a["cache_mem_k"]), "mem_v": values(a["cache_mem_v"]),
        "rel_pad": np.pad(a["rel_bias"], ((0, 0), (0, 0), (SEQ + P - 257, 0)), mode="edge"),
        "sinks": a["sinks"].reshape(1, -1)[0],
        "ln_gt": gs.reshape(-1, KC, P).transpose(2, 0, 1).reshape(P, -1),
        "ln_bt": bs.reshape(-1, KC, P).transpose(2, 0, 1).reshape(P, -1),
        "ident": np.eye(P), "causal": causal, "swa_mask": swa, "cos": cos, "sin": sin,
    }
    nc = bacc.Bacc("TRN2", target_bir_lowering=False, num_devices=1)
    feed, args = {}, []
    for name, v in arrays.items():
        v = np.ascontiguousarray(v, dtype=f32)
        feed[f"in_{name}"] = v
        args.append(nc.dram_tensor(f"in_{name}", v.shape, F32, kind="ExternalInput").ap())
    for i, shape in enumerate(_OUTS):
        args.append(nc.dram_tensor(f"out_{i}", shape, F32, kind="ExternalOutput").ap())
    encoder_step(nc, *args)
    res = run(nc, [feed], core_ids=[0]).results[0]
    y, fk_, fv_, fl_, bk_, bv_, sk_, sv_, mk_, mv_ = (res[f"out_{i}"] for i in range(len(_OUTS)))

    def heads(x, lo, hi):
        return np.ascontiguousarray(x[:, :, :, lo:hi].transpose(0, 3, 1, 2)[:, None])

    def logf(lo, hi):
        return np.ascontiguousarray(fl_[:, :, lo:hi].transpose(0, 2, 1)[:, None])

    mem_v = np.ascontiguousarray(mv_.transpose(0, 3, 2, 1, 4).reshape(DEPTH, NMEM, GH, HD)[:, None])
    y = np.ascontiguousarray(y.reshape(DM, TOK).T)
    return (y[None, :SEQ], y[None, SEQ:],
            heads(fk_, 0, SEQ), heads(fv_, 0, SEQ), logf(0, SEQ),
            heads(bk_, 0, SEQ), heads(bv_, 0, SEQ),
            heads(sk_, 0, P), heads(sv_, 0, P),
            heads(mk_, 0, NMEM), mem_v,
            heads(fk_, SEQ, TOK), heads(fv_, SEQ, TOK), logf(SEQ, TOK),
            heads(bk_, SEQ, TOK), heads(bv_, SEQ, TOK),
            heads(sk_, P, P + DEC), heads(sv_, P, P + DEC))
```
